# Optimizing a Trainium2 kernel written in Bass

```python
import math
import jax, jax.numpy as jnp
from jax import lax
import numpy as np

D_MODEL = 1024
BATCH = 1
SEQ = 512
DEPTH = 1
DEC_BATCH = 1
DEC_SEQ = 32
PAST_LEN = 512

CHUNK = 64
GDN_HEADS = 8
GDN_DK = 128
GDN_DV = 128
GDN_DIM = GDN_HEADS * GDN_DK
GDN_VDIM = GDN_HEADS * GDN_DV
QKV_DIM = 2 * GDN_DIM + GDN_VDIM
CONV_W = 4
LRU_WIDTH = D_MODEL
LRU_BLOCKS = 8
LRU_BW = LRU_WIDTH // LRU_BLOCKS
LRU_C = 8.0
V_END = QKV_DIM
Z_END = V_END + GDN_VDIM
B_END = Z_END + GDN_HEADS
A_END = B_END + GDN_HEADS
LX_END = A_END + LRU_WIDTH
IN_DIM = LX_END + LRU_WIDTH
MIX_DIM = GDN_VDIM + LRU_WIDTH
N_EXPERTS = 64
TOP_K = 8
N_GROUPS = 8
TOPK_GROUPS = 4
EXPERT_FF = 256
SHARED_FF = 256
ROUTED_SCALE = 2.5
MOE_BLOCK = 128
DN_ALPHA = (2.0 * DEPTH) ** 0.25
DN_BETA = (8.0 * DEPTH) ** -0.25
LN_EPS = 1e-5
RMS_EPS = 1e-6

kernel_name = 'hybrid_gdn_rglru_moe_stream_step'

def layer_norm(x, g, b):
    xf = x.astype(jnp.float32)
    mu = jnp.mean(xf, -1, keepdims=True)
    xc = xf - mu
    var = jnp.mean(xc * xc, -1, keepdims=True)
    return (xc * lax.rsqrt(var + LN_EPS) * g + b).astype(x.dtype)

def l2norm(t):
    return t * lax.rsqrt(jnp.sum(t * t, -1, keepdims=True) + 1e-6)

def causal_dwconv(x, buf, w, b=None):
    T = x.shape[1]
    xp = jnp.concatenate([buf.astype(x.dtype), x], axis=1)
    out = xp[:, 0:T] * w[0]
    for j in range(1, CONV_W):
        out = out + xp[:, j:j + T] * w[j]
    if b is not None:
        out = out + b
    return out, xp[:, T:]

def gdn_chunked(q, k, v, beta, g, s0, chunk):
    bsz, T, H, dk = q.shape
    dv = v.shape[-1]
    n = T // chunk

    def blocks(t):
        t = t.reshape((bsz, n, chunk, H) + t.shape[3:])
        return jnp.moveaxis(t, 3, 1)

    q, k, v, beta, g = blocks(q), blocks(k), blocks(v), blocks(beta), blocks(g)
    g = jnp.cumsum(g, axis=-1)
    causal = jnp.tril(jnp.ones((chunk, chunk), bool))
    strict = jnp.tril(jnp.ones((chunk, chunk), bool), -1)
    decay = jnp.exp(jnp.where(causal, g[..., :, None] - g[..., None, :], -jnp.inf))
    k_beta = k * beta[..., None]
    lower = jnp.where(strict, jnp.einsum('bhnid,bhnjd->bhnij', k_beta, k) * decay, 0.0)
    m = lower + jnp.eye(chunk, dtype=lower.dtype)
    rhs = jnp.concatenate([v * beta[..., None], k_beta * jnp.exp(g)[..., None]], -1)
    sol = lax.linalg.triangular_solve(m, rhs, left_side=True, lower=True, unit_diagonal=True)
    u, w = sol[..., :dv], sol[..., dv:]
    qk = jnp.einsum('bhnid,bhnjd->bhnij', q, k) * decay
    g_last = g[..., -1]
    q_dec = q * jnp.exp(g)[..., None]
    k_dec = k * jnp.exp(g_last[..., None] - g)[..., None]

    def step(s, inp):
        u_c, w_c, qk_c, qd_c, kd_c, gl_c = inp
        v_new = u_c - jnp.einsum('bhcd,bhde->bhce', w_c, s)
        o_c = jnp.einsum('bhcd,bhde->bhce', qd_c, s) + jnp.einsum('bhij,bhje->bhie', qk_c, v_new)
        s = s * jnp.exp(gl_c)[..., None, None] + jnp.einsum('bhcd,bhce->bhde', kd_c, v_new)
        return s, o_c

    xs = tuple(jnp.moveaxis(t, 2, 0) for t in (u, w, qk, q_dec, k_dec, g_last))
    s_fin, o = lax.scan(step, s0, xs)
    o = jnp.moveaxis(jnp.moveaxis(o, 0, 2), 1, 3).reshape(bsz, T, H, dv)
    return o, s_fin

def _lin_combine(e1, e2):
    a1, b1 = e1
    a2, b2 = e2
    return a1 * a2, a2 * b1 + b2

def route(x2, router_w, router_bias):
    T = x2.shape[0]
    scores = jax.nn.sigmoid((x2 @ router_w).astype(jnp.float32))
    biased = scores + router_bias.astype(jnp.float32)
    grp = biased.reshape(T, N_GROUPS, N_EXPERTS // N_GROUPS)
    grp_score = lax.top_k(grp, 2)[0].sum(-1)
    _, gidx = lax.top_k(grp_score, TOPK_GROUPS)
    gmask = jax.nn.one_hot(gidx, N_GROUPS).sum(-2) > 0
    emask = jnp.repeat(gmask, N_EXPERTS // N_GROUPS, axis=-1)
    _, idx = lax.top_k(jnp.where(emask, biased, -jnp.inf), TOP_K)
    gw = jnp.take_along_axis(scores, idx, -1)
    gw = gw / jnp.sum(gw, -1, keepdims=True) * ROUTED_SCALE
    return idx, gw

def routed_experts(x2, idx, gw, w_gate, w_up, w_down):
    T, D = x2.shape
    A = T * TOP_K
    n_blocks = (A + N_EXPERTS * (MOE_BLOCK - 1)) // MOE_BLOCK + 1
    flat_e = idx.reshape(A)
    order = jnp.argsort(flat_e)
    e_sorted = flat_e[order]
    counts = jnp.bincount(flat_e, length=N_EXPERTS)
    padded = (counts + MOE_BLOCK - 1) // MOE_BLOCK * MOE_BLOCK
    pad_end = jnp.cumsum(padded)
    pad_start = pad_end - padded
    start = jnp.cumsum(counts) - counts
    dest = pad_start[e_sorted] + jnp.arange(A) - start[e_sorted]
    row_tok = jnp.full((n_blocks * MOE_BLOCK,), T, jnp.int32).at[dest].set((order // TOP_K).astype(jnp.int32))
    row_gate = jnp.zeros((n_blocks * MOE_BLOCK,), jnp.float32).at[dest].set(gw.reshape(A)[order])
    blk_e = jnp.minimum(jnp.searchsorted(pad_end, jnp.arange(n_blocks) * MOE_BLOCK, side='right'), N_EXPERTS - 1)
    x_pad = jnp.concatenate([x2, jnp.zeros((1, D), x2.dtype)], 0)

    def one_block(args):
        rows, gates, e = args
        xb = x_pad[rows]
        h = jax.nn.silu(xb @ w_gate[e]) * (xb @ w_up[e])
        return (h @ w_down[e]) * gates[:, None].astype(xb.dtype)

    ys = lax.map(one_block, (row_tok.reshape(n_blocks, MOE_BLOCK), row_gate.reshape(n_blocks, MOE_BLOCK), blk_e))
    return jax.ops.segment_sum(ys.reshape(-1, D), row_tok, num_segments=T + 1)[:T]

def hybrid_layer(x, gdn_buf, s0, lru_buf, h0, start_pos, gdn_chunk,
                 w_in, gdn_conv_w, gdn_a_log, gdn_dt_bias, gdn_norm_w,
                 lru_conv_w, lru_conv_b, lru_wa, lru_ba, lru_wx, lru_bx, lru_lambda,
                 w_out, ln1_g, ln1_b, router_w, router_bias,
                 exp_w_gate, exp_w_up, exp_w_down, sh_w_gate, sh_w_up, sh_w_down, ln2_g, ln2_b):
    f32 = jnp.float32
    bsz, T, _ = x.shape
    proj = x @ w_in
    qkv_raw, z, b_raw, a_raw, lx, ly = jnp.split(proj, [V_END, Z_END, B_END, A_END, LX_END], axis=-1)

    qkv, gdn_buf_new = causal_dwconv(qkv_raw, gdn_buf, gdn_conv_w)
    qkv = jax.nn.silu(qkv.astype(f32))
    q, k, v = jnp.split(qkv, [GDN_DIM, 2 * GDN_DIM], axis=-1)
    q = l2norm(q.reshape(bsz, T, GDN_HEADS, GDN_DK)) * (GDN_DK ** -0.5)
    k = l2norm(k.reshape(bsz, T, GDN_HEADS, GDN_DK))
    v = v.reshape(bsz, T, GDN_HEADS, GDN_DV)
    beta = jax.nn.sigmoid(b_raw.astype(f32))
    g = -jnp.exp(gdn_a_log.astype(f32)) * jax.nn.softplus(a_raw.astype(f32) + gdn_dt_bias.astype(f32))
    o, s_new = gdn_chunked(q, k, v, beta, g, s0.astype(f32), gdn_chunk)
    o = o * lax.rsqrt(jnp.mean(o * o, -1, keepdims=True) + RMS_EPS) * gdn_norm_w.astype(f32)
    o = o * jax.nn.silu(z.astype(f32).reshape(bsz, T, GDN_HEADS, GDN_DV))
    o = o.reshape(bsz, T, GDN_VDIM)

    xc, lru_buf_new = causal_dwconv(lx, lru_buf, lru_conv_w, lru_conv_b)
    xc = xc.astype(f32)
    xb = xc.reshape(bsz, T, LRU_BLOCKS, LRU_BW)
    r = jax.nn.sigmoid(jnp.einsum('btki,kij->btkj', xb, lru_wa.astype(f32)).reshape(bsz, T, LRU_WIDTH) + lru_ba.astype(f32))
    i = jax.nn.sigmoid(jnp.einsum('btki,kij->btkj', xb, lru_wx.astype(f32)).reshape(bsz, T, LRU_WIDTH) + lru_bx.astype(f32))
    log_a = LRU_C * r * jax.nn.log_sigmoid(lru_lambda.astype(f32))
    a = jnp.exp(log_a)
    mult = jnp.sqrt(-jnp.expm1(2.0 * log_a))
    pos = start_pos + jnp.arange(T)
    mult = jnp.where((pos == 0)[None, :, None], 1.0, mult)
    bt = mult * i * xc
    bt = bt.at[:, 0].add(a[:, 0] * h0.astype(f32))
    _, h = lax.associative_scan(_lin_combine, (a, bt), axis=1)
    h_new = h[:, -1]
    lru_out = h * jax.nn.gelu(ly.astype(f32))

    mix = jnp.concatenate([o, lru_out], -1).astype(x.dtype) @ w_out
    h1 = layer_norm(DN_ALPHA * x + mix, ln1_g, ln1_b)

    x2 = h1.reshape(-1, D_MODEL)
    idx, gw = route(x2, router_w, router_bias)
    shared = (jax.nn.silu(x2 @ sh_w_gate) * (x2 @ sh_w_up)) @ sh_w_down
    ffn = shared + routed_experts(x2, idx, gw, exp_w_gate, exp_w_up, exp_w_down).astype(shared.dtype)
    y = layer_norm(DN_ALPHA * h1 + ffn.reshape(h1.shape), ln2_g, ln2_b)
    dt = x.dtype
    return y, gdn_buf_new.astype(dt), s_new.astype(dt), lru_buf_new.astype(dt), h_new.astype(dt)

def setup_inputs(seed: int = 0) -> dict:
    key = jax.random.key(seed)
    ks = jax.random.split(key, 40)
    f32 = jnp.float32
    L = DEPTH

    def nrm(k, shape, scale):
        return jax.random.normal(k, shape, f32) * scale

    dt = jnp.exp(jax.random.uniform(ks[10], (L, GDN_HEADS), f32, math.log(1e-3), math.log(1e-1)))
    s_lam = jax.random.uniform(ks[15], (L, LRU_WIDTH), f32, 0.9, 0.999) ** (1.0 / LRU_C)
    return {
        'x_prompt': nrm(ks[0], (BATCH, SEQ, D_MODEL), 1.0),
        'x_sample': nrm(ks[1], (DEC_BATCH, DEC_SEQ, D_MODEL), 1.0),
        'state_gdn_conv': nrm(ks[2], (L, DEC_BATCH, CONV_W - 1, QKV_DIM), 1.0),
        'state_gdn': nrm(ks[3], (L, DEC_BATCH, GDN_HEADS, GDN_DK, GDN_DV), 0.5),
        'state_lru_conv': nrm(ks[4], (L, DEC_BATCH, CONV_W - 1, LRU_WIDTH), 1.0),
        'state_lru': nrm(ks[5], (L, DEC_BATCH, LRU_WIDTH), 1.0),
        'w_in': nrm(ks[6], (L, D_MODEL, IN_DIM), D_MODEL ** -0.5),
        'gdn_conv_w': nrm(ks[7], (L, CONV_W, QKV_DIM), CONV_W ** -0.5),
        'gdn_a_log': jnp.log(jax.random.uniform(ks[8], (L, GDN_HEADS), f32, 1.0, 16.0)),
        'gdn_dt_bias': dt + jnp.log(-jnp.expm1(-dt)),
        'gdn_norm_w': 1.0 + nrm(ks[9], (L, GDN_DV), 0.02),
        'lru_conv_w': nrm(ks[11], (L, CONV_W, LRU_WIDTH), CONV_W ** -0.5),
        'lru_conv_b': nrm(ks[12], (L, LRU_WIDTH), 0.02),
        'lru_wa': nrm(ks[13], (L, LRU_BLOCKS, LRU_BW, LRU_BW), LRU_BW ** -0.5),
        'lru_ba': nrm(ks[14], (L, LRU_WIDTH), 0.02),
        'lru_wx': nrm(ks[16], (L, LRU_BLOCKS, LRU_BW, LRU_BW), LRU_BW ** -0.5),
        'lru_bx': nrm(ks[17], (L, LRU_WIDTH), 0.02),
        'lru_lambda': jnp.log(s_lam) - jnp.log1p(-s_lam),
        'w_out': nrm(ks[18], (L, MIX_DIM, D_MODEL), MIX_DIM ** -0.5 * DN_BETA),
        'ln1_g': 1.0 + nrm(ks[19], (L, D_MODEL), 0.02),
        'ln1_b': nrm(ks[20], (L, D_MODEL), 0.02),
        'router_w': nrm(ks[21], (L, D_MODEL, N_EXPERTS), D_MODEL ** -0.5),
        'router_bias': nrm(ks[22], (L, N_EXPERTS), 0.01),
        'exp_w_gate': nrm(ks[23], (L, N_EXPERTS, D_MODEL, EXPERT_FF), D_MODEL ** -0.5),
        'exp_w_up': nrm(ks[24], (L, N_EXPERTS, D_MODEL, EXPERT_FF), D_MODEL ** -0.5),
        'exp_w_down': nrm(ks[25], (L, N_EXPERTS, EXPERT_FF, D_MODEL), EXPERT_FF ** -0.5 * DN_BETA),
        'sh_w_gate': nrm(ks[26], (L, D_MODEL, SHARED_FF), D_MODEL ** -0.5),
        'sh_w_up': nrm(ks[27], (L, D_MODEL, SHARED_FF), D_MODEL ** -0.5),
        'sh_w_down': nrm(ks[28], (L, SHARED_FF, D_MODEL), SHARED_FF ** -0.5 * DN_BETA),
        'ln2_g': 1.0 + nrm(ks[29], (L, D_MODEL), 0.02),
        'ln2_b': nrm(ks[30], (L, D_MODEL), 0.02),
    }

def reference(x_prompt, x_sample, state_gdn_conv, state_gdn, state_lru_conv, state_lru,
              w_in, gdn_conv_w, gdn_a_log, gdn_dt_bias, gdn_norm_w,
              lru_conv_w, lru_conv_b, lru_wa, lru_ba, lru_wx, lru_bx, lru_lambda,
              w_out, ln1_g, ln1_b, router_w, router_bias,
              exp_w_gate, exp_w_up, exp_w_down, sh_w_gate, sh_w_up, sh_w_down, ln2_g, ln2_b):
    yp, ys = x_prompt, x_sample
    bp = x_prompt.shape[0]
    gc_p, gs_p, lc_p, ls_p = [], [], [], []
    gc_s, gs_s, lc_s, ls_s = [], [], [], []
    for l in range(DEPTH):
        lw = (w_in[l], gdn_conv_w[l], gdn_a_log[l], gdn_dt_bias[l], gdn_norm_w[l],
              lru_conv_w[l], lru_conv_b[l], lru_wa[l], lru_ba[l], lru_wx[l], lru_bx[l], lru_lambda[l],
              w_out[l], ln1_g[l], ln1_b[l], router_w[l], router_bias[l],
              exp_w_gate[l], exp_w_up[l], exp_w_down[l], sh_w_gate[l], sh_w_up[l], sh_w_down[l],
              ln2_g[l], ln2_b[l])
        yp, a1, a2, a3, a4 = hybrid_layer(
            yp,
            jnp.zeros((bp, CONV_W - 1, QKV_DIM), yp.dtype),
            jnp.zeros((bp, GDN_HEADS, GDN_DK, GDN_DV), jnp.float32),
            jnp.zeros((bp, CONV_W - 1, LRU_WIDTH), yp.dtype),
            jnp.zeros((bp, LRU_WIDTH), jnp.float32),
            0, CHUNK, *lw)
        gc_p.append(a1); gs_p.append(a2); lc_p.append(a3); ls_p.append(a4)
        ys, b1, b2, b3, b4 = hybrid_layer(
            ys, state_gdn_conv[l], state_gdn[l], state_lru_conv[l], state_lru[l],
            PAST_LEN, ys.shape[1], *lw)
        gc_s.append(b1); gs_s.append(b2); lc_s.append(b3); ls_s.append(b4)
    return (yp, ys,
            jnp.stack(gc_p, 0), jnp.stack(gs_p, 0), jnp.stack(lc_p, 0), jnp.stack(ls_p, 0),
            jnp.stack(gc_s, 0), jnp.stack(gs_s, 0), jnp.stack(lc_s, 0), jnp.stack(ls_s, 0))


_drawn_inputs = setup_inputs


def setup_inputs(seed=0):
    import zlib

    import numpy as np

    out = dict(_drawn_inputs(seed))
    spreads = {}
    factors = {'gdn_norm_w': 2.821, 'lru_ba': 8.0, 'lru_bx': 7.56, 'ln2_g': 2.914, 'ln2_b': 2.769}
    for name, (base, spread) in spreads.items():
        noise = np.random.default_rng([zlib.crc32(name.encode()), seed]).standard_normal(out[name].shape)
        drawn = base * np.exp(spread * noise) if base else spread * noise
        out[name] = __import__('jax').numpy.asarray(drawn.astype(out[name].dtype))
    for name, factor in factors.items():
        out[name] = (out[name] * factor).astype(out[name].dtype)
    return out
```

```python
from contextlib import ExitStack

import numpy as np

import concourse.bass as bass
from concourse import mybir

F32 = mybir.dt.float32
BF16 = mybir.dt.bfloat16
I32 = mybir.dt.int32
U32 = mybir.dt.uint32
ALU = mybir.AluOpType
ACT = mybir.ActivationFunctionType
AX = mybir.AxisListType

P = 128
D = 1024
SEQ = 512
DEC = 32
H = 8
DC = D // P
TILES = SEQ // P
QKV = 3 * D
CONV = 4
NQ = QKV // P
NCH = 6 * D // P
LRU_C = 8.0
GAP = CONV - 1
S0 = SEQ + GAP
TW = S0 + DEC + 1
HALF = TW // 2
RW = TW + GAP
NE = 64
TOPK = 8
NG = 8
TOPG = 4
GE = NE // NG
FF = 256
FC = FF // P
T = SEQ + DEC
NB = (T * TOPK + NE * (P - 1)) // P + 1
NB2 = (NB + 1) // 2
NO_ROW = 8192.0
SCALE = 2.5
ALPHA = 2.0 ** 0.25
LN_EPS = 1e-5
RMS_EPS = 1e-6
BIG = 1e30
LEVELS = 7

CONSTS = {}
_at = 0
for _name, _n in (("ident", P), ("tri", P), ("before", P), ("ones", P), ("masks", LEVELS * P), ("future", P),
                  ("slots", P), ("experts", NE), ("row_base", TILES + 1), ("valid", TILES + 1), ("row", 1), ("block", 2 * NB2 + 1),
                  ("over", TILES + 1)):
    CONSTS[_name] = (_at, _n)
    _at += _n
N_CONSTS = _at

PARAMS = {}
_at = 0
for _name, _n in (("conv_w", 4 * 32), ("conv_b", 32), ("hist", 3 * 32), ("h0", DC), ("lam", DC), ("gate_b", 2 * DC),
                  ("dt", H), ("a_log", H), ("norm_w", 1), ("route_b", NE)):
    PARAMS[_name] = (_at, _n)
    _at += _n
N_PARAMS = _at


class Steps:

    def __init__(self, engine, sem, base=0):
        self.engine, self.sem, self.n, self.base = engine, sem, 0, base

    def done(self, instruction):
        instruction.then_inc(self.sem, 1)
        self.n += 1
        return self

    def wait(self):
        self.engine.wait_ge(self.sem, self.n + self.base)

    def link(self, instruction):
        self.done(instruction).wait()


class Views:

    def __init__(self, tile, table):
        self.tile, self.table = tile, table

    def __call__(self, name, *dims):
        at, n = self.table[name]
        view = self.tile[:, at:at + n]
        if dims:
            names = [f"d{i}" for i in range(len(dims))]
            view = view.rearrange(f"p ({' '.join(names)}) -> p {' '.join(names)}", **dict(zip(names, dims)))
        return view


def rsqrt(nc, steps, out, y, scratch, factor=1.0):
    g, h = scratch
    steps.link(nc.vector.tensor_scalar(g.bitcast(I32), y.bitcast(I32), -0.5, 1597463007.0, ALU.mult, ALU.add))
    for step in range(4):
        steps.link(nc.vector.tensor_tensor(h, g, g, ALU.mult))
        steps.link(nc.vector.tensor_tensor(h, h, y, ALU.mult))
        steps.link(nc.vector.tensor_scalar(h, h, -0.5, 1.5, ALU.mult, ALU.add))
        if step < 3:
            steps.link(nc.vector.tensor_tensor(g, g, h, ALU.mult))
        else:
            steps.link(nc.vector.scalar_tensor_tensor(out, g, factor, h, ALU.mult, ALU.mult))


class Memory:

    def __init__(self, nc, ctx):
        def sb(name, words, dt=F32):
            return ctx.enter_context(nc.sbuf_tensor(name, [P, words], dt))

        self.consts = Views(sb("consts", N_CONSTS), CONSTS)
        self.params = Views(sb("params", N_PARAMS), PARAMS)
        self.long = sb("long", 16384)
        self.zt = sb("zt", DC * TW)
        self.lru = sb("lru", DC * TW)
        self.work = sb("work", 20480)
        self.states = sb("states", 2 * H * P)
        self.decay = sb("decay", 8 * (TILES + 1) * H)
        self.bank = [ctx.enter_context(nc.psum_tensor(f"bank{i}", [P, 512], F32)) for i in range(8)]

    def carve(self, tile, at, *dims):
        n = int(np.prod(dims))
        view = tile[:, at:at + n]
        if len(dims) > 1:
            names = [f"d{i}" for i in range(len(dims))]
            view = view.rearrange(f"p ({' '.join(names)}) -> p {' '.join(names)}", **dict(zip(names, dims)))
        return view


def projection_stage(nc, mem, dram):
    with ExitStack() as ctx:
        def sem(name):
            return ctx.enter_context(nc.semaphore(name))

        C, PR = mem.consts, mem.params
        carve = mem.carve
        w_buf = [carve(mem.work, 4096 * i, DC, 512) for i in range(2)]
        x_t = carve(mem.work, 8192, DC, TW)
        t_r = carve(mem.work, 8192 + DC * TW, DC, TW)
        raw = [carve(mem.work, 8192 + 2 * DC * TW + RW * i, RW) for i in range(4)]
        conv = [carve(mem.work, 8192 + 2 * DC * TW + RW * 4 + TW * i, TW) for i in range(2)]
        qkv = carve(mem.long, 0, 24, TW)
        t_i, xc = qkv[:, 8:16, :], qkv[:, 16:24, :]
        mult = carve(mem.zt, 0, DC, TW)
        zt = mult
        lru = carve(mem.lru, 0, DC, TW)
        gates = carve(mem.states, 0, 2 * DC, P)
        n_d = (TILES + 1) * H
        beta, g_, gsum, gneg, eg, egl, egd, gtot = (
            carve(mem.decay, n_d * i, TILES + 1, H) for i in range(8))
        small = ctx.enter_context(nc.sbuf_tensor("small", [P, 640], F32))
        w_ba = carve(small, 0, DC, 2 * H)
        ba = carve(small, 128, TILES + 1, 2 * H)
        soft_x, soft_w, soft_z, soft_z2, soft_p = (carve(small, 208 + 48 * i, 48) for i in range(5))
        c_lru = carve(small, 448, DC)
        c_neg = carve(small, 456, DC)
        gate_half = carve(small, 464, 2 * DC)
        nexp_a = carve(small, 480, H)
        last_h = carve(small, 488, DC, 2)
        tails = ctx.enter_context(nc.sbuf_tensor("tails", [P, 32, 2 * GAP], F32))

        s_const, s_x, s_gates = sem("consts_loaded"), sem("x_loaded"), sem("gates_loaded")
        s_win = [sem("w_in_loaded_0"), sem("w_in_loaded_1")]
        s_proj, s_psum = sem("channels_projected"), sem("psum_read")
        s_ba = sem("ba_projected")
        s_soft_e, s_softp = sem("softplus_exp"), sem("lru_rate_ready")
        s_g, s_gs, s_gread = sem("log_decay_ready"), sem("decay_summed"), sem("decay_exp_ready")
        s_conv, s_fin = sem("conv_ready"), sem("channels_finished")
        s_gate, s_gateread = sem("gates_projected"), sem("gates_read")
        s_tanh, s_a, s_mult2, s_mult = sem("rate_tanh_ready"), sem("a_ready"), sem("mult_squared"), sem("mult_ready")
        s_lru = sem("lru_done")
        s_v = sem("vector_steps")
        s_zero = sem("pads_zeroed")
        s_out = sem("outputs_stored")
        block = ctx.enter_context(nc.Block())

        @block.sync
        def _(sp):
            sp.dma_start(mem.consts.tile[:, :], dram["consts"]).then_inc(s_const, 16)
            sp.dma_start(mem.params.tile[:, :], dram["params"]).then_inc(s_const, 16)
            sp.dma_start(x_t, dram["x_t"]).then_inc(s_x, 16)
            sp.dma_start(w_ba, dram["w_ba"]).then_inc(s_x, 16)
            for g in range(2):
                sp.dma_start(w_buf[g], dram["w_in"][g]).then_inc(s_win[g], 16)
            sp.dma_start(gates, dram["gates"]).then_inc(s_gates, 16)
            with sp.Fori(1, 6) as u:
                for g in range(2):
                    sp.wait_ge(s_proj, u * 8 + (4 * g - 4))
                    sp.dma_start(w_buf[g], dram["w_in"][bass.ds(u * 2 + g, 1)].rearrange("a p k n -> (a p) k n"))\
                        .then_inc(s_win[g], 16)
            sp.wait_ge(s_lru, 2)
            sp.dma_start(dram["lru_last"], last_h).then_inc(s_out, 16)
            sp.wait_ge(s_conv, 32)
            sp.dma_start(dram["tails"], tails[:, :, :]).then_inc(s_out, 16)
            sp.wait_ge(s_out, 32)

        def project(pe, u, g, j, first):
            n = u * 8 + (g * 4 + j)
            if not first:
                pe.wait_ge(s_psum, n - 1)
            for half in range(2):
                bank = mem.bank[2 * (j % 2) + half]
                for k in range(DC):
                    last = nc.tensor.matmul(bank[:, 0:HALF], w_buf[g][:, k, j * P:(j + 1) * P],
                                            x_t[:, k, half * HALF:(half + 1) * HALF],
                                            start=(k == 0), stop=(k == DC - 1))
            last.then_inc(s_proj, 1)
            return last

        @block.tensor
        def _(pe):
            pe.wait_ge(s_x, 32)
            for t in range(TILES + 1):
                at, w = (t * P, P) if t < TILES else (S0, DEC)
                for k in range(DC):
                    last = nc.tensor.matmul(mem.bank[4][0:w, 16 * t:16 * t + 16], x_t[:, k, at:at + w], w_ba[:, k, :],
                                            start=(k == 0), stop=(k == DC - 1))
            last.then_inc(s_ba, 1)
            for u in range(2):
                for g in range(2):
                    pe.wait_ge(s_win[g], 16 * (u + 1))
                    for j in range(4):
                        project(pe, u, g, j, u == 0 and g == 0 and j < 2)
                        if u == 0 and g == 0 and j == 1:
                            pe.wait_ge(s_g, 1)
                            nc.tensor.matmul(mem.bank[5][:, 0:n_d], C("tri"), g_.rearrange("p t h -> p (t h)"),
                                             start=True, stop=True)
                            nc.tensor.matmul(mem.bank[6][:, 0:n_d], C("ones"), g_.rearrange("p t h -> p (t h)"),
                                             start=True, stop=True).then_inc(s_gs, 1)
                        if u == 1:
                            b = 4 * g + j
                            if b == 0:
                                pe.wait_ge(s_gates, 16)
                                pe.wait_ge(s_gread, 1)
                            pe.wait_ge(s_conv, b + 1)
                            if b:
                                pe.wait_ge(s_gateread, b)
                            for m in range(2):
                                for half in range(2):
                                    last = nc.tensor.matmul(mem.bank[4 + 2 * m + half][:, 0:HALF], gates[:, m * DC + b, :],
                                                            xc[:, b, half * HALF:(half + 1) * HALF],
                                                            start=True, stop=True)
                            last.then_inc(s_gate, 1)
            with pe.Fori(2, 6) as u:
                for g in range(2):
                    pe.wait_ge(s_win[g], u * 16 + 16)
                    for j in range(4):
                        project(pe, u, g, j, False)

        def two_halves(j, out, func, **kw):
            nc.scalar.activation(out[0], mem.bank[2 * (j % 2)][:, 0:HALF], func, **kw)
            return nc.scalar.activation(out[1], mem.bank[2 * (j % 2) + 1][:, 0:HALF], func, **kw)

        def halves(x):
            return x[:, 0:HALF], x[:, HALF:TW]

        def evacuate(act, n, j, m, first):
            act.wait_ge(s_proj, n + 1)
            if not first:
                act.wait_ge(s_conv, m - 3)
            two_halves(j, halves(raw[j % 4][:, GAP:RW]), ACT.Copy).then_inc(s_psum, 1)

        @block.scalar
        def _(act):
            act.wait_ge(s_soft_e, 1)
            nc.scalar.activation(soft_w, soft_w, ACT.Exp, scale=-1.0).then_inc(s_a, 1)
            act.wait_ge(s_const, 32)
            nc.scalar.activation(nexp_a, PR("a_log"), ACT.Exp).then_inc(s_a, 1)
            nc.scalar.activation(beta, ba[:, :, 0:H], ACT.Tanh, scale=0.5).then_inc(s_a, 1)
            for j in range(2):
                evacuate(act, j, j, j, True)
            act.wait_ge(s_gs, 1)
            flat = [v.rearrange("p t h -> p (t h)") for v in (gsum, gneg, eg, egl, gtot)]
            nc.scalar.activation(flat[0], mem.bank[5][:, 0:n_d], ACT.Copy)
            nc.scalar.activation(flat[1], mem.bank[5][:, 0:n_d], ACT.Copy, scale=-1.0)
            nc.scalar.activation(flat[2], mem.bank[5][:, 0:n_d], ACT.Exp)
            nc.scalar.activation(flat[4], mem.bank[6][:, 0:n_d], ACT.Copy)
            nc.scalar.activation(flat[3], mem.bank[6][:, 0:n_d], ACT.Exp).then_inc(s_gread, 1)
            for j in range(2, 8):
                evacuate(act, j, j, j, j < 4)
            for j in range(8):
                act.wait_ge(s_proj, 8 + j + 1)
                two_halves(j, halves(lru[:, j, :]), ACT.Gelu_apprx_tanh).then_inc(s_psum, 1)
                act.wait_ge(s_gate, j + 1)
                if j == 0:
                    act.wait_ge(s_softp, 1)
                for m, out in enumerate((t_r, t_i)):
                    for half, part in enumerate(halves(out[:, j, :])):
                        last = nc.scalar.activation(part, mem.bank[4 + 2 * m + half][:, 0:HALF], ACT.Tanh,
                                                    bias=gate_half[:, m * DC + j:m * DC + j + 1], scale=0.5)
                last.then_inc(s_gateread, 1)
            act.wait_ge(s_gateread, 8)
            for j in range(8):
                last = nc.scalar.activation(mult[:, j, :], t_r[:, j, :], ACT.Tanh, bias=c_neg[:, j:j + 1],
                                            scale=c_neg[:, j:j + 1])
            last.then_inc(s_tanh, 1)
            for j in range(8):
                last = nc.scalar.activation(t_r[:, j, :], t_r[:, j, :], ACT.Exp, bias=c_lru[:, j:j + 1],
                                            scale=c_lru[:, j:j + 1])
            last.then_inc(s_a, 1)
            act.wait_ge(s_mult2, 1)
            nc.scalar.activation(mult, mult, ACT.Sqrt).then_inc(s_mult, 1)

            def silu(u, j):
                act.wait_ge(s_conv, u * 8 + (j - 8 + 1))
                nc.scalar.activation(qkv[:, bass.ds(u * 8 + (j - 16), 1), :].rearrange("p a t -> p (a t)"),
                                     conv[j % 2], ACT.Silu).then_inc(s_fin, 1)

            def convolved_unit(u):
                for j in range(8):
                    evacuate(act, u * 8 + j, j, u * 8 + (j - 8), False)
                    if j:
                        silu(u, j - 1)
                silu(u, 7)

            convolved_unit(2)
            act.wait_ge(s_lru, 1)
            with act.Fori(3, 5) as u:
                convolved_unit(u)
            act.wait_ge(s_lru, 2)
            for j in range(8):
                act.wait_ge(s_proj, 40 + j + 1)
                two_halves(j, halves(zt[:, j, :]), ACT.Silu).then_inc(s_psum, 1)

        def convolve(dve, steps, n, m, j, out):
            r = raw[j % 4]
            one = (lambda name, k: PR(name)[:, bass.ds(m * k[0] + k[1], k[2])])
            dve.wait_ge(s_psum, n + 1)
            steps.link(nc.vector.tensor_scalar(r[:, S0:S0 + GAP], one("hist", (3, 0, 3)), 1.0, None, ALU.mult))
            for which, at in enumerate((SEQ, S0 + DEC)):
                nc.vector.tensor_scalar(tails[:, bass.ds(m, 1), GAP * which:GAP * (which + 1)]
                                        .rearrange("p a t -> p (a t)"), r[:, at:at + GAP], 1.0, None, ALU.mult)
            acc = conv[j % 2]
            steps.link(nc.vector.tensor_scalar(acc, r[:, 0:TW], one("conv_w", (4, 0, 1)), one("conv_b", (1, 0, 1)),
                                               ALU.mult, ALU.add))
            for k in range(1, CONV):
                last = nc.vector.scalar_tensor_tensor(out if k == CONV - 1 else acc, r[:, k:k + TW],
                                                      one("conv_w", (4, k, 1)), acc, ALU.mult, ALU.add)
                if k < CONV - 1:
                    steps.link(last)
            return last

        LINKS = 4

        @block.vector
        def _(dve):
            steps = Steps(dve, s_v)
            for r in raw:
                nc.vector.memset(r[:, 0:GAP], 0.0)
            last = nc.vector.memset(ba, 0.0)
            last.then_inc(s_zero, 1)
            dve.wait_ge(s_const, 32)
            dve.wait_ge(s_ba, 1)
            dve.wait_ge(s_zero, 1)
            nc.vector.tensor_copy(ba[:, 0:TILES, :], mem.bank[4][:, 0:16 * TILES].rearrange("p (t c) -> p t c", c=16))
            steps.link(nc.vector.tensor_copy(ba[0:DEC, TILES, :], mem.bank[4][0:DEC, 16 * TILES:16 * TILES + 16]))
            nc.vector.tensor_scalar(soft_x[:, 0:DC], PR("lam"), -1.0, None, ALU.mult)
            steps.link(nc.vector.tensor_tensor(
                soft_x[:, DC:].rearrange("p (t h) -> p t h", h=H), ba[:, :, H:2 * H],
                PR("dt").unsqueeze(1).to_broadcast([P, TILES + 1, H]), ALU.add))
            steps.link(nc.vector.tensor_scalar(soft_w, soft_x, -1.0, None, ALU.mult))
            nc.vector.tensor_tensor(soft_w, soft_w, soft_x, ALU.max).then_inc(s_soft_e, 1)
            dve.wait_ge(s_a, 1)
            steps.link(nc.vector.tensor_scalar(soft_z, soft_w, 2.0, None, ALU.add))
            steps.link(nc.vector.reciprocal(soft_z, soft_z))
            steps.link(nc.vector.tensor_tensor(soft_z, soft_z, soft_w, ALU.mult))
            steps.link(nc.vector.tensor_tensor(soft_z2, soft_z, soft_z, ALU.mult))
            steps.link(nc.vector.tensor_scalar(soft_p, soft_z2, 1.0 / 15, None, ALU.mult))
            for odd in (13, 11, 9, 7, 5, 3):
                steps.link(nc.vector.scalar_tensor_tensor(soft_p, soft_p, 1.0 / odd, soft_z2, ALU.add, ALU.mult))
            steps.link(nc.vector.scalar_tensor_tensor(soft_p, soft_p, 1.0, soft_z, ALU.add, ALU.mult))
            steps.link(nc.vector.tensor_scalar(soft_x, soft_x, 0.0, None, ALU.max))
            steps.link(nc.vector.scalar_tensor_tensor(soft_x, soft_p, 2.0, soft_x, ALU.mult, ALU.add))
            nc.vector.tensor_scalar(c_lru, soft_x[:, 0:DC], -0.5 * LRU_C, None, ALU.mult)
            nc.vector.tensor_scalar(c_neg, soft_x[:, 0:DC], 0.5 * LRU_C, None, ALU.mult)
            nc.vector.tensor_scalar(gate_half, PR("gate_b"), 0.5, None, ALU.mult).then_inc(s_softp, 1)
            dve.wait_ge(s_a, 3)
            valid = C("valid").unsqueeze(2).to_broadcast([P, TILES + 1, H])
            steps.link(nc.vector.tensor_scalar(nexp_a, nexp_a, -1.0, None, ALU.mult))
            steps.link(nc.vector.tensor_tensor(g_, soft_x[:, DC:].rearrange("p (t h) -> p t h", h=H),
                                               nexp_a.unsqueeze(1).to_broadcast([P, TILES + 1, H]), ALU.mult))
            nc.vector.tensor_tensor(g_, g_, valid, ALU.mult).then_inc(s_g, 1)
            steps.link(nc.vector.tensor_scalar(beta, beta, 0.5, 0.5, ALU.mult, ALU.add))
            steps.link(nc.vector.tensor_tensor(beta, beta, valid, ALU.mult))
            for j in range(8):
                convolve(dve, steps, j, j, j, xc[:, j, :]).then_inc(s_conv, 1)
            dve.wait_ge(s_gateread, 8)
            steps.link(nc.vector.scalar_tensor_tensor(t_i, t_i, 1.0, xc, ALU.add, ALU.mult))
            dve.wait_ge(s_tanh, 1)
            flat = mult.rearrange("p k t -> p (k t)")
            m2 = xc.rearrange("p k t -> p (k t)")
            steps.link(nc.vector.tensor_scalar(m2, flat, 1.0, None, ALU.add))
            steps.link(nc.vector.reciprocal(m2, m2))
            nc.vector.scalar_tensor_tensor(flat, m2, 2.0, flat, ALU.mult, ALU.mult).then_inc(s_mult2, 1)
            dve.wait_ge(s_mult, 1)
            steps.link(nc.vector.memset(mult[:, :, 0:1], 1.0))
            steps.link(nc.vector.scalar_tensor_tensor(t_i, t_i, 0.5, mult, ALU.mult, ALU.mult))
            dve.wait_ge(s_a, 4)
            for j in range(8):
                nc.vector.tensor_tensor_scan(out=mult[:, j, 0:S0], data0=t_r[:, j, 0:S0], data1=t_i[:, j, 0:S0],
                                             initial=0.0, op0=ALU.mult, op1=ALU.add)
                last = nc.vector.tensor_tensor_scan(out=mult[:, j, S0:TW], data0=t_r[:, j, S0:TW],
                                                    data1=t_i[:, j, S0:TW], initial=PR("h0")[:, j:j + 1],
                                                    op0=ALU.mult, op1=ALU.add)
            last.then_inc(s_lru, 1)
            dve.wait_ge(s_lru, 1)
            nc.vector.tensor_copy(last_h[:, :, 0:1], mult[:, :, SEQ - 1:SEQ])
            nc.vector.tensor_copy(last_h[:, :, 1:2], mult[:, :, S0 + DEC - 1:S0 + DEC])
            nc.vector.tensor_tensor(lru, lru, mult, ALU.mult).then_inc(s_lru, 1)
            base = steps.n
            with dve.Fori(2, 5) as u:
                inner = Steps(dve, s_v, u * (8 * LINKS) + (base - 16 * LINKS))
                for j in range(8):
                    dve.wait_ge(s_fin, u * 8 + ((j - 1 if j >= 2 else 0) - 16))
                    convolve(dve, inner, u * 8 + j, u * 8 + (j - 8), j, conv[j % 2]).then_inc(s_conv, 1)
                assert inner.n == 8 * LINKS


def token_tiles():
    return [(t, t * P, P, LEVELS, 0) for t in range(TILES)] + [(TILES, S0, DEC, 5, 1)]


def delta_rule_stage(nc, mem, dram):
    with ExitStack() as ctx:
        def sem(name):
            return ctx.enter_context(nc.semaphore(name))

        C, PR = mem.consts, mem.params
        carve = mem.carve
        qkv = carve(mem.long, 0, 24, TW)
        zt = carve(mem.zt, 0, DC, TW)
        state = [carve(mem.states, H * P * i, H, P) for i in range(2)]
        n_d = (TILES + 1) * H
        beta, g_, gsum, gneg, eg, egl, egd, gtot = (carve(mem.decay, n_d * i, TILES + 1, H) for i in range(8))
        squares = carve(mem.work, 0, 2 * H, P)
        (rg, decay, lower_t, attn_t, x_inv, x_inv_t, joined, v_beta, k_dec, rhs, new, o_state, o, o_sq) = (
            carve(mem.work, 2 * H * P + H * P * i, H, P) for i in range(14))
        small = ctx.enter_context(nc.sbuf_tensor("factors", [P, 160], F32))
        norm, norm_a, norm_b, norm_c = (carve(small, 16 * i, 2 * H) for i in range(4))
        row_f, ks_f, kd_f, qs_f, o_sum, o_a, o_b, o_rs = (carve(small, 64 + 8 * i, H) for i in range(8))
        ident_b = ctx.enter_context(nc.sbuf_tensor("ident_bf16", [P, P], BF16))
        future_b = ctx.enter_context(nc.sbuf_tensor("future_bf16", [P, 4 * P], BF16))

        s_state, s_setup, s_egd = sem("state_loaded"), sem("masks_ready"), sem("decay_to_end_ready")
        s_sq, s_ss = sem("squares_ready"), sem("square_sums_ready")
        s_vt, s_kt = sem("v_transposed"), sem("k_transposed")
        s_vb, s_kd = sem("v_beta_ready"), sem("k_decayed_ready")
        s_norm, s_rg, s_grow, s_et = sem("factors_ready"), sem("decay_rows_ready"), sem("decay_sums_ready"), sem("decay_ready")
        s_kk, s_kq, s_u, s_at = sem("kk_ready"), sem("kq_ready"), sem("lower_ready"), sem("attention_ready")
        s_pa, s_p, s_px, s_x = sem("join_product"), sem("join_ready"), sem("join_applied"), sem("inverse_ready")
        s_ks, s_r, s_vn, s_vns = sem("k_state_ready"), sem("rhs_ready"), sem("new_values"), sem("new_values_read")
        s_os, s_osr, s_oa, s_o = sem("q_state_ready"), sem("q_state_read"), sem("attended"), sem("o_ready")
        s_su, s_s = sem("state_update"), sem("state_ready")
        s_on, s_ot, s_otr = sem("o_normed"), sem("o_transposed"), sem("o_gated")
        s_v = sem("delta_vector_steps")
        s_out = sem("states_stored")
        block = ctx.enter_context(nc.Block())
        groups = [(g, slice(4 * g, 4 * g + 4)) for g in range(2)]

        def in_bank(b, rows, width):
            return mem.bank[b][0:rows, :].rearrange("p (h i) -> p h i", h=4)[:, :, 0:width]

        def inverse_steps(t, level, g):
            return 2 * LEVELS * t + 2 * level + g + 1

        @block.sync
        def _(sp):
            sp.dma_start(state[1], dram["state"]).then_inc(s_state, 16)
            sp.wait_ge(s_s, 2 * TILES)
            sp.dma_start(dram["states"][0], state[0]).then_inc(s_out, 16)
            sp.wait_ge(s_s, 2 * TILES + 2)
            sp.dma_start(dram["states"][1], state[1]).then_inc(s_out, 16)
            sp.wait_ge(s_out, 32)

        @block.tensor
        def _(pe):
            pe.wait_ge(s_setup, 1)
            for t, at, w, levels, stream in token_tiles():
                q, k, v = (qkv[:, 8 * i:8 * i + 8, at:at + w] for i in range(3))
                pe.wait_ge(s_sq, t + 1)
                if t:
                    pe.wait_ge(s_osr, 2 * t)
                for j in range(2 * H):
                    last = nc.tensor.matmul(mem.bank[6][0:w, j:j + 1], squares[:, j, 0:w], C("ones")[:, 0:1],
                                            start=True, stop=True)
                last.then_inc(s_ss, 1)
                for g, hs in groups:
                    if t:
                        pe.wait_ge(s_s, 2 * t)
                    for h in range(4):
                        last = nc.tensor.transpose(in_bank(g, w, P)[:, h, :], v[:, 4 * g + h, :], C("ident"))
                    last.then_inc(s_vt, 1)
                for g, hs in groups:
                    if t:
                        pe.wait_ge(s_o, 2 * t)
                    for h in range(4):
                        last = nc.tensor.transpose(in_bank(2 + g, w, P)[:, h, :], k[:, 4 * g + h, :], C("ident"))
                    last.then_inc(s_kt, 1)
                for g, hs in groups:
                    if t:
                        pe.wait_ge(s_otr, 2 * t)
                    pe.wait_ge(s_rg, 2 * t + g + 1)
                    nc.tensor.matmul(in_bank(4 + g, w, w), C("ones")[0:w, 0:w], rg[0:w, hs, 0:w], start=True, stop=False)
                    nc.tensor.matmul(in_bank(4 + g, w, w), ident_b[0:w, 0:w],
                                     future_b[0:w, :].rearrange("p (h i) -> p h i", h=4)[:, :, 0:w],
                                     start=False, stop=True).then_inc(s_grow, 1)
                for g, hs in groups:
                    pe.wait_ge(s_vb, 2 * t + g + 1)
                    for h in range(4):
                        last = nc.tensor.matmul(in_bank(g, w, w)[:, h, :], k[:, 4 * g + h, :], k[:, 4 * g + h, :],
                                                start=True, stop=True)
                    last.then_inc(s_kk, 1)
                for g, hs in groups:
                    pe.wait_ge(s_kd, 2 * t + g + 1)
                    for h in range(4):
                        last = nc.tensor.matmul(in_bank(2 + g, w, w)[:, h, :], k[:, 4 * g + h, :], q[:, 4 * g + h, :],
                                                start=True, stop=True)
                    last.then_inc(s_kq, 1)
                for g, hs in groups:
                    pe.wait_ge(s_norm, t + 1)
                    if stream:
                        pe.wait_ge(s_state, 16)
                    elif t:
                        pe.wait_ge(s_s, 2 * t)
                    for h in range(4):
                        last = nc.tensor.matmul(in_bank(6 + g, w, P)[:, h, :], k[:, 4 * g + h, :],
                                                state[stream][:, 4 * g + h, :], start=True, stop=True)
                    last.then_inc(s_ks, 1)
                for level in range(levels):
                    for g, hs in groups:
                        if level:
                            pe.wait_ge(s_x, inverse_steps(t, level - 1, g))
                        else:
                            pe.wait_ge(s_u, 2 * t + g + 1)
                            pe.wait_ge(s_et, 2 * t + g + 1)
                        for h in range(4):
                            last = nc.tensor.matmul(in_bank(4 + g, w, w)[:, h, :], lower_t[0:w, 4 * g + h, 0:w],
                                                    x_inv[0:w, 4 * g + h, 0:w] if level else C("ident")[0:w, 0:w],
                                                    start=True, stop=True)
                        last.then_inc(s_pa, 1)
                    for g, hs in groups:
                        pe.wait_ge(s_p, inverse_steps(t, level, g))
                        if not level:
                            pe.wait_ge(s_at, 2 * t + g + 1)
                        for h in range(4):
                            if 0 < level < levels - 1:
                                nc.tensor.matmul(in_bank(g, w, w)[:, h, :], x_inv_t[0:w, 4 * g + h, 0:w],
                                                 joined[0:w, 4 * g + h, 0:w], start=True, stop=True)
                            last = nc.tensor.matmul(in_bank(2 + g, w, w)[:, h, :], joined[0:w, 4 * g + h, 0:w],
                                                    x_inv_t[0:w, 4 * g + h, 0:w] if level else C("ident")[0:w, 0:w],
                                                    start=True, stop=True)
                        last.then_inc(s_px, 1)
                for g, hs in groups:
                    pe.wait_ge(s_r, 2 * t + g + 1)
                    pe.wait_ge(s_x, inverse_steps(t, levels - 1, g))
                    for h in range(4):
                        last = nc.tensor.matmul(in_bank(4 + g, w, P)[:, h, :], x_inv_t[0:w, 4 * g + h, 0:w],
                                                rhs[0:w, 4 * g + h, :], start=True, stop=True)
                    last.then_inc(s_vn, 1)
                for g, hs in groups:
                    for h in range(4):
                        last = nc.tensor.matmul(in_bank(6 + g, w, P)[:, h, :], q[:, 4 * g + h, :],
                                                state[stream][:, 4 * g + h, :], start=True, stop=True)
                    last.then_inc(s_os, 1)
                for g, hs in groups:
                    pe.wait_ge(s_vns, 2 * t + g + 1)
                    for h in range(4):
                        last = nc.tensor.matmul(in_bank(2 + g, w, P)[:, h, :], attn_t[0:w, 4 * g + h, 0:w],
                                                new[0:w, 4 * g + h, :], start=True, stop=True)
                    last.then_inc(s_oa, 1)
                for g, hs in groups:
                    for h in range(4):
                        last = nc.tensor.matmul(in_bank(g, P, P)[:, h, :], k_dec[0:w, 4 * g + h, :],
                                                new[0:w, 4 * g + h, :], start=True, stop=True)
                    last.then_inc(s_su, 1)
                for g, hs in groups:
                    pe.wait_ge(s_on, t + 1)
                    for h in range(4):
                        last = nc.tensor.transpose(in_bank(4 + g, P, w)[:, h, :], o[0:w, 4 * g + h, :],
                                                   C("ident")[0:w, 0:w])
                    last.then_inc(s_ot, 1)

        @block.scalar
        def _(act):
            act.wait_ge(s_setup, 1)
            nc.scalar.activation(egd, egd, ACT.Exp).then_inc(s_egd, 1)
            for t, at, w, levels, stream in token_tiles():
                if t:
                    act.wait_ge(s_ss, t)
                nc.scalar.activation(squares[:, :, 0:w], qkv[:, 0:2 * H, at:at + w], ACT.Square).then_inc(s_sq, 1)
                for g, hs in groups:
                    act.wait_ge(s_vt, 2 * t + g + 1)
                    if t:
                        act.wait_ge(s_r, 2 * t)
                    for h in range(4):
                        last = nc.scalar.activation(v_beta[0:w, 4 * g + h, :], in_bank(g, w, P)[:, h, :], ACT.Copy,
                                                    scale=beta[0:w, t, 4 * g + h:4 * g + h + 1])
                    last.then_inc(s_vb, 1)
                act.wait_ge(s_norm, t + 1)
                for g, hs in groups:
                    act.wait_ge(s_kt, 2 * t + g + 1)
                    if t:
                        act.wait_ge(s_su, 2 * t)
                    for h in range(4):
                        last = nc.scalar.activation(k_dec[0:w, 4 * g + h, :], in_bank(2 + g, w, P)[:, h, :], ACT.Copy,
                                                    scale=kd_f[0:w, 4 * g + h:4 * g + h + 1])
                    last.then_inc(s_kd, 1)
                for g, hs in groups:
                    act.wait_ge(s_grow, 2 * t + g + 1)
                    if t:
                        act.wait_ge(s_at, 2 * t)
                    for h in range(4):
                        last = nc.scalar.activation(decay[0:w, 4 * g + h, 0:w], in_bank(4 + g, w, w)[:, h, :], ACT.Exp,
                                                    bias=gneg[0:w, t, 4 * g + h:4 * g + h + 1])
                    last.then_inc(s_et, 1)
                for g, hs in groups:
                    act.wait_ge(s_vn, 2 * t + g + 1)
                    if t:
                        act.wait_ge(s_su, 2 * t)
                    nc.scalar.activation(new[0:w, hs, :], in_bank(4 + g, w, P), ACT.Copy).then_inc(s_vns, 1)
                for g, hs in groups:
                    act.wait_ge(s_os, 2 * t + g + 1)
                    if t:
                        act.wait_ge(s_o, 2 * t)
                    for h in range(4):
                        last = nc.scalar.activation(o_state[0:w, 4 * g + h, :], in_bank(6 + g, w, P)[:, h, :], ACT.Copy,
                                                    scale=qs_f[0:w, 4 * g + h:4 * g + h + 1])
                    last.then_inc(s_osr, 1)

        @block.vector
        def _(dve):
            steps = Steps(dve, s_v)
            nc.vector.memset(state[0], 0.0)
            nc.vector.tensor_copy(ident_b[:, :], C("ident"))
            nc.vector.tensor_copy(future_b[:, :].rearrange("p (h i) -> p h i", h=4),
                                  C("future").unsqueeze(1).to_broadcast([P, 4, P]))
            nc.vector.tensor_tensor(egd, gtot, gsum, ALU.subtract).then_inc(s_setup, 1)
            dve.wait_ge(s_egd, 1)
            for t, at, w, levels, stream in token_tiles():
                for g, hs in groups:
                    if t:
                        dve.wait_ge(s_grow, 2 * t)
                    for h in range(4 * g, 4 * g + 4):
                        last = nc.vector.tensor_scalar(rg[0:w, h, 0:w], C("tri")[0:w, 0:w], g_[0:w, t, h:h + 1], None,
                                                       ALU.mult)
                    last.then_inc(s_rg, 1)
                dve.wait_ge(s_ss, t + 1)
                if t:
                    dve.wait_ge(s_osr, 2 * t)
                steps.link(nc.vector.tensor_scalar(norm_a[0:w], mem.bank[6][0:w, 0:2 * H], 1e-6, None, ALU.add))
                rsqrt(nc, steps, norm[0:w], norm_a[0:w], (norm_b[0:w], norm_c[0:w]))
                rk, rq = norm[0:w, H:2 * H], norm[0:w, 0:H]
                steps.done(nc.vector.tensor_scalar(rq, rq, P ** -0.5, None, ALU.mult))
                steps.done(nc.vector.tensor_tensor(row_f[0:w], rk, beta[0:w, t, :], ALU.mult))
                steps.done(nc.vector.tensor_tensor(kd_f[0:w], rk, egd[0:w, t, :], ALU.mult)).wait()
                steps.link(nc.vector.tensor_tensor(ks_f[0:w], row_f[0:w], eg[0:w, t, :], ALU.mult))
                steps.link(nc.vector.tensor_scalar(ks_f[0:w], ks_f[0:w], -1.0, None, ALU.mult))
                nc.vector.tensor_tensor(qs_f[0:w], rq, eg[0:w, t, :], ALU.mult).then_inc(s_norm, 1)
                for out, done, ready in ((lower_t, s_u, s_kk), (attn_t, s_at, s_kq)):
                    for g, hs in groups:
                        dve.wait_ge(ready, 2 * t + g + 1)
                        dve.wait_ge(s_et, 2 * t + g + 1)
                        for h in range(4):
                            n = 4 * g + h
                            last = nc.vector.scalar_tensor_tensor(
                                out[0:w, n, 0:w], in_bank(g + (2 if out is attn_t else 0), w, w)[:, h, :],
                                norm[0:w, H + n:H + n + 1], decay[0:w, n, 0:w], ALU.mult, ALU.mult)
                        last.then_inc(done, 1)
                for g, hs in groups:
                    dve.wait_ge(s_ks, 2 * t + g + 1)
                    dve.wait_ge(s_vb, 2 * t + g + 1)
                    for h in range(4):
                        n = 4 * g + h
                        last = nc.vector.scalar_tensor_tensor(rhs[0:w, n, :], in_bank(6 + g, w, P)[:, h, :],
                                                              ks_f[0:w, n:n + 1], v_beta[0:w, n, :], ALU.mult, ALU.add)
                    last.then_inc(s_r, 1)
                eye = C("ident")[0:w, 0:w].unsqueeze(1).to_broadcast([w, 4, w])
                for level in range(levels):
                    mask = C("masks")[0:w, P * level:P * level + w]
                    for g, hs in groups:
                        dve.wait_ge(s_pa, inverse_steps(t, level, g))
                        for h in range(4):
                            n = 4 * g + h
                            last = nc.vector.scalar_tensor_tensor(joined[0:w, n, 0:w], in_bank(4 + g, w, w)[:, h, :],
                                                                  row_f[0:w, n:n + 1], mask, ALU.mult, ALU.mult)
                        last.then_inc(s_p, 1)
                    for g, hs in groups:
                        if not level:
                            dve.wait_ge(s_p, inverse_steps(t, level, g))
                            nc.vector.tensor_tensor(x_inv[0:w, hs, 0:w], eye, joined[0:w, hs, 0:w], ALU.subtract)
                        dve.wait_ge(s_px, inverse_steps(t, level, g))
                        if 0 < level < levels - 1:
                            nc.vector.tensor_tensor(x_inv[0:w, hs, 0:w], x_inv[0:w, hs, 0:w], in_bank(g, w, w),
                                                    ALU.subtract)
                        nc.vector.tensor_tensor(x_inv_t[0:w, hs, 0:w], x_inv_t[0:w, hs, 0:w] if level else eye,
                                                in_bank(2 + g, w, w), ALU.subtract).then_inc(s_x, 1)
                if stream:
                    pass
                for g, hs in groups:
                    dve.wait_ge(s_oa, 2 * t + g + 1)
                    dve.wait_ge(s_osr, 2 * t + g + 1)
                    if t:
                        dve.wait_ge(s_ot, 2 * t)
                    for h in range(4):
                        n = 4 * g + h
                        last = nc.vector.scalar_tensor_tensor(o[0:w, n, :], in_bank(2 + g, w, P)[:, h, :],
                                                              norm[0:w, n:n + 1], o_state[0:w, n, :], ALU.mult, ALU.add)
                    last.then_inc(s_o, 1)
                for g, hs in groups:
                    dve.wait_ge(s_su, 2 * t + g + 1)
                    for h in range(4):
                        n = 4 * g + h
                        last = nc.vector.scalar_tensor_tensor(state[stream][:, n, :], state[stream][:, n, :],
                                                              egl[:, t, n:n + 1], in_bank(g, P, P)[:, h, :],
                                                              ALU.mult, ALU.add)
                    last.then_inc(s_s, 1)
                dve.wait_ge(s_o, 2 * t + 2)
                steps.link(nc.vector.tensor_tensor(o_sq[0:w], o[0:w], o[0:w], ALU.mult))
                steps.link(nc.vector.tensor_reduce(o_sum[0:w], o_sq[0:w], AX.X, ALU.add))
                steps.link(nc.vector.tensor_scalar(o_sum[0:w], o_sum[0:w], 1.0 / P, RMS_EPS, ALU.mult, ALU.add))
                rsqrt(nc, steps, o_rs[0:w], o_sum[0:w], (o_a[0:w], o_b[0:w]))
                nc.vector.tensor_tensor(o[0:w], o[0:w], o_rs[0:w].unsqueeze(2).to_broadcast([w, H, P]), ALU.mult)\
                    .then_inc(s_on, 1)
                for g, hs in groups:
                    dve.wait_ge(s_ot, 2 * t + g + 1)
                    nc.vector.scalar_tensor_tensor(zt[:, hs, at:at + w], in_bank(4 + g, P, w), PR("norm_w"),
                                                   zt[:, hs, at:at + w], ALU.mult, ALU.mult).then_inc(s_otr, 1)


class Routing:

    def __init__(self, mem):
        at = 0

        def take(*dims):
            nonlocal at
            view = mem.carve(mem.states, at, *dims)
            at += int(np.prod(dims))
            return view

        self.chosen = take(TILES + 1, NE)
        self.dest = take(TILES + 1, NE)
        self.row = take(TILES + 1, NE)
        self.weight = take(TILES + 1, TOPK)
        self.block_expert = take(P).bitcast(I32)
        self.n_blocks = take(2).bitcast(I32)
        self.count, self.n, self.upto, self.first = (take(NE) for _ in range(4))
        self.over = take(NE, TILES + 1)
        self.block_col = take(2)


def layer_norm(nc, steps, x, stats, gain, bias, out):
    for i in range(2):
        last = nc.vector.bn_stats(stats[:, 6 * i:6 * i + 6], x[:, 512 * i:512 * i + 512])
    steps.link(last)
    steps.link(nc.vector.bn_aggr(stats[:, 12:14], stats[:, 0:12]))
    steps.link(nc.vector.tensor_scalar(stats[:, 14:15], stats[:, 13:14], LN_EPS, None, ALU.add))
    rsqrt(nc, steps, stats[:, 15:16], stats[:, 14:15], (stats[:, 16:17], stats[:, 17:18]))
    steps.link(nc.vector.tensor_scalar(x, x, stats[:, 12:13], stats[:, 15:16], ALU.subtract, ALU.mult))
    steps.link(nc.vector.tensor_tensor(x, x, gain, ALU.mult))
    return nc.vector.tensor_tensor(out, x, bias, ALU.add)


def mixing_stage(nc, mem, dram, route):
    with ExitStack() as ctx:
        def sem(name):
            return ctx.enter_context(nc.semaphore(name))

        C, PR = mem.consts, mem.params
        carve = mem.carve
        zt = carve(mem.zt, 0, DC, TW)
        lru = carve(mem.lru, 0, DC, TW)
        w_out = carve(mem.long, 0, 2 * DC, D)
        at = 0

        def take(*dims):
            nonlocal at
            view = carve(mem.work, at, *dims)
            at += int(np.prod(dims))
            return view

        w_gu, w_dn, w_router, ln = take(DC, 2 * FF), take(FC, D), take(DC, NE), take(2, D)
        x = [take(D) for _ in range(2)]
        x1, h1_t = take(D), take(DC, P)
        h1 = [take(D) for _ in range(2)]
        acc = [take(D) for _ in range(2)]
        act_g, hidden, hidden_t = take(FF), take(FF), take(FC, P)
        stats, scores, biased, masked = take(32), take(NE), take(NE), take(NE)
        best, group, group_best, group_f = take(NG, 8), take(NG), take(NG), take(NG)
        group_i, top_i = take(8).bitcast(U32), take(8).bitcast(U32)
        group_eq, group_on, penalty, top_v, total = take(NG, TOPG), take(NG), take(NG), take(8), take(2)
        expert, which = take(TOPK), take(NE)
        hot, hot_s = take(TOPK, NE), take(TOPK, NE)
        assert at <= 20480

        s_w = [sem(f"w_out_loaded_{i}") for i in range(4)]
        s_sh = sem("shared_loaded")
        s_x = [sem("x_loaded_0"), sem("x_loaded_1")]
        s_mix, s_x1, s_h1, s_ht, s_htr = sem("mixed"), sem("mix_read"), sem("h1_ready"), sem("h1_transposed"), sem("h1_t_ready")
        s_ro, s_sc, s_gu, s_g, s_hid = sem("routed_scores"), sem("scores_read"), sem("shared_up"), sem("shared_gate_ready"), sem("shared_hidden")
        s_hdt, s_hdr, s_dn, s_acc = sem("hidden_transposed"), sem("hidden_t_ready"), sem("shared_down"), sem("residual_ready")
        s_h1out = [sem("h1_stored_0"), sem("h1_stored_1")]
        s_accout = [sem("residual_stored_0"), sem("residual_stored_1")]
        s_sel, s_rank, s_eb, s_ebt, s_v = sem("chosen_ready"), sem("ranks_ready"), sem("block_experts"), sem("block_experts_row"), sem("mix_vector_steps")
        block = ctx.enter_context(nc.Block())
        tiles = token_tiles()
        h1_rows, acc_rows = dram["h1"], dram["residual"]

        @block.sync
        def _(sp):
            for i in range(4):
                sp.dma_start(w_out[:, 4 * i:4 * i + 4, :], dram["w_out"][:, 4 * i:4 * i + 4, :]).then_inc(s_w[i], 16)
            sp.dma_start(x[0], dram["x_rows"][0:P, :]).then_inc(s_x[0], 16)
            sp.dma_start(x[1], dram["x_rows"][P:2 * P, :]).then_inc(s_x[1], 16)
            n_gu = DC * 2 * FF
            sp.dma_start(w_gu, dram["w_sh"][:, 0:n_gu].rearrange("p (k n) -> p k n", k=DC)).then_inc(s_sh, 16)
            sp.dma_start(w_dn, dram["w_sh"][:, n_gu:].rearrange("p (k n) -> p k n", k=FC)).then_inc(s_sh, 16)
            sp.dma_start(w_router, dram["w_router"]).then_inc(s_sh, 16)
            sp.dma_start(ln, dram["norms"][:, 0:2, :]).then_inc(s_sh, 16)
            for t, _, w, _, _ in tiles:
                rows = slice(P * t, P * t + w)
                sp.wait_ge(s_h1, t + 1)
                sp.dma_start(h1_rows[rows, :], h1[t % 2][0:w]).then_inc(s_h1out[t % 2], 16)
                if t + 2 <= TILES:
                    w2 = tiles[t + 2][2]
                    sp.dma_start(x[t % 2][0:w2], dram["x_rows"][P * (t + 2):P * (t + 2) + w2, :]).then_inc(s_x[t % 2], 16)
                sp.wait_ge(s_acc, t + 1)
                sp.dma_start(acc_rows[rows, :], acc[t % 2][0:w]).then_inc(s_accout[t % 2], 16)
            for i, n in ((0, 3), (1, 2)):
                sp.wait_ge(s_h1out[i], 16 * n)
                sp.wait_ge(s_accout[i], 16 * n)

        @block.tensor
        def _(pe):
            def mix(t):
                _, at, w, _, _ = tiles[t]
                if t:
                    pe.wait_ge(s_x1, t)
                for n in range(2):
                    for f in range(2 * DC):
                        if t == 0 and n == 0 and f % 4 == 0:
                            pe.wait_ge(s_w[f // 4], 16)
                        half = (zt if f < DC else lru)[:, f % DC, at:at + w]
                        last = nc.tensor.matmul(mem.bank[n][0:w, :], half, w_out[:, f, 512 * n:512 * n + 512],
                                                start=(f == 0), stop=(f == 2 * DC - 1))
                last.then_inc(s_mix, 1)

            mix(0)
            pe.wait_ge(s_sh, 64)
            for t, at, w, _, _ in tiles:
                if t < TILES:
                    mix(t + 1)
                pe.wait_ge(s_h1, t + 1)
                for k in range(DC):
                    last = nc.tensor.transpose(mem.bank[2 + k // 4][:, P * (k % 4):P * (k % 4) + w],
                                               h1[t % 2][0:w, P * k:P * k + P], C("ident")[0:w, 0:w])
                last.then_inc(s_ht, 1)
                pe.wait_ge(s_htr, t + 1)
                if t:
                    pe.wait_ge(s_hdr, t)
                for k in range(DC):
                    last = nc.tensor.matmul(mem.bank[4][0:w, 0:NE], h1_t[:, k, 0:w], w_router[:, k, :],
                                            start=(k == 0), stop=(k == DC - 1))
                last.then_inc(s_ro, 1)
                for k in range(DC):
                    last = nc.tensor.matmul(mem.bank[5][0:w, :], h1_t[:, k, 0:w], w_gu[:, k, :],
                                            start=(k == 0), stop=(k == DC - 1))
                last.then_inc(s_gu, 1)
                pe.wait_ge(s_hid, t + 1)
                pe.wait_ge(s_sc, t + 1)
                for c in range(FC):
                    last = nc.tensor.transpose(mem.bank[4][:, P * c:P * c + w], hidden[0:w, P * c:P * c + P],
                                               C("ident")[0:w, 0:w])
                last.then_inc(s_hdt, 1)
                pe.wait_ge(s_hdr, t + 1)
                if t:
                    pe.wait_ge(s_acc, t)
                for n in range(2):
                    for c in range(FC):
                        last = nc.tensor.matmul(mem.bank[6 + n][0:w, :], hidden_t[:, c, 0:w],
                                                w_dn[:, c, 512 * n:512 * n + 512], start=(c == 0), stop=(c == FC - 1))
                last.then_inc(s_dn, 1)
            pe.wait_ge(s_sel, TILES + 1)
            for t in range(TILES + 1):
                for other in range(t + 1):
                    nc.tensor.matmul(mem.bank[0][:, NE * t:NE * t + NE], C("before" if other == t else "ones"),
                                     route.chosen[:, other, :], start=(other == 0), stop=(other == t))
            for t in range(TILES + 1):
                last = nc.tensor.matmul(mem.bank[1][:, 0:NE], C("ones"), route.chosen[:, t, :],
                                        start=(t == 0), stop=(t == TILES))
            last.then_inc(s_rank, 1)
            pe.wait_ge(s_eb, 1)
            nc.tensor.matmul(mem.bank[2][0:1, 0:P], route.block_col[:, 0:1], C("ident"), start=True, stop=True)\
                .then_inc(s_ebt, 1)

        @block.scalar
        def _(act):
            for t, at, w, _, _ in tiles:
                act.wait_ge(s_ht, t + 1)
                if t:
                    act.wait_ge(s_gu, t)
                for i in range(2):
                    last = nc.scalar.activation(h1_t[:, 4 * i:4 * i + 4, 0:w],
                                                mem.bank[2 + i][:, :].rearrange("p (k i) -> p k i", k=4)[:, :, 0:w],
                                                ACT.Copy)
                last.then_inc(s_htr, 1)
                act.wait_ge(s_ro, t + 1)
                if t:
                    act.wait_ge(s_sel, t)
                nc.scalar.activation(scores[0:w], mem.bank[4][0:w, 0:NE], ACT.Tanh, scale=0.5).then_inc(s_sc, 1)
                act.wait_ge(s_gu, t + 1)
                nc.scalar.activation(act_g[0:w], mem.bank[5][0:w, 0:FF], ACT.Silu).then_inc(s_g, 1)

        @block.vector
        def _(dve):
            steps = Steps(dve, s_v)
            steps.link(nc.vector.memset(route.chosen, 0.0))
            steps.link(nc.vector.memset(route.row, 0.0))

            def choose(t, w):
                sc, bi, ma = scores[0:w], biased[0:w], masked[0:w]
                experts = C("experts")[0:w]
                steps.link(nc.vector.tensor_scalar(sc, sc, 0.5, 0.5, ALU.mult, ALU.add))
                steps.link(nc.vector.tensor_tensor(bi, sc, PR("route_b")[0:w], ALU.add))
                for n in range(NG):
                    last = nc.vector.max(best[0:w, n, :], bi[:, GE * n:GE * n + GE])
                steps.link(last)
                steps.link(nc.vector.tensor_tensor(group[0:w], best[0:w, :, 0], best[0:w, :, 1], ALU.add))
                steps.link(nc.vector.max(group_best[0:w], group[0:w]))
                steps.link(nc.vector.max_index(group_i[0:w], group_best[0:w], group[0:w]))
                steps.link(nc.vector.tensor_copy(group_f[0:w], group_i[0:w]))
                steps.link(nc.vector.tensor_tensor(
                    group_eq[0:w], experts[:, 0:NG].unsqueeze(2).to_broadcast([w, NG, TOPG]),
                    group_f[0:w, 0:TOPG].unsqueeze(1).to_broadcast([w, NG, TOPG]), ALU.is_equal))
                steps.link(nc.vector.tensor_reduce(group_on[0:w], group_eq[0:w], AX.X, ALU.add))
                steps.link(nc.vector.tensor_scalar(penalty[0:w], group_on[0:w], -1.0, BIG, ALU.add, ALU.mult))
                by_group = [v.rearrange("p (g e) -> p g e", g=NG) for v in (bi, ma)]
                steps.link(nc.vector.tensor_tensor(by_group[1], by_group[0],
                                                   group_on[0:w].unsqueeze(2).to_broadcast([w, NG, GE]), ALU.mult))
                steps.link(nc.vector.tensor_tensor(by_group[1], by_group[1],
                                                   penalty[0:w].unsqueeze(2).to_broadcast([w, NG, GE]), ALU.add))
                steps.link(nc.vector.max(top_v[0:w], ma))
                steps.link(nc.vector.max_index(top_i[0:w], top_v[0:w], ma))
                steps.link(nc.vector.tensor_copy(expert[0:w], top_i[0:w]))
                steps.link(nc.vector.tensor_tensor(
                    hot[0:w], experts.unsqueeze(1).to_broadcast([w, TOPK, NE]),
                    expert[0:w].unsqueeze(2).to_broadcast([w, TOPK, NE]), ALU.is_equal))
                steps.link(nc.vector.tensor_tensor(hot_s[0:w], hot[0:w], sc.unsqueeze(1).to_broadcast([w, TOPK, NE]),
                                                   ALU.mult))
                steps.link(nc.vector.tensor_reduce(route.weight[0:w, t, :], hot_s[0:w], AX.X, ALU.add))
                steps.link(nc.vector.tensor_reduce(total[0:w, 0:1], route.weight[0:w, t, :], AX.X, ALU.add))
                steps.link(nc.vector.reciprocal(total[0:w, 1:2], total[0:w, 0:1]))
                steps.link(nc.vector.tensor_scalar(route.weight[0:w, t, :], route.weight[0:w, t, :], total[0:w, 1:2],
                                                   SCALE, ALU.mult, ALU.mult))
                steps.link(nc.vector.tensor_tensor(
                    hot_s[0:w], hot[0:w], experts[:, 0:TOPK].unsqueeze(2).to_broadcast([w, TOPK, NE]), ALU.mult))
                steps.link(nc.vector.tensor_reduce(which[0:w], hot_s[0:w].rearrange("p j e -> p e j"), AX.X, ALU.add))
                nc.vector.tensor_scalar(route.row[0:w, t, :], which[0:w], C("row_base")[0:w, t:t + 1], None, ALU.add)
                nc.vector.tensor_reduce(route.chosen[0:w, t, :], hot[0:w].rearrange("p j e -> p e j"), AX.X, ALU.add)\
                    .then_inc(s_sel, 1)

            def normalise(t):
                _, _, w, _, _ = tiles[t]
                dve.wait_ge(s_x[t % 2], 16 * (t // 2 + 1))
                dve.wait_ge(s_mix, t + 1)
                for n in range(2):
                    last = nc.vector.scalar_tensor_tensor(
                        x1[0:w, 512 * n:512 * n + 512], x[t % 2][0:w, 512 * n:512 * n + 512], ALPHA,
                        mem.bank[n][0:w, :], ALU.mult, ALU.add)
                last.then_inc(s_x1, 1)
                dve.wait_ge(s_x1, t + 1)
                if t >= 2:
                    dve.wait_ge(s_h1out[t % 2], 16 * (t // 2))
                layer_norm(nc, steps, x1[0:w], stats[0:w], ln[0:w, 0, :], ln[0:w, 1, :], h1[t % 2][0:w])\
                    .then_inc(s_h1, 1)

            dve.wait_ge(s_sh, 64)
            normalise(0)
            for t, at, w, _, _ in tiles:
                dve.wait_ge(s_sc, t + 1)
                dve.wait_ge(s_g, t + 1)
                nc.vector.tensor_tensor(hidden[0:w], act_g[0:w], mem.bank[5][0:w, FF:2 * FF], ALU.mult).then_inc(s_hid, 1)
                dve.wait_ge(s_hdt, t + 1)
                if t:
                    dve.wait_ge(s_dn, t)
                nc.vector.tensor_copy(hidden_t[:, :, 0:w], mem.bank[4][:, 0:FC * P]
                                      .rearrange("p (c i) -> p c i", c=FC)[:, :, 0:w]).then_inc(s_hdr, 1)
                if t < TILES:
                    normalise(t + 1)
                dve.wait_ge(s_dn, t + 1)
                dve.wait_ge(s_h1, t + 1)
                if t >= 2:
                    dve.wait_ge(s_accout[t % 2], 16 * (t // 2))
                for n in range(2):
                    last = nc.vector.scalar_tensor_tensor(
                        acc[t % 2][0:w, 512 * n:512 * n + 512], h1[t % 2][0:w, 512 * n:512 * n + 512], ALPHA,
                        mem.bank[6 + n][0:w, :], ALU.mult, ALU.add)
                last.then_inc(s_acc, 1)
                choose(t, w)
            dve.wait_ge(s_rank, 1)
            r = route
            steps.link(nc.vector.tensor_copy(r.count, mem.bank[1][:, 0:NE]))
            steps.link(nc.vector.tensor_tensor(r.over, r.count.unsqueeze(2).to_broadcast([P, NE, TILES + 1]),
                                               C("over").unsqueeze(1).to_broadcast([P, NE, TILES + 1]), ALU.is_gt))
            steps.link(nc.vector.tensor_reduce(r.n, r.over, AX.X, ALU.add))
            steps.link(nc.vector.tensor_tensor_scan(out=r.upto, data0=C("ones")[:, 0:NE], data1=r.n, initial=0.0,
                                                    op0=ALU.mult, op1=ALU.add))
            steps.link(nc.vector.tensor_tensor(r.first, r.upto, r.n, ALU.subtract))
            steps.link(nc.vector.tensor_scalar(r.first, r.first, float(P), None, ALU.mult))
            steps.link(nc.vector.tensor_tensor(r.dest, mem.bank[0][:, 0:(TILES + 1) * NE]
                                               .rearrange("p (t e) -> p t e", e=NE),
                                               r.first.unsqueeze(1).to_broadcast([P, TILES + 1, NE]), ALU.add))
            steps.link(nc.vector.scalar_tensor_tensor(r.dest, r.dest, 1.0, r.chosen, ALU.add, ALU.mult))
            steps.link(nc.vector.tensor_scalar(r.dest, r.dest, -1.0, None, ALU.add))
            steps.link(nc.vector.tensor_scalar(r.n, r.upto, C("row"), None, ALU.is_le))
            steps.link(nc.vector.tensor_reduce(r.block_col[:, 0:1], r.n, AX.X, ALU.add))
            nc.vector.tensor_scalar(r.block_col[:, 0:1], r.block_col[:, 0:1], NE - 1.0, None, ALU.min).then_inc(s_eb, 1)
            nc.vector.tensor_copy(r.n_blocks[0:1, 0:1], r.upto[0:1, NE - 1:NE])
            dve.wait_ge(s_ebt, 1)
            nc.vector.tensor_copy(r.block_expert[0:1, :], mem.bank[2][0:1, 0:P])


W_GU = DC * 2 * FF
W_EXP = W_GU + FC * D


def expert_stage(nc, mem, dram, route):
    with ExitStack() as ctx:
        def sem(name):
            return ctx.enter_context(nc.semaphore(name))

        C = mem.consts
        carve = mem.carve
        weights = [carve(mem.long, W_EXP * i, W_EXP) for i in range(2)]
        w_gu = [w[:, 0:W_GU].rearrange("p (k n) -> p k n", k=DC) for w in weights]
        w_dn = [w[:, W_GU:].rearrange("p (k n) -> p k n", k=FC) for w in weights]
        at = 0

        def take(*dims):
            nonlocal at
            view = carve(mem.work, at, *dims)
            at += int(np.prod(dims))
            return view

        rows = [take(D) for _ in range(2)]
        rows_t = [take(DC, P) for _ in range(2)]
        y = [take(D) for _ in range(2)]
        hot = take(TILES + 1, P)
        act_g, hidden, hidden_t = take(FF), take(FF), take(FC, P)
        row_id = [ctx.enter_context(nc.sbuf_tensor(f"row_id{i}", [P, 1], U32)) for i in range(2)]
        token = [ctx.enter_context(nc.sbuf_tensor(f"token{i}", [P, 1], U32)) for i in range(2)]

        s_w = [[sem(f"expert_{n}_loaded_{i}") for i in range(2)] for n in ("gate_up", "down")]
        s_clear, s_end, s_gate = sem("rows_cleared"), sem("blocks_ended"), sem("row_moves_begun")
        s_hot, s_idp, s_rid, s_id = sem("slot_matches"), sem("ids_summed"), sem("row_ids_ready"), sem("tokens_ready")
        s_rows = [sem("rows_gathered_0"), sem("rows_gathered_1")]
        s_xt, s_xtr = sem("rows_transposed"), sem("rows_t_ready")
        s_gu, s_g, s_hid, s_hdt, s_hdr = sem("up_ready"), sem("gate_ready"), sem("hidden_ready"), sem("hidden_transposed"), sem("hidden_t_ready")
        s_dn, s_y0, s_y1 = sem("down_ready"), sem("y_left_ready"), sem("y_right_ready")
        s_out = [sem("y_stored_0"), sem("y_stored_1")]
        block = ctx.enter_context(nc.Block())

        def used_blocks(engine, body):
            for i in range(2):
                body(i, i, True)
            n = engine.value_load(route.n_blocks[0:1, 0:1], min_val=T * TOPK // P, max_val=2 * NB2)
            with engine.Fori(1, NB2) as pair:
                for i in range(2):
                    with engine.If(pair * 2 + i < n):
                        body(pair * 2 + i, i, False)
                    engine.nop()
            return n

        def expert_of(engine, b):
            return engine.value_load(route.block_expert[0:1, bass.ds(b, 1)], min_val=0, max_val=NE - 1)

        @block.sync
        def _(sp):
            def load(b, i, first):
                e = expert_of(sp, b)
                if not first:
                    sp.wait_ge(s_gu, b - 1)
                sp.dma_start(weights[i][:, 0:W_GU], dram["w_exp"][bass.ds(e, 1), :, 0:W_GU]
                             .rearrange("a p n -> (a p) n")).then_inc(s_w[0][i], 16)
                if not first:
                    sp.wait_ge(s_dn, b - 1)
                sp.dma_start(weights[i][:, W_GU:], dram["w_exp"][bass.ds(e, 1), :, W_GU:]
                             .rearrange("a p n -> (a p) n")).then_inc(s_w[1][i], 16)

            used_blocks(sp, load)

        @block.gpsimd
        def _(pool):
            pool.memset(rows[0], 0.0)
            pool.memset(rows[1], 0.0).then_inc(s_clear, 1)
            pool.wait_ge(s_clear, 1)

            def gather(b, i, first):
                pool.wait_ge(s_id, b + 1)
                if not first:
                    pool.wait_ge(s_xt, b - 1)
                pool.sem_inc(s_gate, 1)
                pool.indirect_dma_start(out=rows[i], out_offset=None, in_=dram["h1"],
                                        in_offset=bass.IndirectOffsetOnAxis(ap=token[i][:, 0:1], axis=0),
                                        bounds_check=T - 1, oob_is_err=False).then_inc(s_rows[i], 16)

            def scatter(b, i):
                pool.wait_ge(s_y0, b + 1)
                pool.wait_ge(s_y1, b + 1)
                pool.sem_inc(s_gate, 1)
                pool.indirect_dma_start(out=dram["expert_rows"],
                                        out_offset=bass.IndirectOffsetOnAxis(ap=row_id[i][:, 0:1], axis=0),
                                        in_=y[i], in_offset=None, bounds_check=T * TOPK - 1, oob_is_err=False)\
                    .then_inc(s_out[i], 16)

            def work(b, i, first):
                gather(b + 1, 1 - i, first and i == 0)
                scatter(b, i)

            gather(0, 0, True)
            n = used_blocks(pool, work)
            even, odd = pool.snap((n >> 1) * 16), pool.snap(((n + 1) >> 1) * 16)
            even_1 = pool.snap((n >> 1) * 16 + 16)
            for done, value in ((s_rows[0], even_1), (s_rows[1], odd), (s_out[0], odd), (s_out[1], even)):
                pool.wait_ge(done, value)
                pool.sem_inc(s_end, 1)

        @block.tensor
        def _(pe):
            def sum_ids(b):
                e = expert_of(pe, b)
                for t in range(TILES + 1):
                    last = nc.tensor.matmul(mem.bank[6][:, 0:1], hot[:, t, :], route.row[:, t, bass.ds(e, 1)],
                                            start=(t == 0), stop=(t == TILES))
                last.then_inc(s_idp, 1)

            def transpose_rows(b, i, first=False):
                pe.wait_ge(s_rows[i], (b - i) * 8 + 16)
                if not first:
                    pe.wait_ge(s_xtr, b)
                for k in range(DC):
                    last = nc.tensor.transpose(mem.bank[k // 4][:, P * (k % 4):P * (k % 4) + P],
                                               rows[i][:, P * k:P * k + P], C("ident"))
                last.then_inc(s_xt, 1)

            def work(b, i, first):
                pe.wait_ge(s_w[0][i], (b - i) * 8 + 16)
                pe.wait_ge(s_xtr, b + 1)
                if not (first and i == 0):
                    pe.wait_ge(s_hid, b)
                for k in range(DC):
                    last = nc.tensor.matmul(mem.bank[2][:, :], rows_t[i][:, k, :], w_gu[i][:, k, :],
                                            start=(k == 0), stop=(k == DC - 1))
                last.then_inc(s_gu, 1)
                pe.wait_ge(s_hot, b + 2)
                pe.wait_ge(s_id, b + 1)
                sum_ids(b + 1)
                pe.wait_ge(s_hid, b + 1)
                if not (first and i == 0):
                    pe.wait_ge(s_hdr, b)
                for c in range(FC):
                    last = nc.tensor.transpose(mem.bank[3][:, P * c:P * c + P], hidden[:, P * c:P * c + P], C("ident"))
                last.then_inc(s_hdt, 1)
                pe.wait_ge(s_w[1][i], (b - i) * 8 + 16)
                pe.wait_ge(s_hdr, b + 1)
                if not (first and i == 0):
                    pe.wait_ge(s_y0, b)
                    pe.wait_ge(s_y1, b)
                for n in range(2):
                    for c in range(FC):
                        last = nc.tensor.matmul(mem.bank[4 + n][:, :], hidden_t[:, c, :], w_dn[i][:, c, 512 * n:512 * n + 512],
                                                start=(c == 0), stop=(c == FC - 1))
                last.then_inc(s_dn, 1)
                transpose_rows(b + 1, 1 - i)

            pe.wait_ge(s_hot, 1)
            sum_ids(0)
            transpose_rows(0, 0, True)
            used_blocks(pe, work)

        @block.scalar
        def _(act):
            def read_rows(b, i, first=False):
                act.wait_ge(s_xt, b + 1)
                if not first:
                    act.wait_ge(s_gu, b - 1)
                for n in range(2):
                    last = nc.scalar.activation(rows_t[i][:, 4 * n:4 * n + 4, :],
                                                mem.bank[n][:, :].rearrange("p (k i) -> p k i", k=4), ACT.Copy)
                last.then_inc(s_xtr, 1)

            def work(b, i, first):
                act.wait_ge(s_gu, b + 1)
                if not (first and i == 0):
                    act.wait_ge(s_hid, b)
                nc.scalar.activation(act_g, mem.bank[2][:, 0:FF], ACT.Silu).then_inc(s_g, 1)
                act.wait_ge(s_dn, b + 1)
                if not first:
                    act.wait_ge(s_out[i], (b - i) * 8)
                nc.scalar.activation(y[i][:, 0:512], mem.bank[4][:, :], ACT.Copy).then_inc(s_y0, 1)
                read_rows(b + 1, 1 - i, first and i == 0)

            read_rows(0, 0, True)
            used_blocks(act, work)

        @block.vector
        def _(dve):
            def match(b, first=False):
                e = expert_of(dve, b)
                if not first:
                    dve.wait_ge(s_idp, b)
                for t in range(TILES + 1):
                    last = nc.vector.tensor_scalar(hot[:, t, :], C("slots"),
                                                   route.dest[:, t, bass.ds(e, 1)], C("block")[:, bass.ds(b, 1)],
                                                   ALU.subtract, ALU.is_equal)
                last.then_inc(s_hot, 1)

            def read_ids(b, i, first=False):
                dve.wait_ge(s_idp, b + 1)
                if not first:
                    dve.wait_ge(s_out[i], (b - i) * 8)
                nc.vector.tensor_scalar(row_id[i][:, :], mem.bank[6][:, 0:1], NO_ROW, None, ALU.add).then_inc(s_rid, 1)
                dve.wait_ge(s_rid, b + 1)
                nc.vector.tensor_scalar(token[i][:, :], row_id[i][:, :], 3, None, ALU.logical_shift_right)\
                    .then_inc(s_id, 1)

            def work(b, i, first):
                match(b + 1)
                dve.wait_ge(s_g, b + 1)
                if not (first and i == 0):
                    dve.wait_ge(s_hdt, b)
                nc.vector.tensor_tensor(hidden, act_g, mem.bank[2][:, FF:2 * FF], ALU.mult).then_inc(s_hid, 1)
                read_ids(b + 1, 1 - i, first and i == 0)
                dve.wait_ge(s_hdt, b + 1)
                if not (first and i == 0):
                    dve.wait_ge(s_dn, b)
                nc.vector.tensor_copy(hidden_t, mem.bank[3][:, 0:FC * P].rearrange("p (c i) -> p c i", c=FC))\
                    .then_inc(s_hdr, 1)
                dve.wait_ge(s_dn, b + 1)
                if not first:
                    dve.wait_ge(s_out[i], (b - i) * 8)
                nc.vector.tensor_copy(y[i][:, 512:D], mem.bank[5][:, :]).then_inc(s_y1, 1)

            match(0, True)
            read_ids(0, 0, True)
            used_blocks(dve, work)


def combine_stage(nc, mem, dram, route):
    with ExitStack() as ctx:
        def sem(name):
            return ctx.enter_context(nc.semaphore(name))

        carve = mem.carve
        got = [carve(mem.work, TOPK * D * i, TOPK, D) for i in range(2)]
        acc = [carve(mem.long, D * i, D) for i in range(2)]
        out = [carve(mem.long, D * (2 + i), D) for i in range(2)]
        ln = carve(mem.long, 4 * D, 2, D)
        stats = carve(mem.long, 6 * D, 32)

        s_ln = sem("norm_loaded")
        s_acc = [sem("residual_loaded_0"), sem("residual_loaded_1")]
        s_got = [sem("expert_rows_loaded_0"), sem("expert_rows_loaded_1")]
        s_used, s_y, s_v = sem("expert_rows_used"), sem("y_ready"), sem("combine_vector_steps")
        s_out = [sem("y_stored_0"), sem("y_stored_1")]
        block = ctx.enter_context(nc.Block())
        tiles = token_tiles()
        by_token = dram["expert_rows"].rearrange("(t j) d -> t j d", j=TOPK)

        @block.sync
        def _(sp):
            def load(t):
                w = tiles[t][2]
                sp.dma_start(acc[t % 2][0:w], dram["residual"][P * t:P * t + w, :]).then_inc(s_acc[t % 2], 16)
                for half in range(2):
                    js = slice(4 * half, 4 * half + 4)
                    sp.dma_start(got[t % 2][0:w, js, :], by_token[P * t:P * t + w, js, :]).then_inc(s_got[t % 2], 16)

            load(0)
            sp.dma_start(ln, dram["norms"][:, 2:4, :]).then_inc(s_ln, 16)
            load(1)
            for t, _, w, _, _ in tiles:
                sp.wait_ge(s_y, t + 1)
                sp.dma_start(dram["y"][P * t:P * t + w, :], out[t % 2][0:w]).then_inc(s_out[t % 2], 16)
                if t + 2 <= TILES:
                    load(t + 2)
            sp.wait_ge(s_out[0], 48)
            sp.wait_ge(s_out[1], 32)

        @block.vector
        def _(dve):
            steps = Steps(dve, s_v)
            dve.wait_ge(s_ln, 16)
            for t, _, w, _, _ in tiles:
                dve.wait_ge(s_acc[t % 2], 16 * (t // 2 + 1))
                dve.wait_ge(s_got[t % 2], 32 * (t // 2 + 1))
                a = acc[t % 2][0:w]
                for j in range(TOPK):
                    steps.link(nc.vector.scalar_tensor_tensor(a, got[t % 2][0:w, j, :], route.weight[0:w, t, j:j + 1], a,
                                                              ALU.mult, ALU.add))
                if t >= 2:
                    dve.wait_ge(s_out[t % 2], 16 * (t // 2))
                layer_norm(nc, steps, a, stats[0:w], ln[0:w, 0, :], ln[0:w, 1, :], out[t % 2][0:w]).then_inc(s_y, 1)


def build(nc, dram):
    with ExitStack() as ctx:
        dram = dict(dram, h1=nc.dram_tensor("h1_rows", (T, D), F32, kind="Internal").ap(),
                    residual=nc.dram_tensor("residual_rows", (T, D), F32, kind="Internal").ap(),
                    expert_rows=nc.dram_tensor("expert_rows", (T * TOPK, D), F32, kind="Internal").ap())
        mem = Memory(nc, ctx)
        route = Routing(mem)
        projection_stage(nc, mem, dram)
        delta_rule_stage(nc, mem, dram)
        mixing_stage(nc, mem, dram, route)
        expert_stage(nc, mem, dram, route)
        combine_stage(nc, mem, dram, route)


def constant_tables():
    c = np.zeros((P, N_CONSTS), np.float32)

    def put(name, value):
        at, n = CONSTS[name]
        c[:, at:at + n] = value

    p, q = np.arange(P)[:, None], np.arange(P)[None, :]
    put("ident", p == q)
    put("tri", p <= q)
    put("before", p < q)
    put("ones", 1.0)
    put("masks", np.concatenate([((p >> l) % 2 == 1) & ((q >> l) == (p >> l) - 1) for l in range(LEVELS)], 1))
    put("future", np.where(q < p, -BIG, 0.0))
    put("slots", q)
    put("experts", np.arange(NE)[None, :])
    t = np.arange(TILES + 1)[None, :]
    put("row_base", TOPK * (p + P * t) - NO_ROW)
    put("valid", (p + P * t) < T)
    put("row", p)
    put("block", -float(P) * np.arange(2 * NB2 + 1)[None, :])
    put("over", P * t)
    return c


def kernel(**inputs):
    from concourse import bacc
    from concourse.bass_utils import run_bass_kernel_spmd

    x = {k: np.asarray(v) for k, v in inputs.items()}

    def feature_major(a, n):
        return a.reshape(-1, n, P).transpose(2, 1, 0)

    def rows(a):
        return np.broadcast_to(a.reshape(1, -1), (P, a.size))

    both = np.concatenate([x["x_prompt"][0], x["x_sample"][0]])
    x_t = np.zeros((P, DC, TW), np.float32)
    x_t[:, :, :SEQ] = feature_major(both[:SEQ], DC)
    x_t[:, :, S0:S0 + DEC] = feature_major(both[SEQ:], DC)
    w = x["w_in"][0]
    v_end, z_end = QKV, QKV + D
    lx, ly = z_end + 2 * H, z_end + 2 * H + D
    order = np.concatenate([w[:, lx:lx + D], w[:, ly:ly + D], w[:, :v_end], w[:, v_end:z_end]], 1)
    w_in = order.reshape(DC, P, 12, 4 * P).transpose(2, 1, 0, 3)
    w_ba = w[:, z_end:lx].reshape(DC, P, 2 * H).transpose(1, 0, 2)
    conv_w = np.concatenate([x["lru_conv_w"][0], x["gdn_conv_w"][0]], 1)
    conv_b = np.concatenate([x["lru_conv_b"][0], np.zeros(QKV, np.float32)])
    hist = np.concatenate([x["state_lru_conv"][0, 0], x["state_gdn_conv"][0, 0]], 1)
    params = np.concatenate([
        feature_major(conv_w, 32).reshape(P, -1), feature_major(conv_b, 32).reshape(P, -1),
        feature_major(hist, 32).reshape(P, -1), feature_major(x["state_lru"][0, 0], DC).reshape(P, -1),
        feature_major(x["lru_lambda"][0], DC).reshape(P, -1),
        feature_major(x["lru_ba"][0], DC).reshape(P, -1), feature_major(x["lru_bx"][0], DC).reshape(P, -1),
        rows(x["gdn_dt_bias"][0]), rows(x["gdn_a_log"][0]), x["gdn_norm_w"][0].reshape(P, 1),
        rows(x["router_bias"][0]),
    ], 1)
    gates = np.concatenate([x["lru_wa"][0], x["lru_wx"][0]]).transpose(1, 0, 2)
    w_gu = np.stack([x["exp_w_gate"][0], x["exp_w_up"][0]], 2).reshape(NE, DC, P, 2 * FF).transpose(0, 2, 1, 3)
    w_dn = x["exp_w_down"][0].reshape(NE, FC, P, D).transpose(0, 2, 1, 3)
    w_exp = np.concatenate([w_gu.reshape(NE, P, -1), w_dn.reshape(NE, P, -1)], 2)
    s_gu = np.stack([x["sh_w_gate"][0], x["sh_w_up"][0]], 1).reshape(DC, P, 2 * FF).transpose(1, 0, 2)
    s_dn = x["sh_w_down"][0].reshape(FC, P, D).transpose(1, 0, 2)
    w_sh = np.concatenate([s_gu.reshape(P, -1), s_dn.reshape(P, -1)], 1)
    ins = {
        "consts": constant_tables(), "params": params, "x_t": x_t, "x_rows": both, "w_in": w_in, "w_ba": w_ba,
        "gates": gates, "state": x["state_gdn"][0, 0].transpose(1, 0, 2),
        "w_out": x["w_out"][0].reshape(2 * DC, P, D).transpose(1, 0, 2),
        "norms": np.stack([rows(x[n][0]) for n in ("ln1_g", "ln1_b", "ln2_g", "ln2_b")], 1),
        "w_router": x["router_w"][0].reshape(DC, P, NE).transpose(1, 0, 2), "w_sh": w_sh, "w_exp": w_exp,
    }
    ins = {k: np.ascontiguousarray(v) for k, v in ins.items()}
    outs = {
        "y": (T, D), "tails": (P, 32, 2 * GAP), "states": (2, P, H, P), "lru_last": (P, DC, 2),
    }
    nc = bacc.Bacc("TRN2", target_bir_lowering=False, num_devices=1)
    dram = {}
    for name, a in ins.items():
        dram[name] = nc.dram_tensor(f"in_{name}", a.shape, mybir.dt.from_np(a.dtype), kind="ExternalInput").ap()
    for name, shape in outs.items():
        dram[name] = nc.dram_tensor(f"out_{name}", shape, F32, kind="ExternalOutput").ap()
    build(nc, dram)
    got = run_bass_kernel_spmd(nc, [{f"in_{k}": v for k, v in ins.items()}], core_ids=[0]).results[0]
    y, tails, states, last = (got[f"out_{n}"] for n in outs)

    def tail(lo, hi, which):
        a = tails[:, lo:hi, GAP * which:GAP * (which + 1)]
        return a.transpose(2, 1, 0).reshape(1, 1, GAP, (hi - lo) * P)

    def result(which):
        return (tail(DC, 32, which), states[which].transpose(1, 0, 2)[None, None], tail(0, DC, which),
                last[:, :, which].T.reshape(1, 1, D))

    return (y[:SEQ][None], y[SEQ:][None], *result(0), *result(1))
```

```python
from contextlib import ExitStack

import numpy as np

import concourse.bass as bass
from concourse import mybir

F32 = mybir.dt.float32
BF16 = mybir.dt.bfloat16
I32 = mybir.dt.int32
U32 = mybir.dt.uint32
F32R = mybir.dt.float32r
ALU = mybir.AluOpType
ACT = mybir.ActivationFunctionType
AX = mybir.AxisListType

P = 128
D = 1024
SEQ = 512
DEC = 32
H = 8
DC = D // P
TILES = SEQ // P
QKV = 3 * D
CONV = 4
NQ = QKV // P
NCH = 6 * D // P
LRU_C = 8.0
GAP = CONV - 1
S0 = SEQ + GAP
TW = S0 + DEC + 1
HALF = TW // 2
RW = TW + GAP
NE = 64
TOPK = 8
NG = 8
TOPG = 4
GE = NE // NG
FF = 256
FC = FF // P
T = SEQ + DEC
NB = (T * TOPK + NE * (P - 1)) // P + 1
NB2 = (NB + 1) // 2
NO_TOKEN = 1024.0
SCALE = 2.5
ALPHA = 2.0 ** 0.25
LN_EPS = 1e-5
RMS_EPS = 1e-6
BIG = 1e30
LEVELS = 7

CONSTS = {}
_at = 0
for _name, _n in (("ident", P), ("tri", P), ("before", P), ("ones", P), ("masks", LEVELS * P), ("future", P),
                  ("slots", P), ("experts", NE), ("token_base", TILES + 1), ("valid", TILES + 1), ("row", 1), ("block", 2 * NB2 + 3),
                  ("over", TILES + 1)):
    CONSTS[_name] = (_at, _n)
    _at += _n
N_CONSTS = _at

PARAMS = {}
_at = 0
for _name, _n in (("conv_w", 4 * 32), ("conv_b", 32), ("hist", 3 * 32), ("h0", DC), ("lam", DC), ("gate_b", 2 * DC),
                  ("dt", H), ("a_log", H), ("norm_w", 1), ("route_b", NE)):
    PARAMS[_name] = (_at, _n)
    _at += _n
N_PARAMS = _at


class Steps:

    def __init__(self, engine, sem, base=0):
        self.engine, self.sem, self.n, self.base = engine, sem, 0, base

    def done(self, instruction):
        instruction.then_inc(self.sem, 1)
        self.n += 1
        return self

    def wait(self):
        self.engine.wait_ge(self.sem, self.n + self.base)

    def link(self, instruction):
        self.done(instruction).wait()


class Views:

    def __init__(self, tile, table):
        self.tile, self.table = tile, table

    def __call__(self, name, *dims):
        at, n = self.table[name]
        view = self.tile[:, at:at + n]
        if dims:
            names = [f"d{i}" for i in range(len(dims))]
            view = view.rearrange(f"p ({' '.join(names)}) -> p {' '.join(names)}", **dict(zip(names, dims)))
        return view


def rsqrt(nc, steps, out, y, scratch, factor=1.0):
    g, h = scratch
    steps.link(nc.vector.tensor_scalar(g.bitcast(I32), y.bitcast(I32), -0.5, 1597463007.0, ALU.mult, ALU.add))
    for step in range(4):
        steps.link(nc.vector.tensor_tensor(h, g, g, ALU.mult))
        steps.link(nc.vector.tensor_tensor(h, h, y, ALU.mult))
        steps.link(nc.vector.tensor_scalar(h, h, -0.5, 1.5, ALU.mult, ALU.add))
        if step < 3:
            steps.link(nc.vector.tensor_tensor(g, g, h, ALU.mult))
        else:
            steps.link(nc.vector.scalar_tensor_tensor(out, g, factor, h, ALU.mult, ALU.mult))


class Memory:

    def __init__(self, nc, ctx):
        self.nc, self.ctx = nc, ctx
        self.consts = Views(self.sbuf(ctx, "consts", N_CONSTS), CONSTS)
        self.params = Views(self.sbuf(ctx, "params", N_PARAMS), PARAMS)
        self.states = self.sbuf(ctx, "states", 2 * H * P)
        self.row = self.sbuf(ctx, "row", (TILES + 1) * NE * 2, F32R)
        self.bank = [ctx.enter_context(nc.psum_tensor(f"bank{i}", [P, 512], F32)) for i in range(8)]

    def sbuf(self, ctx, name, words, dt=F32):
        return ctx.enter_context(self.nc.sbuf_tensor(name, [P, words], dt))

    def mixed_rows(self, ctx):
        self.zt = self.sbuf(ctx, "zt", DC * TW)
        self.lru = self.sbuf(ctx, "lru", DC * TW)

    def delta_inputs(self, ctx):
        self.qkv = self.sbuf(ctx, "qkv", NQ * TW)
        self.decay = self.sbuf(ctx, "decay", 8 * (TILES + 1) * H)

    def carve(self, tile, at, *dims):
        n = int(np.prod(dims))
        view = tile[:, at:at + n]
        if len(dims) > 1:
            names = [f"d{i}" for i in range(len(dims))]
            view = view.rearrange(f"p ({' '.join(names)}) -> p {' '.join(names)}", **dict(zip(names, dims)))
        return view


def projection_stage(nc, mem, dram):
    with ExitStack() as ctx:
        def sem(name):
            return ctx.enter_context(nc.semaphore(name))

        C, PR = mem.consts, mem.params
        carve = mem.carve
        def take(name, *dims, dt=F32):
            return carve(mem.sbuf(ctx, name, int(np.prod(dims)), dt), 0, *dims)

        w_raw = [take(f"w_raw{i}", DC, P) for i in range(2)]
        w_hi = [take(f"w_hi{i}", DC, P, dt=F32R) for i in range(2)]
        w_lo = [take(f"w_lo{i}", DC, P, dt=F32R) for i in range(2)]
        x_hi, x_lo = take("x_hi", DC, TW, dt=F32R), take("x_lo", DC, TW, dt=F32R)
        t_r = take("rate", DC, TW)
        raw = [take(f"raw{i}", RW) for i in range(4)]
        conv = [take(f"conv{i}", TW) for i in range(2)]
        qkv = carve(mem.qkv, 0, NQ, TW)
        t_i, xc = qkv[:, 8:16, :], qkv[:, 16:24, :]
        zt = carve(mem.zt, 0, DC, TW)
        x_t, mult = zt, zt
        lru = carve(mem.lru, 0, DC, TW)
        gates = carve(mem.states, 0, 2 * DC, P)
        n_d = (TILES + 1) * H
        beta, g_, gsum, gneg, eg, egl, egd, gtot = (
            carve(mem.decay, n_d * i, TILES + 1, H) for i in range(8))
        small = ctx.enter_context(nc.sbuf_tensor("small", [P, 640], F32))
        w_ba = carve(small, 0, DC, 2 * H)
        ba = carve(small, 128, TILES + 1, 2 * H)
        soft_x, soft_w, soft_z, soft_z2, soft_p = (carve(small, 208 + 48 * i, 48) for i in range(5))
        c_lru = carve(small, 448, DC)
        c_neg = carve(small, 456, DC)
        gate_half = carve(small, 464, 2 * DC)
        nexp_a = carve(small, 480, H)
        last_h = carve(small, 488, DC, 2)
        tails = ctx.enter_context(nc.sbuf_tensor("tails", [P, 32, 2 * GAP], F32))

        s_const, s_wba, s_gates = sem("consts_loaded"), sem("w_ba_loaded"), sem("gates_loaded")
        s_x = [sem("x_left_loaded"), sem("x_right_loaded")]
        s_xhi, s_xlo = sem("x_hi_ready"), sem("x_lo_ready")
        s_win = [sem("w_in_loaded_0"), sem("w_in_loaded_1")]
        s_whi, s_wlo = sem("w_hi_ready"), sem("w_lo_ready")
        s_proj, s_psum = sem("channels_projected"), sem("psum_read")
        s_ba, s_exp = sem("ba_projected"), sem("small_exps_ready")
        s_soft_e, s_softp = sem("softplus_argument"), sem("lru_rate_ready")
        s_g, s_gs, s_gread = sem("log_decay_ready"), sem("decay_summed"), sem("decay_exp_ready")
        s_conv, s_fin = sem("conv_ready"), sem("channels_finished")
        s_gate, s_gateread, s_gated = sem("gates_projected"), sem("gates_read"), sem("inputs_gated")
        s_a, s_sq, s_mult2, s_mult = sem("a_ready"), sem("a_squared"), sem("mult_squared"), sem("mult_ready")
        s_lru, s_lru_out, s_last = sem("channels_scanned"), sem("lru_outputs_ready"), sem("last_rows_ready")
        s_v = sem("vector_steps")
        s_load = sem("load_waits_passed")
        s_out = sem("outputs_stored")
        block = ctx.enter_context(nc.Block())

        @block.sync
        def _(sp):
            def load(m, i, first=False):
                if not first:
                    sp.wait_ge(s_wlo, m - 1)
                    sp.sem_inc(s_load, 1)
                sp.dma_start(w_raw[i], dram["w_in"][bass.ds(m, 1)].rearrange("a p k n -> (a p) k n"))\
                    .then_inc(s_win[i], 16)

            load(0, 0, True)
            for half in range(2):
                ks = slice(4 * half, 4 * half + 4)
                sp.dma_start(x_t[:, ks, :], dram["x_t"][:, ks, :]).then_inc(s_x[half], 16)
            load(1, 1, True)
            sp.dma_start(w_ba, dram["w_ba"]).then_inc(s_wba, 16)
            sp.dma_start(mem.consts.tile[:, :], dram["consts"]).then_inc(s_const, 16)
            sp.dma_start(mem.params.tile[:, :], dram["params"]).then_inc(s_const, 16)
            load(2, 0)
            load(3, 1)
            sp.dma_start(gates, dram["gates"]).then_inc(s_gates, 16)
            with sp.Fori(2, NCH // 2) as pair:
                for i in range(2):
                    load(pair * 2 + i, i)
            sp.wait_ge(s_last, 1)
            sp.dma_start(dram["lru_last"], last_h).then_inc(s_out, 16)
            sp.wait_ge(s_conv, 32)
            sp.dma_start(dram["tails"], tails[:, :, :]).then_inc(s_out, 16)
            sp.wait_ge(s_out, 32)

        @block.gpsimd
        def _(pool):
            def split(m, i):
                pool.wait_ge(s_whi, m + 1)
                pool.tensor_tensor(w_lo[i], w_raw[i], w_hi[i], ALU.subtract).then_inc(s_wlo, 1)

            with pool.Fori(0, 11) as pair:
                for i in range(2):
                    split(pair * 2 + i, i)
            for j in range(8):
                pool.wait_ge(s_lru, j + 1)
                pool.tensor_tensor(lru[:, j, :], lru[:, j, :], mult[:, j, :], ALU.mult).then_inc(s_lru_out, 1)
                if j % 2:
                    split(22 + j // 2, (j // 2) % 2)
            with pool.Fori(13, NCH // 2) as pair:
                for i in range(2):
                    split(pair * 2 + i, i)

        def project(pe, n, j, first=False):
            pe.wait_ge(s_wlo, n + 1)
            if not first:
                pe.wait_ge(s_psum, n - 1)
            wh, wl = w_hi[j % 2], w_lo[j % 2]
            for half in range(2):
                out = mem.bank[2 * (j % 2) + half][:, 0:HALF]
                at = slice(half * HALF, (half + 1) * HALF)
                for k in range(DC):
                    if isinstance(n, int) and n == 0 and half == 0:
                        pe.wait_ge(s_xlo, k + 1)
                    nc.tensor.matmul(out, wh[:, k, :], x_hi[:, k, at], start=(k == 0), stop=False)
                    nc.tensor.matmul(out, wh[:, k, :], x_lo[:, k, at], start=False, stop=False)
                    last = nc.tensor.matmul(out, wl[:, k, :], x_hi[:, k, at], start=False, stop=(k == DC - 1))
            last.then_inc(s_proj, 1)

        @block.tensor
        def _(pe):
            for n in range(16):
                project(pe, n, n % 8, n < 2)
                if n == 0:
                    pe.wait_ge(s_wba, 16)
                    for t in range(TILES + 1):
                        at, w = (t * P, P) if t < TILES else (S0, DEC)
                        for k in range(DC):
                            last = nc.tensor.matmul(mem.bank[4][0:w, 16 * t:16 * t + 16], x_t[:, k, at:at + w],
                                                    w_ba[:, k, :], start=(k == 0), stop=(k == DC - 1))
                    last.then_inc(s_ba, 1)
                if n == 3:
                    pe.wait_ge(s_g, 1)
                    nc.tensor.matmul(mem.bank[5][:, 0:n_d], C("tri"), g_.rearrange("p t h -> p (t h)"),
                                     start=True, stop=True)
                    nc.tensor.matmul(mem.bank[6][:, 0:n_d], C("ones"), g_.rearrange("p t h -> p (t h)"),
                                     start=True, stop=True).then_inc(s_gs, 1)
                if n >= 8:
                    b = n - 8
                    if b == 0:
                        pe.wait_ge(s_gates, 16)
                        pe.wait_ge(s_gread, 1)
                    pe.wait_ge(s_conv, b + 1)
                    if b:
                        pe.wait_ge(s_gateread, b)
                    for m in range(2):
                        for half in range(2):
                            last = nc.tensor.matmul(mem.bank[4 + 2 * m + half][:, 0:HALF], gates[:, m * DC + b, :],
                                                    xc[:, b, half * HALF:(half + 1) * HALF], start=True, stop=True)
                    last.then_inc(s_gate, 1)
            with pe.Fori(2, 6) as u:
                for j in range(8):
                    project(pe, u * 8 + j, j)

        def two_halves(j, out, func, **kw):
            nc.scalar.activation(out[0], mem.bank[2 * (j % 2)][:, 0:HALF], func, **kw)
            return nc.scalar.activation(out[1], mem.bank[2 * (j % 2) + 1][:, 0:HALF], func, **kw)

        def halves(x):
            return x[:, 0:HALF], x[:, HALF:TW]

        def evacuate(act, n, j, m, first):
            act.wait_ge(s_proj, n + 1)
            if not first:
                act.wait_ge(s_conv, m - 3)
            two_halves(j, halves(raw[j % 4][:, GAP:RW]), ACT.Copy).then_inc(s_psum, 1)

        @block.scalar
        def _(act):
            def split(m, j):
                act.wait_ge(s_win[j % 2], (m - j % 2) * 8 + 16)
                nc.scalar.activation(w_hi[j % 2], w_raw[j % 2], ACT.Copy).then_inc(s_whi, 1)

            split(0, 0)
            for k in range(DC):
                act.wait_ge(s_x[k // 4], 16)
                nc.scalar.activation(x_hi[:, k, :], x_t[:, k, :], ACT.Copy).then_inc(s_xhi, 1)
            split(1, 1)
            for n in range(8):
                evacuate(act, n, n, n, n < 4)
                split(n + 2, (n + 2) % 8)
                if n == 0:
                    act.wait_ge(s_soft_e, 1)
                    nc.scalar.activation(soft_w, soft_w, ACT.Exp, scale=-1.0)
                    nc.scalar.activation(nexp_a, PR("a_log"), ACT.Exp)
                    nc.scalar.activation(beta, ba[:, :, 0:H], ACT.Tanh, scale=0.5).then_inc(s_exp, 1)
                if n == 3:
                    act.wait_ge(s_gs, 1)
                    flat = [v.rearrange("p t h -> p (t h)") for v in (gsum, gneg, eg, egl, gtot)]
                    nc.scalar.activation(flat[0], mem.bank[5][:, 0:n_d], ACT.Copy)
                    nc.scalar.activation(flat[1], mem.bank[5][:, 0:n_d], ACT.Copy, scale=-1.0)
                    nc.scalar.activation(flat[2], mem.bank[5][:, 0:n_d], ACT.Exp)
                    nc.scalar.activation(flat[4], mem.bank[6][:, 0:n_d], ACT.Copy)
                    nc.scalar.activation(flat[3], mem.bank[6][:, 0:n_d], ACT.Exp).then_inc(s_gread, 1)
            act.wait_ge(s_softp, 1)
            for j in range(8):
                act.wait_ge(s_proj, 8 + j + 1)
                two_halves(j, halves(lru[:, j, :]), ACT.Gelu_apprx_tanh).then_inc(s_psum, 1)
                split(10 + j, (10 + j) % 8)
                act.wait_ge(s_gate, j + 1)
                for m, out in enumerate((t_r, t_i)):
                    for half, part in enumerate(halves(out[:, j, :])):
                        last = nc.scalar.activation(part, mem.bank[4 + 2 * m + half][:, 0:HALF], ACT.Tanh,
                                                    bias=gate_half[:, m * DC + j:m * DC + j + 1], scale=0.5)
                last.then_inc(s_gateread, 1)
                act.wait_ge(s_gateread, j + 1)
                nc.scalar.activation(mult[:, j, :], t_r[:, j, :], ACT.Tanh, bias=c_neg[:, j:j + 1],
                                     scale=c_neg[:, j:j + 1])

            def silu(u, j):
                act.wait_ge(s_conv, u * 8 + (j - 8 + 1))
                nc.scalar.activation(qkv[:, bass.ds(u * 8 + (j - 16), 1), :].rearrange("p a t -> p (a t)"),
                                     conv[j % 2], ACT.Silu).then_inc(s_fin, 1)

            def convolved_tile(u, j):
                evacuate(act, u * 8 + j, j, u * 8 + (j - 8), False)
                split(u * 8 + (j + 2), (j + 2) % 8)
                if j:
                    silu(u, j - 1)

            for j in range(8):
                last = nc.scalar.activation(t_r[:, j, :], t_r[:, j, :], ACT.Exp, bias=c_lru[:, j:j + 1],
                                            scale=c_lru[:, j:j + 1])
            last.then_inc(s_a, 1)
            for j in range(8):
                convolved_tile(2, j)
                if j == 0:
                    act.wait_ge(s_a, 1)
                    act.wait_ge(s_gated, 8)
                    nc.scalar.activation(xc, t_r, ACT.Square).then_inc(s_sq, 1)
                if j == 3:
                    act.wait_ge(s_mult2, 1)
                    nc.scalar.activation(mult, mult, ACT.Sqrt).then_inc(s_mult, 1)
            silu(2, 7)
            act.wait_ge(s_lru, 8)
            with act.Fori(3, 5) as u:
                for j in range(8):
                    convolved_tile(u, j)
                silu(u, 7)
            act.wait_ge(s_lru_out, 8)
            act.wait_ge(s_last, 1)
            for j in range(8):
                act.wait_ge(s_proj, 40 + j + 1)
                two_halves(j, halves(zt[:, j, :]), ACT.Silu).then_inc(s_psum, 1)
                if j < 6:
                    split(42 + j, (42 + j) % 8)

        def convolve(dve, steps, n, m, j, out):
            r = raw[j % 4]
            one = (lambda name, k: PR(name)[:, bass.ds(m * k[0] + k[1], k[2])])
            dve.wait_ge(s_psum, n + 1)
            steps.link(nc.vector.tensor_scalar(r[:, S0:S0 + GAP], one("hist", (3, 0, 3)), 1.0, None, ALU.mult))
            for which, at in enumerate((SEQ, S0 + DEC)):
                nc.vector.tensor_scalar(tails[:, bass.ds(m, 1), GAP * which:GAP * (which + 1)]
                                        .rearrange("p a t -> p (a t)"), r[:, at:at + GAP], 1.0, None, ALU.mult)
            acc = conv[j % 2]
            steps.link(nc.vector.tensor_scalar(acc, r[:, 0:TW], one("conv_w", (4, 0, 1)), one("conv_b", (1, 0, 1)),
                                               ALU.mult, ALU.add))
            for k in range(1, CONV):
                last = nc.vector.scalar_tensor_tensor(out if k == CONV - 1 else acc, r[:, k:k + TW],
                                                      one("conv_w", (4, k, 1)), acc, ALU.mult, ALU.add)
                if k < CONV - 1:
                    steps.link(last)
            return last

        LINKS = 4

        @block.vector
        def _(dve):
            steps = Steps(dve, s_v)
            for r in raw:
                nc.vector.memset(r[:, 0:GAP], 0.0)
            steps.link(nc.vector.memset(ba, 0.0))
            for k in range(DC):
                dve.wait_ge(s_xhi, k + 1)
                nc.vector.tensor_tensor(x_lo[:, k, :], x_t[:, k, :], x_hi[:, k, :], ALU.subtract).then_inc(s_xlo, 1)
            dve.wait_ge(s_const, 32)
            dve.wait_ge(s_ba, 1)
            nc.vector.tensor_copy(ba[:, 0:TILES, :], mem.bank[4][:, 0:16 * TILES].rearrange("p (t c) -> p t c", c=16))
            steps.link(nc.vector.tensor_copy(ba[0:DEC, TILES, :], mem.bank[4][0:DEC, 16 * TILES:16 * TILES + 16]))
            nc.vector.tensor_scalar(soft_x[:, 0:DC], PR("lam"), -1.0, None, ALU.mult)
            steps.link(nc.vector.tensor_tensor(
                soft_x[:, DC:].rearrange("p (t h) -> p t h", h=H), ba[:, :, H:2 * H],
                PR("dt").unsqueeze(1).to_broadcast([P, TILES + 1, H]), ALU.add))
            steps.link(nc.vector.tensor_scalar(soft_w, soft_x, -1.0, None, ALU.mult))
            nc.vector.tensor_tensor(soft_w, soft_w, soft_x, ALU.max).then_inc(s_soft_e, 1)
            dve.wait_ge(s_exp, 1)
            steps.link(nc.vector.tensor_scalar(soft_z, soft_w, 2.0, None, ALU.add))
            steps.link(nc.vector.reciprocal(soft_z, soft_z))
            steps.link(nc.vector.tensor_tensor(soft_z, soft_z, soft_w, ALU.mult))
            steps.link(nc.vector.tensor_tensor(soft_z2, soft_z, soft_z, ALU.mult))
            steps.link(nc.vector.tensor_scalar(soft_p, soft_z2, 1.0 / 15, None, ALU.mult))
            for odd in (13, 11, 9, 7, 5, 3):
                steps.link(nc.vector.scalar_tensor_tensor(soft_p, soft_p, 1.0 / odd, soft_z2, ALU.add, ALU.mult))
            steps.link(nc.vector.scalar_tensor_tensor(soft_p, soft_p, 1.0, soft_z, ALU.add, ALU.mult))
            steps.link(nc.vector.tensor_scalar(soft_x, soft_x, 0.0, None, ALU.max))
            steps.link(nc.vector.scalar_tensor_tensor(soft_x, soft_p, 2.0, soft_x, ALU.mult, ALU.add))
            nc.vector.tensor_scalar(c_lru, soft_x[:, 0:DC], -0.5 * LRU_C, None, ALU.mult)
            nc.vector.tensor_scalar(c_neg, soft_x[:, 0:DC], 0.5 * LRU_C, None, ALU.mult)
            nc.vector.tensor_scalar(gate_half, PR("gate_b"), 0.5, None, ALU.mult).then_inc(s_softp, 1)
            valid = C("valid").unsqueeze(2).to_broadcast([P, TILES + 1, H])
            steps.link(nc.vector.tensor_scalar(nexp_a, nexp_a, -1.0, None, ALU.mult))
            steps.link(nc.vector.tensor_tensor(g_, soft_x[:, DC:].rearrange("p (t h) -> p t h", h=H),
                                               nexp_a.unsqueeze(1).to_broadcast([P, TILES + 1, H]), ALU.mult))
            nc.vector.tensor_tensor(g_, g_, valid, ALU.mult).then_inc(s_g, 1)
            steps.link(nc.vector.tensor_scalar(beta, beta, 0.5, 0.5, ALU.mult, ALU.add))
            steps.link(nc.vector.tensor_tensor(beta, beta, valid, ALU.mult))
            for j in range(8):
                convolve(dve, steps, j, j, j, xc[:, j, :]).then_inc(s_conv, 1)
            for j in range(8):
                dve.wait_ge(s_gateread, j + 1)
                nc.vector.scalar_tensor_tensor(t_i[:, j, :], t_i[:, j, :], 1.0, xc[:, j, :], ALU.add, ALU.mult)\
                    .then_inc(s_gated, 1)

            def convolved_tile(steps, u, j):
                if j >= 2 or not isinstance(u, int):
                    dve.wait_ge(s_fin, u * 8 + ((j - 1 if j >= 2 else 0) - 16))
                convolve(dve, steps, u * 8 + j, u * 8 + (j - 8), j, conv[j % 2]).then_inc(s_conv, 1)

            for j in range(8):
                convolved_tile(steps, 2, j)
                if j == 1:
                    dve.wait_ge(s_sq, 1)
                    nc.vector.scalar_tensor_tensor(mult, xc, 1.0, mult, ALU.add, ALU.mult).then_inc(s_mult2, 1)
                if j == 3:
                    dve.wait_ge(s_mult, 1)
                    steps.link(nc.vector.memset(mult[:, :, 0:1], 1.0))
                if j >= 4:
                    for c in (2 * j - 8, 2 * j - 7):
                        steps.link(nc.vector.scalar_tensor_tensor(t_i[:, c, :], t_i[:, c, :], 0.5, mult[:, c, :],
                                                                  ALU.mult, ALU.mult))
                        nc.vector.tensor_tensor_scan(out=mult[:, c, 0:S0], data0=t_r[:, c, 0:S0],
                                                     data1=t_i[:, c, 0:S0], initial=0.0, op0=ALU.mult, op1=ALU.add)
                        nc.vector.tensor_tensor_scan(out=mult[:, c, S0:TW], data0=t_r[:, c, S0:TW],
                                                     data1=t_i[:, c, S0:TW], initial=PR("h0")[:, c:c + 1],
                                                     op0=ALU.mult, op1=ALU.add).then_inc(s_lru, 1)
            dve.wait_ge(s_lru, 8)
            nc.vector.tensor_copy(last_h[:, :, 0:1], mult[:, :, SEQ - 1:SEQ])
            nc.vector.tensor_copy(last_h[:, :, 1:2], mult[:, :, S0 + DEC - 1:S0 + DEC]).then_inc(s_last, 1)
            base = steps.n
            with dve.Fori(3, 5) as u:
                inner = Steps(dve, s_v, u * (8 * LINKS) + (base - 24 * LINKS))
                for j in range(8):
                    convolved_tile(inner, u, j)
                assert inner.n == 8 * LINKS


def token_tiles():
    return [(t, t * P, P, LEVELS, 0) for t in range(TILES)] + [(TILES, S0, DEC, 5, 1)]


def delta_rule_stage(nc, mem, dram):
    with ExitStack() as ctx:
        def sem(name):
            return ctx.enter_context(nc.semaphore(name))

        C, PR = mem.consts, mem.params
        carve = mem.carve
        work = mem.sbuf(ctx, "delta_work", 16 * H * P)
        qkv = carve(mem.qkv, 0, NQ, TW)
        zt = carve(mem.zt, 0, DC, TW)
        state = [carve(mem.states, H * P * i, H, P) for i in range(2)]
        n_d = (TILES + 1) * H
        beta, g_, gsum, gneg, eg, egl, egd, gtot = (carve(mem.decay, n_d * i, TILES + 1, H) for i in range(8))
        squares = carve(work, 0, 2 * H, P)
        (rg, decay, lower_t, attn_t, x_inv, x_inv_t, joined, v_beta, k_dec, rhs, new, o_state, o, o_sq) = (
            carve(work, 2 * H * P + H * P * i, H, P) for i in range(14))
        small = ctx.enter_context(nc.sbuf_tensor("factors", [P, 160], F32))
        norm, norm_a, norm_b, norm_c = (carve(small, 16 * i, 2 * H) for i in range(4))
        row_f, ks_f, kd_f, qs_f, o_sum, o_a, o_b, o_rs = (carve(small, 64 + 8 * i, H) for i in range(8))
        ident_b = ctx.enter_context(nc.sbuf_tensor("ident_bf16", [P, P], BF16))
        future_b = ctx.enter_context(nc.sbuf_tensor("future_bf16", [P, 4 * P], BF16))

        s_state, s_setup, s_egd = sem("state_loaded"), sem("masks_ready"), sem("decay_to_end_ready")
        s_sq, s_ss = sem("squares_ready"), sem("square_sums_ready")
        s_vt, s_kt = sem("v_transposed"), sem("k_transposed")
        s_vb, s_kd = sem("v_beta_ready"), sem("k_decayed_ready")
        s_norm, s_rg, s_grow, s_et = sem("factors_ready"), sem("decay_rows_ready"), sem("decay_sums_ready"), sem("decay_ready")
        s_kk, s_kq, s_u, s_at = sem("kk_ready"), sem("kq_ready"), sem("lower_ready"), sem("attention_ready")
        s_pa, s_p, s_px, s_x = sem("join_product"), sem("join_ready"), sem("join_applied"), sem("inverse_ready")
        s_ks, s_r, s_vn, s_vns = sem("k_state_ready"), sem("rhs_ready"), sem("new_values"), sem("new_values_read")
        s_os, s_osr, s_oa, s_o = sem("q_state_ready"), sem("q_state_read"), sem("attended"), sem("o_ready")
        s_su, s_s = sem("state_update"), sem("state_ready")
        s_on, s_ot, s_otr = sem("o_normed"), sem("o_transposed"), sem("o_gated")
        s_v = sem("delta_vector_steps")
        s_out = sem("states_stored")
        block = ctx.enter_context(nc.Block())
        groups = [(g, slice(4 * g, 4 * g + 4)) for g in range(2)]

        def in_bank(b, rows, width):
            return mem.bank[b][0:rows, :].rearrange("p (h i) -> p h i", h=4)[:, :, 0:width]

        def inverse_steps(t, level, g):
            return 2 * LEVELS * t + 2 * level + g + 1

        @block.sync
        def _(sp):
            sp.dma_start(state[1], dram["state"]).then_inc(s_state, 16)
            sp.wait_ge(s_s, 2 * TILES)
            sp.dma_start(dram["states"][0], state[0]).then_inc(s_out, 16)
            sp.wait_ge(s_s, 2 * TILES + 2)
            sp.dma_start(dram["states"][1], state[1]).then_inc(s_out, 16)
            sp.wait_ge(s_out, 32)

        @block.tensor
        def _(pe):
            pe.wait_ge(s_setup, 1)
            for t, at, w, levels, stream in token_tiles():
                q, k, v = (qkv[:, 8 * i:8 * i + 8, at:at + w] for i in range(3))
                pe.wait_ge(s_sq, t + 1)
                if t:
                    pe.wait_ge(s_osr, 2 * t)
                for j in range(2 * H):
                    last = nc.tensor.matmul(mem.bank[6][0:w, j:j + 1], squares[:, j, 0:w], C("ones")[:, 0:1],
                                            start=True, stop=True)
                last.then_inc(s_ss, 1)
                for g, hs in groups:
                    if t:
                        pe.wait_ge(s_s, 2 * t)
                    for h in range(4):
                        last = nc.tensor.transpose(in_bank(g, w, P)[:, h, :], v[:, 4 * g + h, :], C("ident"))
                    last.then_inc(s_vt, 1)
                for g, hs in groups:
                    if t:
                        pe.wait_ge(s_o, 2 * t)
                    for h in range(4):
                        last = nc.tensor.transpose(in_bank(2 + g, w, P)[:, h, :], k[:, 4 * g + h, :], C("ident"))
                    last.then_inc(s_kt, 1)
                for g, hs in groups:
                    if t:
                        pe.wait_ge(s_otr, 2 * t)
                    pe.wait_ge(s_rg, 2 * t + g + 1)
                    nc.tensor.matmul(in_bank(4 + g, w, w), C("ones")[0:w, 0:w], rg[0:w, hs, 0:w], start=True, stop=False)
                    nc.tensor.matmul(in_bank(4 + g, w, w), ident_b[0:w, 0:w],
                                     future_b[0:w, :].rearrange("p (h i) -> p h i", h=4)[:, :, 0:w],
                                     start=False, stop=True).then_inc(s_grow, 1)
                for g, hs in groups:
                    pe.wait_ge(s_vb, 2 * t + g + 1)
                    for h in range(4):
                        last = nc.tensor.matmul(in_bank(g, w, w)[:, h, :], k[:, 4 * g + h, :], k[:, 4 * g + h, :],
                                                start=True, stop=True)
                    last.then_inc(s_kk, 1)
                for g, hs in groups:
                    pe.wait_ge(s_kd, 2 * t + g + 1)
                    for h in range(4):
                        last = nc.tensor.matmul(in_bank(2 + g, w, w)[:, h, :], k[:, 4 * g + h, :], q[:, 4 * g + h, :],
                                                start=True, stop=True)
                    last.then_inc(s_kq, 1)
                for g, hs in groups:
                    pe.wait_ge(s_norm, t + 1)
                    if stream:
                        pe.wait_ge(s_state, 16)
                    elif t:
                        pe.wait_ge(s_s, 2 * t)
                    for h in range(4):
                        last = nc.tensor.matmul(in_bank(6 + g, w, P)[:, h, :], k[:, 4 * g + h, :],
                                                state[stream][:, 4 * g + h, :], start=True, stop=True)
                    last.then_inc(s_ks, 1)
                for level in range(levels):
                    for g, hs in groups:
                        if level:
                            pe.wait_ge(s_x, inverse_steps(t, level - 1, g))
                        else:
                            pe.wait_ge(s_u, 2 * t + g + 1)
                            pe.wait_ge(s_et, 2 * t + g + 1)
                        for h in range(4):
                            last = nc.tensor.matmul(in_bank(4 + g, w, w)[:, h, :], lower_t[0:w, 4 * g + h, 0:w],
                                                    x_inv[0:w, 4 * g + h, 0:w] if level else C("ident")[0:w, 0:w],
                                                    start=True, stop=True)
                        last.then_inc(s_pa, 1)
                    for g, hs in groups:
                        pe.wait_ge(s_p, inverse_steps(t, level, g))
                        if not level:
                            pe.wait_ge(s_at, 2 * t + g + 1)
                        for h in range(4):
                            if 0 < level < levels - 1:
                                nc.tensor.matmul(in_bank(g, w, w)[:, h, :], x_inv_t[0:w, 4 * g + h, 0:w],
                                                 joined[0:w, 4 * g + h, 0:w], start=True, stop=True)
                            last = nc.tensor.matmul(in_bank(2 + g, w, w)[:, h, :], joined[0:w, 4 * g + h, 0:w],
                                                    x_inv_t[0:w, 4 * g + h, 0:w] if level else C("ident")[0:w, 0:w],
                                                    start=True, stop=True)
                        last.then_inc(s_px, 1)
                for g, hs in groups:
                    pe.wait_ge(s_r, 2 * t + g + 1)
                    pe.wait_ge(s_x, inverse_steps(t, levels - 1, g))
                    for h in range(4):
                        last = nc.tensor.matmul(in_bank(4 + g, w, P)[:, h, :], x_inv_t[0:w, 4 * g + h, 0:w],
                                                rhs[0:w, 4 * g + h, :], start=True, stop=True)
                    last.then_inc(s_vn, 1)
                for g, hs in groups:
                    for h in range(4):
                        last = nc.tensor.matmul(in_bank(6 + g, w, P)[:, h, :], q[:, 4 * g + h, :],
                                                state[stream][:, 4 * g + h, :], start=True, stop=True)
                    last.then_inc(s_os, 1)
                for g, hs in groups:
                    pe.wait_ge(s_vns, 2 * t + g + 1)
                    for h in range(4):
                        last = nc.tensor.matmul(in_bank(2 + g, w, P)[:, h, :], attn_t[0:w, 4 * g + h, 0:w],
                                                new[0:w, 4 * g + h, :], start=True, stop=True)
                    last.then_inc(s_oa, 1)
                for g, hs in groups:
                    for h in range(4):
                        last = nc.tensor.matmul(in_bank(g, P, P)[:, h, :], k_dec[0:w, 4 * g + h, :],
                                                new[0:w, 4 * g + h, :], start=True, stop=True)
                    last.then_inc(s_su, 1)
                for g, hs in groups:
                    pe.wait_ge(s_on, t + 1)
                    for h in range(4):
                        last = nc.tensor.transpose(in_bank(4 + g, P, w)[:, h, :], o[0:w, 4 * g + h, :],
                                                   C("ident")[0:w, 0:w])
                    last.then_inc(s_ot, 1)

        @block.scalar
        def _(act):
            act.wait_ge(s_setup, 1)
            nc.scalar.activation(egd, egd, ACT.Exp).then_inc(s_egd, 1)
            for t, at, w, levels, stream in token_tiles():
                if t:
                    act.wait_ge(s_ss, t)
                nc.scalar.activation(squares[:, :, 0:w], qkv[:, 0:2 * H, at:at + w], ACT.Square).then_inc(s_sq, 1)
                for g, hs in groups:
                    act.wait_ge(s_vt, 2 * t + g + 1)
                    if t:
                        act.wait_ge(s_r, 2 * t)
                    for h in range(4):
                        last = nc.scalar.activation(v_beta[0:w, 4 * g + h, :], in_bank(g, w, P)[:, h, :], ACT.Copy,
                                                    scale=beta[0:w, t, 4 * g + h:4 * g + h + 1])
                    last.then_inc(s_vb, 1)
                act.wait_ge(s_norm, t + 1)
                for g, hs in groups:
                    act.wait_ge(s_kt, 2 * t + g + 1)
                    if t:
                        act.wait_ge(s_su, 2 * t)
                    for h in range(4):
                        last = nc.scalar.activation(k_dec[0:w, 4 * g + h, :], in_bank(2 + g, w, P)[:, h, :], ACT.Copy,
                                                    scale=kd_f[0:w, 4 * g + h:4 * g + h + 1])
                    last.then_inc(s_kd, 1)
                for g, hs in groups:
                    act.wait_ge(s_grow, 2 * t + g + 1)
                    if t:
                        act.wait_ge(s_at, 2 * t)
                    for h in range(4):
                        last = nc.scalar.activation(decay[0:w, 4 * g + h, 0:w], in_bank(4 + g, w, w)[:, h, :], ACT.Exp,
                                                    bias=gneg[0:w, t, 4 * g + h:4 * g + h + 1])
                    last.then_inc(s_et, 1)
                for g, hs in groups:
                    act.wait_ge(s_vn, 2 * t + g + 1)
                    if t:
                        act.wait_ge(s_su, 2 * t)
                    nc.scalar.activation(new[0:w, hs, :], in_bank(4 + g, w, P), ACT.Copy).then_inc(s_vns, 1)
                for g, hs in groups:
                    act.wait_ge(s_os, 2 * t + g + 1)
                    if t:
                        act.wait_ge(s_o, 2 * t)
                    for h in range(4):
                        last = nc.scalar.activation(o_state[0:w, 4 * g + h, :], in_bank(6 + g, w, P)[:, h, :], ACT.Copy,
                                                    scale=qs_f[0:w, 4 * g + h:4 * g + h + 1])
                    last.then_inc(s_osr, 1)

        @block.vector
        def _(dve):
            steps = Steps(dve, s_v)
            nc.vector.memset(state[0], 0.0)
            nc.vector.tensor_copy(ident_b[:, :], C("ident"))
            nc.vector.tensor_copy(future_b[:, :].rearrange("p (h i) -> p h i", h=4),
                                  C("future").unsqueeze(1).to_broadcast([P, 4, P]))
            nc.vector.tensor_tensor(egd, gtot, gsum, ALU.subtract).then_inc(s_setup, 1)
            dve.wait_ge(s_egd, 1)
            for t, at, w, levels, stream in token_tiles():
                for g, hs in groups:
                    if t:
                        dve.wait_ge(s_grow, 2 * t)
                    for h in range(4 * g, 4 * g + 4):
                        last = nc.vector.tensor_scalar(rg[0:w, h, 0:w], C("tri")[0:w, 0:w], g_[0:w, t, h:h + 1], None,
                                                       ALU.mult)
                    last.then_inc(s_rg, 1)
                dve.wait_ge(s_ss, t + 1)
                if t:
                    dve.wait_ge(s_osr, 2 * t)
                steps.link(nc.vector.tensor_scalar(norm_a[0:w], mem.bank[6][0:w, 0:2 * H], 1e-6, None, ALU.add))
                rsqrt(nc, steps, norm[0:w], norm_a[0:w], (norm_b[0:w], norm_c[0:w]))
                rk, rq = norm[0:w, H:2 * H], norm[0:w, 0:H]
                steps.done(nc.vector.tensor_scalar(rq, rq, P ** -0.5, None, ALU.mult))
                steps.done(nc.vector.tensor_tensor(row_f[0:w], rk, beta[0:w, t, :], ALU.mult))
                steps.done(nc.vector.tensor_tensor(kd_f[0:w], rk, egd[0:w, t, :], ALU.mult)).wait()
                steps.link(nc.vector.tensor_tensor(ks_f[0:w], row_f[0:w], eg[0:w, t, :], ALU.mult))
                steps.link(nc.vector.tensor_scalar(ks_f[0:w], ks_f[0:w], -1.0, None, ALU.mult))
                nc.vector.tensor_tensor(qs_f[0:w], rq, eg[0:w, t, :], ALU.mult).then_inc(s_norm, 1)
                for out, done, ready in ((lower_t, s_u, s_kk), (attn_t, s_at, s_kq)):
                    for g, hs in groups:
                        dve.wait_ge(ready, 2 * t + g + 1)
                        dve.wait_ge(s_et, 2 * t + g + 1)
                        for h in range(4):
                            n = 4 * g + h
                            last = nc.vector.scalar_tensor_tensor(
                                out[0:w, n, 0:w], in_bank(g + (2 if out is attn_t else 0), w, w)[:, h, :],
                                norm[0:w, H + n:H + n + 1], decay[0:w, n, 0:w], ALU.mult, ALU.mult)
                        last.then_inc(done, 1)
                for g, hs in groups:
                    dve.wait_ge(s_ks, 2 * t + g + 1)
                    dve.wait_ge(s_vb, 2 * t + g + 1)
                    for h in range(4):
                        n = 4 * g + h
                        last = nc.vector.scalar_tensor_tensor(rhs[0:w, n, :], in_bank(6 + g, w, P)[:, h, :],
                                                              ks_f[0:w, n:n + 1], v_beta[0:w, n, :], ALU.mult, ALU.add)
                    last.then_inc(s_r, 1)
                eye = C("ident")[0:w, 0:w].unsqueeze(1).to_broadcast([w, 4, w])
                for level in range(levels):
                    mask = C("masks")[0:w, P * level:P * level + w]
                    for g, hs in groups:
                        dve.wait_ge(s_pa, inverse_steps(t, level, g))
                        for h in range(4):
                            n = 4 * g + h
                            last = nc.vector.scalar_tensor_tensor(joined[0:w, n, 0:w], in_bank(4 + g, w, w)[:, h, :],
                                                                  row_f[0:w, n:n + 1], mask, ALU.mult, ALU.mult)
                        last.then_inc(s_p, 1)
                    for g, hs in groups:
                        if not level:
                            dve.wait_ge(s_p, inverse_steps(t, level, g))
                            nc.vector.tensor_tensor(x_inv[0:w, hs, 0:w], eye, joined[0:w, hs, 0:w], ALU.subtract)
                        dve.wait_ge(s_px, inverse_steps(t, level, g))
                        if 0 < level < levels - 1:
                            nc.vector.tensor_tensor(x_inv[0:w, hs, 0:w], x_inv[0:w, hs, 0:w], in_bank(g, w, w),
                                                    ALU.subtract)
                        nc.vector.tensor_tensor(x_inv_t[0:w, hs, 0:w], x_inv_t[0:w, hs, 0:w] if level else eye,
                                                in_bank(2 + g, w, w), ALU.subtract).then_inc(s_x, 1)
                if stream:
                    pass
                for g, hs in groups:
                    dve.wait_ge(s_oa, 2 * t + g + 1)
                    dve.wait_ge(s_osr, 2 * t + g + 1)
                    if t:
                        dve.wait_ge(s_ot, 2 * t)
                    for h in range(4):
                        n = 4 * g + h
                        last = nc.vector.scalar_tensor_tensor(o[0:w, n, :], in_bank(2 + g, w, P)[:, h, :],
                                                              norm[0:w, n:n + 1], o_state[0:w, n, :], ALU.mult, ALU.add)
                    last.then_inc(s_o, 1)
                for g, hs in groups:
                    dve.wait_ge(s_su, 2 * t + g + 1)
                    for h in range(4):
                        n = 4 * g + h
                        last = nc.vector.scalar_tensor_tensor(state[stream][:, n, :], state[stream][:, n, :],
                                                              egl[:, t, n:n + 1], in_bank(g, P, P)[:, h, :],
                                                              ALU.mult, ALU.add)
                    last.then_inc(s_s, 1)
                dve.wait_ge(s_o, 2 * t + 2)
                steps.link(nc.vector.tensor_tensor(o_sq[0:w], o[0:w], o[0:w], ALU.mult))
                steps.link(nc.vector.tensor_reduce(o_sum[0:w], o_sq[0:w], AX.X, ALU.add))
                steps.link(nc.vector.tensor_scalar(o_sum[0:w], o_sum[0:w], 1.0 / P, RMS_EPS, ALU.mult, ALU.add))
                rsqrt(nc, steps, o_rs[0:w], o_sum[0:w], (o_a[0:w], o_b[0:w]))
                nc.vector.tensor_tensor(o[0:w], o[0:w], o_rs[0:w].unsqueeze(2).to_broadcast([w, H, P]), ALU.mult)\
                    .then_inc(s_on, 1)
                for g, hs in groups:
                    dve.wait_ge(s_ot, 2 * t + g + 1)
                    nc.vector.scalar_tensor_tensor(zt[:, hs, at:at + w], in_bank(4 + g, P, w), PR("norm_w"),
                                                   zt[:, hs, at:at + w], ALU.mult, ALU.mult).then_inc(s_otr, 1)


class Routing:

    def __init__(self, mem):
        at = 0

        def take(*dims):
            nonlocal at
            view = mem.carve(mem.states, at, *dims)
            at += int(np.prod(dims))
            return view

        self.chosen = take(TILES + 1, NE)
        self.dest = take(TILES + 1, NE)
        self.row = mem.carve(mem.row, 0, TILES + 1, NE, 2)
        self.weight = take(TILES + 1, TOPK)
        self.block_expert = take(P).bitcast(I32)
        self.n_blocks = take(2).bitcast(I32)
        self.count, self.n, self.upto, self.first = (take(NE) for _ in range(4))
        self.over = take(NE, TILES + 1)
        self.block_col = take(2)


def layer_norm(nc, steps, x, stats, gain, bias, out):
    for i in range(2):
        last = nc.vector.bn_stats(stats[:, 6 * i:6 * i + 6], x[:, 512 * i:512 * i + 512])
    steps.link(last)
    steps.link(nc.vector.bn_aggr(stats[:, 12:14], stats[:, 0:12]))
    steps.link(nc.vector.tensor_scalar(stats[:, 14:15], stats[:, 13:14], LN_EPS, None, ALU.add))
    rsqrt(nc, steps, stats[:, 15:16], stats[:, 14:15], (stats[:, 16:17], stats[:, 17:18]))
    steps.link(nc.vector.tensor_scalar(x, x, stats[:, 12:13], stats[:, 15:16], ALU.subtract, ALU.mult))
    steps.link(nc.vector.tensor_tensor(x, x, gain, ALU.mult))
    return nc.vector.tensor_tensor(out, x, bias, ALU.add)


def mixing_stage(nc, mem, dram, route):
    with ExitStack() as ctx:
        def sem(name):
            return ctx.enter_context(nc.semaphore(name))

        C, PR = mem.consts, mem.params
        carve = mem.carve
        zt = carve(mem.zt, 0, DC, TW)
        lru = carve(mem.lru, 0, DC, TW)
        w_out = carve(mem.sbuf(ctx, "w_out", 2 * DC * D), 0, 2 * DC, D)
        work = mem.sbuf(ctx, "mixing_work", 20480)
        at = 0

        def take(*dims):
            nonlocal at
            view = carve(work, at, *dims)
            at += int(np.prod(dims))
            return view

        w_gu, w_dn, w_router, ln = take(DC, 2 * FF), take(FC, D), take(DC, NE), take(2, D)
        x = [take(D) for _ in range(2)]
        x1, h1_t = take(D), take(DC, P)
        h1 = [take(D) for _ in range(2)]
        acc = [take(D) for _ in range(2)]
        act_g, hidden, hidden_t = take(FF), take(FF), take(FC, P)
        stats, scores, biased, masked = take(32), take(NE), take(NE), take(NE)
        best, group, group_best, group_f = take(NG, 8), take(NG), take(NG), take(NG)
        group_i, top_i = take(8).bitcast(U32), take(8).bitcast(U32)
        group_eq, group_on, penalty, top_v, total = take(NG, TOPG), take(NG), take(NG), take(8), take(2)
        expert, which = take(TOPK), take(NE)
        hot, hot_s = take(TOPK, NE), take(TOPK, NE)
        assert at <= 20480

        s_w = [sem(f"w_out_loaded_{i}") for i in range(4)]
        s_sh = sem("shared_loaded")
        s_x = [sem("x_loaded_0"), sem("x_loaded_1")]
        s_mix, s_x1, s_h1, s_ht, s_htr = sem("mixed"), sem("mix_read"), sem("h1_ready"), sem("h1_transposed"), sem("h1_t_ready")
        s_ro, s_sc, s_gu, s_g, s_hid = sem("routed_scores"), sem("scores_read"), sem("shared_up"), sem("shared_gate_ready"), sem("shared_hidden")
        s_hdt, s_hdr, s_dn, s_acc = sem("hidden_transposed"), sem("hidden_t_ready"), sem("shared_down"), sem("residual_ready")
        s_h1out = [sem("h1_stored_0"), sem("h1_stored_1")]
        s_accout = [sem("residual_stored_0"), sem("residual_stored_1")]
        s_sel, s_rank, s_eb, s_ebt, s_v = sem("chosen_ready"), sem("ranks_ready"), sem("block_experts"), sem("block_experts_row"), sem("mix_vector_steps")
        block = ctx.enter_context(nc.Block())
        tiles = token_tiles()
        h1_rows, acc_rows = dram["h1"], dram["residual"]

        @block.sync
        def _(sp):
            for i in range(4):
                sp.dma_start(w_out[:, 4 * i:4 * i + 4, :], dram["w_out"][:, 4 * i:4 * i + 4, :]).then_inc(s_w[i], 16)
            sp.dma_start(x[0], dram["x_rows"][0:P, :]).then_inc(s_x[0], 16)
            sp.dma_start(x[1], dram["x_rows"][P:2 * P, :]).then_inc(s_x[1], 16)
            n_gu = DC * 2 * FF
            sp.dma_start(w_gu, dram["w_sh"][:, 0:n_gu].rearrange("p (k n) -> p k n", k=DC)).then_inc(s_sh, 16)
            sp.dma_start(w_dn, dram["w_sh"][:, n_gu:].rearrange("p (k n) -> p k n", k=FC)).then_inc(s_sh, 16)
            sp.dma_start(w_router, dram["w_router"]).then_inc(s_sh, 16)
            sp.dma_start(ln, dram["norms"][:, 0:2, :]).then_inc(s_sh, 16)
            for t, _, w, _, _ in tiles:
                rows = slice(P * t, P * t + w)
                sp.wait_ge(s_h1, t + 1)
                sp.dma_start(h1_rows[rows, :], h1[t % 2][0:w]).then_inc(s_h1out[t % 2], 16)
                if t + 2 <= TILES:
                    w2 = tiles[t + 2][2]
                    sp.dma_start(x[t % 2][0:w2], dram["x_rows"][P * (t + 2):P * (t + 2) + w2, :]).then_inc(s_x[t % 2], 16)
                sp.wait_ge(s_acc, t + 1)
                sp.dma_start(acc_rows[rows, :], acc[t % 2][0:w]).then_inc(s_accout[t % 2], 16)
            for i, n in ((0, 3), (1, 2)):
                sp.wait_ge(s_h1out[i], 16 * n)
                sp.wait_ge(s_accout[i], 16 * n)

        @block.tensor
        def _(pe):
            def mix(t):
                _, at, w, _, _ = tiles[t]
                if t:
                    pe.wait_ge(s_x1, t)
                for n in range(2):
                    for f in range(2 * DC):
                        if t == 0 and n == 0 and f % 4 == 0:
                            pe.wait_ge(s_w[f // 4], 16)
                        half = (zt if f < DC else lru)[:, f % DC, at:at + w]
                        last = nc.tensor.matmul(mem.bank[n][0:w, :], half, w_out[:, f, 512 * n:512 * n + 512],
                                                start=(f == 0), stop=(f == 2 * DC - 1))
                last.then_inc(s_mix, 1)

            mix(0)
            pe.wait_ge(s_sh, 64)
            for t, at, w, _, _ in tiles:
                if t < TILES:
                    mix(t + 1)
                pe.wait_ge(s_h1, t + 1)
                for k in range(DC):
                    last = nc.tensor.transpose(mem.bank[2 + k // 4][:, P * (k % 4):P * (k % 4) + w],
                                               h1[t % 2][0:w, P * k:P * k + P], C("ident")[0:w, 0:w])
                last.then_inc(s_ht, 1)
                pe.wait_ge(s_htr, t + 1)
                if t:
                    pe.wait_ge(s_hdr, t)
                for k in range(DC):
                    last = nc.tensor.matmul(mem.bank[4][0:w, 0:NE], h1_t[:, k, 0:w], w_router[:, k, :],
                                            start=(k == 0), stop=(k == DC - 1))
                last.then_inc(s_ro, 1)
                for k in range(DC):
                    last = nc.tensor.matmul(mem.bank[5][0:w, :], h1_t[:, k, 0:w], w_gu[:, k, :],
                                            start=(k == 0), stop=(k == DC - 1))
                last.then_inc(s_gu, 1)
                pe.wait_ge(s_hid, t + 1)
                pe.wait_ge(s_sc, t + 1)
                for c in range(FC):
                    last = nc.tensor.transpose(mem.bank[4][:, P * c:P * c + w], hidden[0:w, P * c:P * c + P],
                                               C("ident")[0:w, 0:w])
                last.then_inc(s_hdt, 1)
                pe.wait_ge(s_hdr, t + 1)
                if t:
                    pe.wait_ge(s_acc, t)
                for n in range(2):
                    for c in range(FC):
                        last = nc.tensor.matmul(mem.bank[6 + n][0:w, :], hidden_t[:, c, 0:w],
                                                w_dn[:, c, 512 * n:512 * n + 512], start=(c == 0), stop=(c == FC - 1))
                last.then_inc(s_dn, 1)
            pe.wait_ge(s_sel, TILES + 1)
            for t in range(TILES + 1):
                for other in range(t + 1):
                    nc.tensor.matmul(mem.bank[0][:, NE * t:NE * t + NE], C("before" if other == t else "ones"),
                                     route.chosen[:, other, :], start=(other == 0), stop=(other == t))
            for t in range(TILES + 1):
                last = nc.tensor.matmul(mem.bank[1][:, 0:NE], C("ones"), route.chosen[:, t, :],
                                        start=(t == 0), stop=(t == TILES))
            last.then_inc(s_rank, 1)
            pe.wait_ge(s_eb, 1)
            nc.tensor.matmul(mem.bank[2][0:1, 0:P], route.block_col[:, 0:1], C("ident"), start=True, stop=True)\
                .then_inc(s_ebt, 1)

        @block.scalar
        def _(act):
            for t, at, w, _, _ in tiles:
                act.wait_ge(s_ht, t + 1)
                if t:
                    act.wait_ge(s_gu, t)
                for i in range(2):
                    last = nc.scalar.activation(h1_t[:, 4 * i:4 * i + 4, 0:w],
                                                mem.bank[2 + i][:, :].rearrange("p (k i) -> p k i", k=4)[:, :, 0:w],
                                                ACT.Copy)
                last.then_inc(s_htr, 1)
                act.wait_ge(s_ro, t + 1)
                if t:
                    act.wait_ge(s_sel, t)
                nc.scalar.activation(scores[0:w], mem.bank[4][0:w, 0:NE], ACT.Tanh, scale=0.5).then_inc(s_sc, 1)
                act.wait_ge(s_gu, t + 1)
                nc.scalar.activation(act_g[0:w], mem.bank[5][0:w, 0:FF], ACT.Silu).then_inc(s_g, 1)

        @block.vector
        def _(dve):
            steps = Steps(dve, s_v)
            steps.link(nc.vector.memset(route.chosen, 0.0))
            steps.link(nc.vector.tensor_scalar(route.row.rearrange("p t e c -> p t (e c)"),
                                               C("token_base").unsqueeze(2).to_broadcast([P, TILES + 1, 2 * NE]),
                                               1.0, None, ALU.mult))

            def choose(t, w):
                sc, bi, ma = scores[0:w], biased[0:w], masked[0:w]
                experts = C("experts")[0:w]
                steps.link(nc.vector.tensor_scalar(sc, sc, 0.5, 0.5, ALU.mult, ALU.add))
                steps.link(nc.vector.tensor_tensor(bi, sc, PR("route_b")[0:w], ALU.add))
                for n in range(NG):
                    last = nc.vector.max(best[0:w, n, :], bi[:, GE * n:GE * n + GE])
                steps.link(last)
                steps.link(nc.vector.tensor_tensor(group[0:w], best[0:w, :, 0], best[0:w, :, 1], ALU.add))
                steps.link(nc.vector.max(group_best[0:w], group[0:w]))
                steps.link(nc.vector.max_index(group_i[0:w], group_best[0:w], group[0:w]))
                steps.link(nc.vector.tensor_copy(group_f[0:w], group_i[0:w]))
                steps.link(nc.vector.tensor_tensor(
                    group_eq[0:w], experts[:, 0:NG].unsqueeze(2).to_broadcast([w, NG, TOPG]),
                    group_f[0:w, 0:TOPG].unsqueeze(1).to_broadcast([w, NG, TOPG]), ALU.is_equal))
                steps.link(nc.vector.tensor_reduce(group_on[0:w], group_eq[0:w], AX.X, ALU.add))
                steps.link(nc.vector.tensor_scalar(penalty[0:w], group_on[0:w], -1.0, BIG, ALU.add, ALU.mult))
                by_group = [v.rearrange("p (g e) -> p g e", g=NG) for v in (bi, ma)]
                steps.link(nc.vector.tensor_tensor(by_group[1], by_group[0],
                                                   group_on[0:w].unsqueeze(2).to_broadcast([w, NG, GE]), ALU.mult))
                steps.link(nc.vector.tensor_tensor(by_group[1], by_group[1],
                                                   penalty[0:w].unsqueeze(2).to_broadcast([w, NG, GE]), ALU.add))
                steps.link(nc.vector.max(top_v[0:w], ma))
                steps.link(nc.vector.max_index(top_i[0:w], top_v[0:w], ma))
                steps.link(nc.vector.tensor_copy(expert[0:w], top_i[0:w]))
                steps.link(nc.vector.tensor_tensor(
                    hot[0:w], experts.unsqueeze(1).to_broadcast([w, TOPK, NE]),
                    expert[0:w].unsqueeze(2).to_broadcast([w, TOPK, NE]), ALU.is_equal))
                steps.link(nc.vector.tensor_tensor(hot_s[0:w], hot[0:w], sc.unsqueeze(1).to_broadcast([w, TOPK, NE]),
                                                   ALU.mult))
                steps.link(nc.vector.tensor_reduce(route.weight[0:w, t, :], hot_s[0:w], AX.X, ALU.add))
                steps.link(nc.vector.tensor_reduce(total[0:w, 0:1], route.weight[0:w, t, :], AX.X, ALU.add))
                steps.link(nc.vector.reciprocal(total[0:w, 1:2], total[0:w, 0:1]))
                steps.link(nc.vector.tensor_scalar(route.weight[0:w, t, :], route.weight[0:w, t, :], total[0:w, 1:2],
                                                   SCALE, ALU.mult, ALU.mult))
                steps.link(nc.vector.tensor_tensor(
                    hot_s[0:w], hot[0:w], experts[:, 0:TOPK].unsqueeze(2).to_broadcast([w, TOPK, NE]), ALU.mult))
                steps.link(nc.vector.tensor_reduce(which[0:w], hot_s[0:w].rearrange("p j e -> p e j"), AX.X, ALU.add))
                nc.vector.tensor_copy(route.row[0:w, t, :, 1], which[0:w])
                nc.vector.tensor_reduce(route.chosen[0:w, t, :], hot[0:w].rearrange("p j e -> p e j"), AX.X, ALU.add)\
                    .then_inc(s_sel, 1)

            def normalise(t):
                _, _, w, _, _ = tiles[t]
                dve.wait_ge(s_x[t % 2], 16 * (t // 2 + 1))
                dve.wait_ge(s_mix, t + 1)
                for n in range(2):
                    last = nc.vector.scalar_tensor_tensor(
                        x1[0:w, 512 * n:512 * n + 512], x[t % 2][0:w, 512 * n:512 * n + 512], ALPHA,
                        mem.bank[n][0:w, :], ALU.mult, ALU.add)
                last.then_inc(s_x1, 1)
                dve.wait_ge(s_x1, t + 1)
                if t >= 2:
                    dve.wait_ge(s_h1out[t % 2], 16 * (t // 2))
                layer_norm(nc, steps, x1[0:w], stats[0:w], ln[0:w, 0, :], ln[0:w, 1, :], h1[t % 2][0:w])\
                    .then_inc(s_h1, 1)

            dve.wait_ge(s_sh, 64)
            normalise(0)
            for t, at, w, _, _ in tiles:
                dve.wait_ge(s_sc, t + 1)
                dve.wait_ge(s_g, t + 1)
                nc.vector.tensor_tensor(hidden[0:w], act_g[0:w], mem.bank[5][0:w, FF:2 * FF], ALU.mult).then_inc(s_hid, 1)
                dve.wait_ge(s_hdt, t + 1)
                if t:
                    dve.wait_ge(s_dn, t)
                nc.vector.tensor_copy(hidden_t[:, :, 0:w], mem.bank[4][:, 0:FC * P]
                                      .rearrange("p (c i) -> p c i", c=FC)[:, :, 0:w]).then_inc(s_hdr, 1)
                if t < TILES:
                    normalise(t + 1)
                dve.wait_ge(s_dn, t + 1)
                dve.wait_ge(s_h1, t + 1)
                if t >= 2:
                    dve.wait_ge(s_accout[t % 2], 16 * (t // 2))
                for n in range(2):
                    last = nc.vector.scalar_tensor_tensor(
                        acc[t % 2][0:w, 512 * n:512 * n + 512], h1[t % 2][0:w, 512 * n:512 * n + 512], ALPHA,
                        mem.bank[6 + n][0:w, :], ALU.mult, ALU.add)
                last.then_inc(s_acc, 1)
                choose(t, w)
            dve.wait_ge(s_rank, 1)
            r = route
            steps.link(nc.vector.tensor_copy(r.count, mem.bank[1][:, 0:NE]))
            steps.link(nc.vector.tensor_tensor(r.over, r.count.unsqueeze(2).to_broadcast([P, NE, TILES + 1]),
                                               C("over").unsqueeze(1).to_broadcast([P, NE, TILES + 1]), ALU.is_gt))
            steps.link(nc.vector.tensor_reduce(r.n, r.over, AX.X, ALU.add))
            steps.link(nc.vector.tensor_tensor_scan(out=r.upto, data0=C("ones")[:, 0:NE], data1=r.n, initial=0.0,
                                                    op0=ALU.mult, op1=ALU.add))
            steps.link(nc.vector.tensor_tensor(r.first, r.upto, r.n, ALU.subtract))
            steps.link(nc.vector.tensor_scalar(r.first, r.first, float(P), None, ALU.mult))
            steps.link(nc.vector.tensor_tensor(r.dest, mem.bank[0][:, 0:(TILES + 1) * NE]
                                               .rearrange("p (t e) -> p t e", e=NE),
                                               r.first.unsqueeze(1).to_broadcast([P, TILES + 1, NE]), ALU.add))
            steps.link(nc.vector.scalar_tensor_tensor(r.dest, r.dest, 1.0, r.chosen, ALU.add, ALU.mult))
            steps.link(nc.vector.tensor_scalar(r.dest, r.dest, -1.0, None, ALU.add))
            steps.link(nc.vector.tensor_scalar(r.n, r.upto, C("row"), None, ALU.is_le))
            steps.link(nc.vector.tensor_reduce(r.block_col[:, 0:1], r.n, AX.X, ALU.add))
            nc.vector.tensor_scalar(r.block_col[:, 0:1], r.block_col[:, 0:1], NE - 1.0, None, ALU.min).then_inc(s_eb, 1)
            nc.vector.tensor_copy(r.n_blocks[0:1, 0:1], r.upto[0:1, NE - 1:NE])
            dve.wait_ge(s_ebt, 1)
            nc.vector.tensor_copy(r.block_expert[0:1, :], mem.bank[2][0:1, 0:P])


W_GU = DC * 2 * FF
W_EXP = W_GU + FC * D
UNIT = 1024
UNITS = W_EXP // UNIT
BY_POOL = (1, 3)
BY_VECTOR = tuple(u for u in range(UNITS) if u not in BY_POOL)


def expert_stage(nc, mem, dram, route):
    with ExitStack() as ctx:
        def sem(name):
            return ctx.enter_context(nc.semaphore(name))

        C = mem.consts
        carve = mem.carve

        def take(name, *dims, dt=F32):
            return carve(mem.sbuf(ctx, name, int(np.prod(dims)), dt), 0, *dims)

        weights = [take(f"weights{i}", W_EXP) for i in range(2)]
        w_hi = [take(f"weights_hi{i}", W_EXP, dt=F32R) for i in range(2)]
        w_lo = [take(f"weights_lo{i}", W_EXP, dt=F32R) for i in range(2)]
        rows = [take(f"rows{i}", D) for i in range(2)]
        x_hi = [take(f"rows_hi{i}", DC, P, dt=F32R) for i in range(2)]
        x_lo = [take(f"rows_lo{i}", DC, P, dt=F32R) for i in range(2)]
        y = [take(f"y{i}", D) for i in range(2)]
        hot = take("slot_match", TILES + 1, P, dt=F32R)
        act_g, hidden = take("gate", FF), take("hidden", FF)
        h_hi, h_lo = (take(n, FC, P, dt=F32R) for n in ("hidden_hi", "hidden_lo"))
        token, row_id = ([ctx.enter_context(nc.sbuf_tensor(f"{n}{i}", [P, 1], U32)) for i in range(2)]
                         for n in ("token", "row_id"))
        row_next = [ctx.enter_context(nc.sbuf_tensor(f"row_next{i}", [P, 1], F32)) for i in range(2)]
        pair_j = ctx.enter_context(nc.sbuf_tensor("which_expert", [P, 1], F32))

        s_w = [[sem(f"expert_{n}_loaded_{i}") for i in range(2)] for n in ("gate_up", "down")]
        s_whi, s_wlo, s_wlo_pool = sem("weights_hi_ready"), sem("weights_lo_ready"), sem("weights_lo_by_pool_ready")
        s_load = sem("load_waits_passed")
        s_clear, s_end, s_move = sem("rows_cleared"), sem("blocks_ended"), sem("row_moves_begun")
        s_hot, s_idp, s_token, s_row, s_next = (sem("slot_matches"), sem("ids_summed"), sem("tokens_ready"),
                                                sem("row_ids_ready"), sem("next_row_ids_ready"))
        s_rows = [sem("rows_gathered_0"), sem("rows_gathered_1")]
        s_j = sem("which_expert_ready")
        s_xt, s_xhi, s_xlo = sem("row_halves_transposed"), sem("row_halves_hi_ready"), sem("row_halves_lo_ready")
        s_gu, s_g, s_hid, s_hdt, s_hhi, s_hlo = (sem("up_ready"), sem("gate_ready"), sem("hidden_ready"),
                                                 sem("hidden_transposed"), sem("hidden_hi_ready"), sem("hidden_lo_ready"))
        s_dn, s_y0, s_y1 = sem("down_ready"), sem("y_left_ready"), sem("y_right_ready")
        s_out = [sem("y_stored_0"), sem("y_stored_1")]
        block = ctx.enter_context(nc.Block())

        def used_blocks(engine, body):
            for i in range(2):
                body(i, i, True)
            n = engine.value_load(route.n_blocks[0:1, 0:1], min_val=T * TOPK // P, max_val=2 * NB2)
            with engine.Fori(1, NB2) as pair:
                for i in range(2):
                    with engine.If(pair * 2 + i < n):
                        body(pair * 2 + i, i, False)
                    engine.nop()
            return n

        def expert_of(engine, b):
            return engine.value_load(route.block_expert[0:1, bass.ds(b, 1)], min_val=0, max_val=NE - 1)

        def unit(x, u):
            return x[:, UNIT * u:UNIT * u + UNIT]

        @block.sync
        def _(sp):
            def load(b, i, first=False):
                e = expert_of(sp, b)
                if not first:
                    sp.wait_ge(s_wlo, (b - 1) * len(BY_VECTOR))
                    sp.sem_inc(s_load, 1)
                    sp.wait_ge(s_wlo_pool, (b - 1) * len(BY_POOL))
                    sp.sem_inc(s_load, 1)
                for part, (at, n) in enumerate(((0, W_GU), (W_GU, W_EXP - W_GU))):
                    sp.dma_start(weights[i][:, at:at + n], dram["w_exp"][bass.ds(e, 1), :, at:at + n]
                                 .rearrange("a p n -> (a p) n")).then_inc(s_w[part][i], 16)

            load(0, 0, True)
            used_blocks(sp, lambda b, i, first: load(b + 1, 1 - i, first and i == 0))

        @block.gpsimd
        def _(pool):
            pool.memset(rows[0], 0.0)
            pool.memset(rows[1], 0.0).then_inc(s_clear, 1)
            pool.wait_ge(s_clear, 1)

            def gather(b, i, first):
                pool.wait_ge(s_token, b + 1)
                if not first:
                    pool.wait_ge(s_xt, b * 2 - 2)
                pool.sem_inc(s_move, 1)
                pool.indirect_dma_start(out=rows[i], out_offset=None, in_=dram["h1"],
                                        in_offset=bass.IndirectOffsetOnAxis(ap=token[i][:, 0:1], axis=0),
                                        bounds_check=T - 1, oob_is_err=False).then_inc(s_rows[i], 16)

            def scatter(b, i):
                pool.wait_ge(s_row, b + 1)
                pool.wait_ge(s_y0, b + 1)
                pool.wait_ge(s_y1, b + 1)
                pool.sem_inc(s_move, 1)
                pool.indirect_dma_start(out=dram["expert_rows"],
                                        out_offset=bass.IndirectOffsetOnAxis(ap=row_id[i][:, 0:1], axis=0),
                                        in_=y[i], in_offset=None, bounds_check=T * TOPK - 1, oob_is_err=False)\
                    .then_inc(s_out[i], 16)

            def split(b, i):
                for n, u in enumerate(BY_POOL):
                    pool.wait_ge(s_whi, b * UNITS + (u + 1))
                    pool.tensor_tensor(unit(w_lo[i], u), unit(weights[i], u), unit(w_hi[i], u), ALU.subtract)\
                        .then_inc(s_wlo_pool, 1)

            def work(b, i, first):
                gather(b + 2, i, False)
                split(b + 1, 1 - i)
                scatter(b, i)

            gather(0, 0, True)
            gather(1, 1, True)
            split(0, 0)
            n = used_blocks(pool, work)
            even, odd = pool.snap(((n + 1) >> 1) * 16), pool.snap((n >> 1) * 16)
            even_rows, odd_rows = pool.snap(((n + 1) >> 1) * 16 + 16), pool.snap((n >> 1) * 16 + 16)
            for done, value in ((s_rows[0], even_rows), (s_rows[1], odd_rows), (s_out[0], even), (s_out[1], odd)):
                pool.wait_ge(done, value)
                pool.sem_inc(s_end, 1)

        @block.tensor
        def _(pe):
            def sum_ids(b, first=False):
                e = expert_of(pe, b)
                pe.wait_ge(s_hot, b + 1)
                if not first:
                    pe.wait_ge(s_next, b)
                for t in range(TILES + 1):
                    last = nc.tensor.matmul(mem.bank[6][:, 0:2], hot[:, t, :],
                                            route.row[:, t, bass.ds(e, 1), :].rearrange("p a c -> p (a c)"),
                                            start=(t == 0), stop=(t == TILES))
                last.then_inc(s_idp, 1)

            def transpose_rows(b, i, half, first=False):
                if half == 0:
                    pe.wait_ge(s_rows[i], (b - i) * 8 + 16)
                if not first:
                    pe.wait_ge(s_xlo, b * 2 - 1 + half)
                for k in range(4):
                    at = P * (4 * half + k)
                    last = nc.tensor.transpose(mem.bank[half][:, P * k:P * k + P], rows[i][:, at:at + P], C("ident"))
                last.then_inc(s_xt, 1)

            def product(out, x_parts, w_parts, c, start, stop):
                (xh, xl), (wh, wl) = x_parts, w_parts
                nc.tensor.matmul(out, xh[:, c, :], wh, start=start, stop=False)
                nc.tensor.matmul(out, xh[:, c, :], wl, start=False, stop=False)
                return nc.tensor.matmul(out, xl[:, c, :], wh, start=False, stop=stop)

            def work(b, i, first):
                sum_ids(b + 2)
                pe.wait_ge(s_xlo, b * 2 + 2)
                if not (first and i == 0):
                    pe.wait_ge(s_hid, b)
                for k in range(DC):
                    if k % 2 == 0:
                        wait_unit(b, k // 2)
                    at = slice(512 * k, 512 * k + 512)
                    last = product(mem.bank[2][:, :], (x_hi[i], x_lo[i]), (w_hi[i][:, at], w_lo[i][:, at]), k,
                                   k == 0, k == DC - 1)
                last.then_inc(s_gu, 1)
                transpose_rows(b + 1, 1 - i, 0)
                pe.wait_ge(s_hid, b + 1)
                if not (first and i == 0):
                    pe.wait_ge(s_hlo, b)
                for c in range(FC):
                    last = nc.tensor.transpose(mem.bank[3][:, P * c:P * c + P], hidden[:, P * c:P * c + P], C("ident"))
                last.then_inc(s_hdt, 1)
                transpose_rows(b + 1, 1 - i, 1)
                pe.wait_ge(s_hlo, b + 1)
                if not (first and i == 0):
                    pe.wait_ge(s_y0, b)
                    pe.wait_ge(s_y1, b)
                for c in range(FC):
                    wait_unit(b, UNITS - FC + c)
                    for n in range(2):
                        at = slice(W_GU + D * c + 512 * n, W_GU + D * c + 512 * n + 512)
                        last = product(mem.bank[4 + n][:, :], (h_hi, h_lo), (w_hi[i][:, at], w_lo[i][:, at]), c,
                                       c == 0, c == FC - 1)
                last.then_inc(s_dn, 1)

            def wait_unit(b, u):
                if u in BY_POOL:
                    pe.wait_ge(s_wlo_pool, b * len(BY_POOL) + (BY_POOL.index(u) + 1))
                else:
                    pe.wait_ge(s_wlo, b * len(BY_VECTOR) + (BY_VECTOR.index(u) + 1))

            sum_ids(0, True)
            sum_ids(1)
            for half in range(2):
                transpose_rows(0, 0, half, True)
            used_blocks(pe, work)

        @block.scalar
        def _(act):
            def split(b, i, units, first=False):
                for u in units:
                    if u == 0:
                        act.wait_ge(s_w[0][i], (b - i) * 8 + 16)
                    if u == UNITS - FC:
                        act.wait_ge(s_w[1][i], (b - i) * 8 + 16)
                        if not first:
                            act.wait_ge(s_dn, b - 1)
                    nc.scalar.activation(unit(w_hi[i], u), unit(weights[i], u), ACT.Copy).then_inc(s_whi, 1)

            def read_rows(b, i, half, first=False):
                if not first:
                    act.wait_ge(s_gu, b - 1)
                act.wait_ge(s_xt, b * 2 + (1 + half))
                nc.scalar.activation(x_hi[i][:, 4 * half:4 * half + 4, :],
                                     mem.bank[half][:, :].rearrange("p (k i) -> p k i", k=4), ACT.Copy)\
                    .then_inc(s_xhi, 1)

            def work(b, i, first):
                begin = first and i == 0
                if not begin:
                    act.wait_ge(s_gu, b)
                split(b + 1, 1 - i, range(UNITS - FC), begin)
                act.wait_ge(s_gu, b + 1)
                if not begin:
                    act.wait_ge(s_hid, b)
                nc.scalar.activation(act_g, mem.bank[2][:, 0:FF], ACT.Silu).then_inc(s_g, 1)
                read_rows(b + 1, 1 - i, 0, begin)
                act.wait_ge(s_hdt, b + 1)
                if not begin:
                    act.wait_ge(s_dn, b)
                nc.scalar.activation(h_hi, mem.bank[3][:, 0:FC * P].rearrange("p (c i) -> p c i", c=FC), ACT.Copy)\
                    .then_inc(s_hhi, 1)
                read_rows(b + 1, 1 - i, 1, begin)
                split(b + 1, 1 - i, range(UNITS - FC, UNITS), begin)
                act.wait_ge(s_dn, b + 1)
                if not first:
                    act.wait_ge(s_out[i], (b - i) * 8)
                nc.scalar.activation(y[i][:, 0:512], mem.bank[4][:, :], ACT.Copy).then_inc(s_y0, 1)

            for half in range(2):
                read_rows(0, 0, half, True)
            split(0, 0, range(UNITS), True)
            used_blocks(act, work)

        @block.vector
        def _(dve):
            def match(b, first=False):
                e = expert_of(dve, b)
                if not first:
                    dve.wait_ge(s_idp, b)
                for t in range(TILES + 1):
                    last = nc.vector.tensor_scalar(hot[:, t, :], C("slots"),
                                                   route.dest[:, t, bass.ds(e, 1)], C("block")[:, bass.ds(b, 1)],
                                                   ALU.subtract, ALU.is_equal)
                last.then_inc(s_hot, 1)

            def read_ids(b, i):
                dve.wait_ge(s_idp, b + 1)
                nc.vector.tensor_scalar(token[i][:, :], mem.bank[6][:, 0:1], NO_TOKEN, None, ALU.add)\
                    .then_inc(s_token, 1)
                nc.vector.tensor_copy(pair_j[:, :], mem.bank[6][:, 1:2]).then_inc(s_j, 1)
                dve.wait_ge(s_j, b + 1)
                nc.vector.scalar_tensor_tensor(row_next[i][:, :], mem.bank[6][:, 0:1], float(TOPK), pair_j[:, :],
                                               ALU.mult, ALU.add).then_inc(s_next, 1)

            def keep_row_id(b, i, first):
                dve.wait_ge(s_next, b + 1)
                if not first:
                    dve.wait_ge(s_out[i], (b - i) * 8)
                nc.vector.tensor_scalar(row_id[i][:, :], row_next[i][:, :], NO_TOKEN * TOPK, None, ALU.add)\
                    .then_inc(s_row, 1)
                dve.wait_ge(s_row, b + 1)

            def split(b, i, units):
                for u in units:
                    if u in BY_VECTOR:
                        dve.wait_ge(s_whi, b * UNITS + (u + 1))
                        nc.vector.tensor_tensor(unit(w_lo[i], u), unit(weights[i], u), unit(w_hi[i], u),
                                                ALU.subtract).then_inc(s_wlo, 1)

            def split_rows(b, i, half):
                dve.wait_ge(s_xhi, b * 2 + (1 + half))
                at = slice(4 * half, 4 * half + 4)
                nc.vector.tensor_tensor(x_lo[i][:, at, :], mem.bank[half][:, :].rearrange("p (k i) -> p k i", k=4),
                                        x_hi[i][:, at, :], ALU.subtract).then_inc(s_xlo, 1)

            def work(b, i, first):
                split(b + 1, 1 - i, range(0, 2))
                keep_row_id(b, i, first)
                read_ids(b + 2, i)
                match(b + 3)
                split(b + 1, 1 - i, range(2, UNITS - FC))
                dve.wait_ge(s_g, b + 1)
                if not (first and i == 0):
                    dve.wait_ge(s_hdt, b)
                nc.vector.tensor_tensor(hidden, act_g, mem.bank[2][:, FF:2 * FF], ALU.mult).then_inc(s_hid, 1)
                split_rows(b + 1, 1 - i, 0)
                dve.wait_ge(s_hhi, b + 1)
                nc.vector.tensor_tensor(h_lo, mem.bank[3][:, 0:FC * P].rearrange("p (c i) -> p c i", c=FC), h_hi,
                                        ALU.subtract).then_inc(s_hlo, 1)
                split_rows(b + 1, 1 - i, 1)
                split(b + 1, 1 - i, range(UNITS - FC, UNITS))
                dve.wait_ge(s_dn, b + 1)
                if not first:
                    dve.wait_ge(s_out[i], (b - i) * 8)
                nc.vector.tensor_copy(y[i][:, 512:D], mem.bank[5][:, :]).then_inc(s_y1, 1)

            match(0, True)
            for b in range(2):
                read_ids(b, b)
                match(b + 1)
            for half in range(2):
                split_rows(0, 0, half)
            split(0, 0, range(UNITS))
            used_blocks(dve, work)


def combine_stage(nc, mem, dram, route):
    with ExitStack() as ctx:
        def sem(name):
            return ctx.enter_context(nc.semaphore(name))

        carve = mem.carve
        work = mem.sbuf(ctx, "combine_work", 2 * TOPK * D)
        long = mem.sbuf(ctx, "combine_rows", 6 * D + 32)
        got = [carve(work, TOPK * D * i, TOPK, D) for i in range(2)]
        acc = [carve(long, D * i, D) for i in range(2)]
        out = [carve(long, D * (2 + i), D) for i in range(2)]
        ln = carve(long, 4 * D, 2, D)
        stats = carve(long, 6 * D, 32)

        s_ln = sem("norm_loaded")
        s_acc = [sem("residual_loaded_0"), sem("residual_loaded_1")]
        s_got = [sem("expert_rows_loaded_0"), sem("expert_rows_loaded_1")]
        s_used, s_y, s_v = sem("expert_rows_used"), sem("y_ready"), sem("combine_vector_steps")
        s_out = [sem("y_stored_0"), sem("y_stored_1")]
        block = ctx.enter_context(nc.Block())
        tiles = token_tiles()
        by_token = dram["expert_rows"].rearrange("(t j) d -> t j d", j=TOPK)

        @block.sync
        def _(sp):
            def load(t):
                w = tiles[t][2]
                sp.dma_start(acc[t % 2][0:w], dram["residual"][P * t:P * t + w, :]).then_inc(s_acc[t % 2], 16)
                for half in range(2):
                    js = slice(4 * half, 4 * half + 4)
                    sp.dma_start(got[t % 2][0:w, js, :], by_token[P * t:P * t + w, js, :]).then_inc(s_got[t % 2], 16)

            load(0)
            sp.dma_start(ln, dram["norms"][:, 2:4, :]).then_inc(s_ln, 16)
            load(1)
            for t, _, w, _, _ in tiles:
                sp.wait_ge(s_y, t + 1)
                sp.dma_start(dram["y"][P * t:P * t + w, :], out[t % 2][0:w]).then_inc(s_out[t % 2], 16)
                if t + 2 <= TILES:
                    load(t + 2)
            sp.wait_ge(s_out[0], 48)
            sp.wait_ge(s_out[1], 32)

        @block.vector
        def _(dve):
            steps = Steps(dve, s_v)
            dve.wait_ge(s_ln, 16)
            for t, _, w, _, _ in tiles:
                dve.wait_ge(s_acc[t % 2], 16 * (t // 2 + 1))
                dve.wait_ge(s_got[t % 2], 32 * (t // 2 + 1))
                a = acc[t % 2][0:w]
                for j in range(TOPK):
                    steps.link(nc.vector.scalar_tensor_tensor(a, got[t % 2][0:w, j, :], route.weight[0:w, t, j:j + 1], a,
                                                              ALU.mult, ALU.add))
                if t >= 2:
                    dve.wait_ge(s_out[t % 2], 16 * (t // 2))
                layer_norm(nc, steps, a, stats[0:w], ln[0:w, 0, :], ln[0:w, 1, :], out[t % 2][0:w]).then_inc(s_y, 1)


def build(nc, dram):
    with ExitStack() as ctx:
        dram = dict(dram, h1=nc.dram_tensor("h1_rows", (T, D), F32, kind="Internal").ap(),
                    residual=nc.dram_tensor("residual_rows", (T, D), F32, kind="Internal").ap(),
                    expert_rows=nc.dram_tensor("expert_rows", (T * TOPK, D), F32, kind="Internal").ap())
        mem = Memory(nc, ctx)
        route = Routing(mem)
        with ExitStack() as front:
            mem.mixed_rows(front)
            with ExitStack() as delta:
                mem.delta_inputs(delta)
                projection_stage(nc, mem, dram)
                delta_rule_stage(nc, mem, dram)
            mixing_stage(nc, mem, dram, route)
        expert_stage(nc, mem, dram, route)
        combine_stage(nc, mem, dram, route)


def constant_tables():
    c = np.zeros((P, N_CONSTS), np.float32)

    def put(name, value):
        at, n = CONSTS[name]
        c[:, at:at + n] = value

    p, q = np.arange(P)[:, None], np.arange(P)[None, :]
    put("ident", p == q)
    put("tri", p <= q)
    put("before", p < q)
    put("ones", 1.0)
    put("masks", np.concatenate([((p >> l) % 2 == 1) & ((q >> l) == (p >> l) - 1) for l in range(LEVELS)], 1))
    put("future", np.where(q < p, -BIG, 0.0))
    put("slots", q)
    put("experts", np.arange(NE)[None, :])
    t = np.arange(TILES + 1)[None, :]
    put("token_base", p + P * t - NO_TOKEN)
    put("valid", (p + P * t) < T)
    put("row", p)
    put("block", -float(P) * np.arange(2 * NB2 + 3)[None, :])
    put("over", P * t)
    return c


def kernel(**inputs):
    from concourse import bacc
    from concourse.bass_utils import run_bass_kernel_spmd

    x = {k: np.asarray(v) for k, v in inputs.items()}

    def feature_major(a, n):
        return a.reshape(-1, n, P).transpose(2, 1, 0)

    def rows(a):
        return np.broadcast_to(a.reshape(1, -1), (P, a.size))

    both = np.concatenate([x["x_prompt"][0], x["x_sample"][0]])
    x_t = np.zeros((P, DC, TW), np.float32)
    x_t[:, :, :SEQ] = feature_major(both[:SEQ], DC)
    x_t[:, :, S0:S0 + DEC] = feature_major(both[SEQ:], DC)
    w = x["w_in"][0]
    v_end, z_end = QKV, QKV + D
    lx, ly = z_end + 2 * H, z_end + 2 * H + D
    order = np.concatenate([w[:, lx:lx + D], w[:, ly:ly + D], w[:, :v_end], w[:, v_end:z_end]], 1)
    w_in = order.reshape(DC, P, NCH, P).transpose(2, 1, 0, 3)
    w_ba = w[:, z_end:lx].reshape(DC, P, 2 * H).transpose(1, 0, 2)
    conv_w = np.concatenate([x["lru_conv_w"][0], x["gdn_conv_w"][0]], 1)
    conv_b = np.concatenate([x["lru_conv_b"][0], np.zeros(QKV, np.float32)])
    hist = np.concatenate([x["state_lru_conv"][0, 0], x["state_gdn_conv"][0, 0]], 1)
    params = np.concatenate([
        feature_major(conv_w, 32).reshape(P, -1), feature_major(conv_b, 32).reshape(P, -1),
        feature_major(hist, 32).reshape(P, -1), feature_major(x["state_lru"][0, 0], DC).reshape(P, -1),
        feature_major(x["lru_lambda"][0], DC).reshape(P, -1),
        feature_major(x["lru_ba"][0], DC).reshape(P, -1), feature_major(x["lru_bx"][0], DC).reshape(P, -1),
        rows(x["gdn_dt_bias"][0]), rows(x["gdn_a_log"][0]), x["gdn_norm_w"][0].reshape(P, 1),
        rows(x["router_bias"][0]),
    ], 1)
    gates = np.concatenate([x["lru_wa"][0], x["lru_wx"][0]]).transpose(1, 0, 2)
    w_gu = np.stack([x["exp_w_gate"][0], x["exp_w_up"][0]], 2).reshape(NE, DC, P, 2 * FF).transpose(0, 2, 1, 3)
    w_dn = x["exp_w_down"][0].reshape(NE, FC, P, D).transpose(0, 2, 1, 3)
    w_exp = np.concatenate([w_gu.reshape(NE, P, -1), w_dn.reshape(NE, P, -1)], 2)
    s_gu = np.stack([x["sh_w_gate"][0], x["sh_w_up"][0]], 1).reshape(DC, P, 2 * FF).transpose(1, 0, 2)
    s_dn = x["sh_w_down"][0].reshape(FC, P, D).transpose(1, 0, 2)
    w_sh = np.concatenate([s_gu.reshape(P, -1), s_dn.reshape(P, -1)], 1)
    ins = {
        "consts": constant_tables(), "params": params, "x_t": x_t, "x_rows": both, "w_in": w_in, "w_ba": w_ba,
        "gates": gates, "state": x["state_gdn"][0, 0].transpose(1, 0, 2),
        "w_out": x["w_out"][0].reshape(2 * DC, P, D).transpose(1, 0, 2),
        "norms": np.stack([rows(x[n][0]) for n in ("ln1_g", "ln1_b", "ln2_g", "ln2_b")], 1),
        "w_router": x["router_w"][0].reshape(DC, P, NE).transpose(1, 0, 2), "w_sh": w_sh, "w_exp": w_exp,
    }
    ins = {k: np.ascontiguousarray(v) for k, v in ins.items()}
    outs = {
        "y": (T, D), "tails": (P, 32, 2 * GAP), "states": (2, P, H, P), "lru_last": (P, DC, 2),
    }
    nc = bacc.Bacc("TRN2", target_bir_lowering=False, num_devices=1)
    dram = {}
    for name, a in ins.items():
        dram[name] = nc.dram_tensor(f"in_{name}", a.shape, mybir.dt.from_np(a.dtype), kind="ExternalInput").ap()
    for name, shape in outs.items():
        dram[name] = nc.dram_tensor(f"out_{name}", shape, F32, kind="ExternalOutput").ap()
    build(nc, dram)
    got = run_bass_kernel_spmd(nc, [{f"in_{k}": v for k, v in ins.items()}], core_ids=[0]).results[0]
    y, tails, states, last = (got[f"out_{n}"] for n in outs)

    def tail(lo, hi, which):
        a = tails[:, lo:hi, GAP * which:GAP * (which + 1)]
        return a.transpose(2, 1, 0).reshape(1, 1, GAP, (hi - lo) * P)

    def result(which):
        return (tail(DC, 32, which), states[which].transpose(1, 0, 2)[None, None], tail(0, DC, which),
                last[:, :, which].T.reshape(1, 1, D))

    return (y[:SEQ][None], y[SEQ:][None], *result(0), *result(1))
```

```python
import functools
from contextlib import ExitStack

import numpy as np

import concourse.bass as bass
from concourse import mybir

F32 = mybir.dt.float32
BF16 = mybir.dt.bfloat16
I32 = mybir.dt.int32
U32 = mybir.dt.uint32
F32R = mybir.dt.float32r
ALU = mybir.AluOpType
ACT = mybir.ActivationFunctionType
AX = mybir.AxisListType

P = 128
D = 1024
SEQ = 512
DEC = 32
H = 8
DC = D // P
TILES = SEQ // P
QKV = 3 * D
CONV = 4
NQ = QKV // P
NCH = 6 * D // P
LRU_C = 8.0
GAP = CONV - 1
S0 = SEQ + GAP
TW = S0 + DEC + 1
HALF = TW // 2
RW = TW + GAP
NE = 64
TOPK = 8
NG = 8
TOPG = 4
GE = NE // NG
FF = 256
FC = FF // P
T = SEQ + DEC
NB = (T * TOPK + NE * (P - 1)) // P + 1
NB2 = (NB + 1) // 2
NO_TOKEN = 1024.0
SCALE = 2.5
ALPHA = 2.0 ** 0.25
LN_EPS = 1e-5
RMS_EPS = 1e-6
BIG = 1e30
LEVELS = 7

CONSTS = {}
_at = 0
for _name, _n in (("ident", P), ("tri", P), ("before", P), ("ones", P), ("masks", LEVELS * P), ("future", P),
                  ("slots", P), ("experts", NE), ("token_base", TILES + 1), ("valid", TILES + 1), ("row", 1), ("ln_eps", 1), ("block", 2 * NB2 + 3),
                  ("over", TILES + 1)):
    CONSTS[_name] = (_at, _n)
    _at += _n
N_CONSTS = _at

PARAMS = {}
_at = 0
for _name, _n in (("conv_w", 4 * 32), ("conv_b", 32), ("hist", 3 * 32), ("h0", DC), ("lam", DC), ("gate_b", 2 * DC),
                  ("dt", H), ("a_log", H), ("norm_w", 1), ("route_b", NE)):
    PARAMS[_name] = (_at, _n)
    _at += _n
N_PARAMS = _at


class Steps:

    def __init__(self, engine, sem, base=0):
        self.engine, self.sem, self.n, self.base = engine, sem, 0, base

    def done(self, instruction):
        instruction.then_inc(self.sem, 1)
        self.n += 1
        return self

    def wait(self):
        self.engine.wait_ge(self.sem, self.n + self.base)

    def link(self, instruction):
        self.done(instruction).wait()


class Views:

    def __init__(self, tile, table):
        self.tile, self.table = tile, table

    def __call__(self, name, *dims):
        at, n = self.table[name]
        view = self.tile[:, at:at + n]
        if dims:
            names = [f"d{i}" for i in range(len(dims))]
            view = view.rearrange(f"p ({' '.join(names)}) -> p {' '.join(names)}", **dict(zip(names, dims)))
        return view


def rsqrt(nc, steps, out, y, scratch, factor=1.0):
    g, h = scratch
    steps.link(nc.vector.tensor_scalar(g.bitcast(I32), y.bitcast(I32), -0.5, 1597463007.0, ALU.mult, ALU.add))
    for step in range(4):
        steps.link(nc.vector.tensor_tensor(h, g, g, ALU.mult))
        steps.link(nc.vector.tensor_tensor(h, h, y, ALU.mult))
        steps.link(nc.vector.tensor_scalar(h, h, -0.5, 1.5, ALU.mult, ALU.add))
        if step < 3:
            steps.link(nc.vector.tensor_tensor(g, g, h, ALU.mult))
        else:
            steps.link(nc.vector.scalar_tensor_tensor(out, g, factor, h, ALU.mult, ALU.mult))


def inverse_root(nc, steps, out, y, root, h):
    steps.link(nc.vector.reciprocal(out, root))
    steps.link(nc.vector.tensor_tensor(h, out, out, ALU.mult))
    steps.link(nc.vector.tensor_tensor(h, h, y, ALU.mult))
    steps.link(nc.vector.tensor_scalar(h, h, -0.5, 1.5, ALU.mult, ALU.add))
    steps.link(nc.vector.tensor_tensor(out, out, h, ALU.mult))


class Memory:

    def __init__(self, nc, ctx):
        self.nc, self.ctx = nc, ctx
        self.consts = Views(self.sbuf(ctx, "consts", N_CONSTS), CONSTS)
        self.params = Views(self.sbuf(ctx, "params", N_PARAMS), PARAMS)
        self.states = self.sbuf(ctx, "states", 2 * H * P)
        self.chosen = self.sbuf(ctx, "chosen", (TILES + 1) * NE, BF16)
        self.passed = ctx.enter_context(nc.semaphore("waits_passed"))
        self.row = self.sbuf(ctx, "row", (TILES + 1) * NE * 2, F32R)
        self.bank = [ctx.enter_context(nc.psum_tensor(f"bank{i}", [P, 512], F32)) for i in range(8)]

    def sbuf(self, ctx, name, words, dt=F32):
        return ctx.enter_context(self.nc.sbuf_tensor(name, [P, words], dt))

    def mixed_rows(self, ctx):
        self.zt = self.sbuf(ctx, "zt", DC * TW)
        self.lru = self.sbuf(ctx, "lru", DC * TW)

    def delta_inputs(self, ctx):
        self.qkv = self.sbuf(ctx, "qkv", NQ * TW)
        self.decay = self.sbuf(ctx, "decay", 8 * (TILES + 1) * H)

    def carve(self, tile, at, *dims):
        n = int(np.prod(dims))
        view = tile[:, at:at + n]
        if len(dims) > 1:
            names = [f"d{i}" for i in range(len(dims))]
            view = view.rearrange(f"p ({' '.join(names)}) -> p {' '.join(names)}", **dict(zip(names, dims)))
        return view


def projection_stage(nc, mem, dram):
    with ExitStack() as ctx:
        def sem(name):
            return ctx.enter_context(nc.semaphore(name))

        C, PR = mem.consts, mem.params
        carve = mem.carve
        def take(name, *dims, dt=F32):
            return carve(mem.sbuf(ctx, name, int(np.prod(dims)), dt), 0, *dims)

        w_raw = [take(f"w_raw{i}", DC, P) for i in range(2)]
        w_hi = [take(f"w_hi{i}", DC, P, dt=F32R) for i in range(2)]
        w_lo = [take(f"w_lo{i}", DC, P, dt=F32R) for i in range(2)]
        x_hi, x_lo = take("x_hi", DC, TW, dt=F32R), take("x_lo", DC, TW, dt=F32R)
        t_r = take("rate", DC, TW)
        raw = [take(f"raw{i}", RW) for i in range(4)]
        conv = [take(f"conv{i}", TW) for i in range(2)]
        qkv = carve(mem.qkv, 0, NQ, TW)
        t_i, xc = qkv[:, 8:16, :], qkv[:, 16:24, :]
        zt = carve(mem.zt, 0, DC, TW)
        x_t, mult = zt, zt
        lru = carve(mem.lru, 0, DC, TW)
        gates = carve(mem.states, 0, 2 * DC, P)
        n_d = (TILES + 1) * H
        beta, g_, gsum, gneg, eg, egl, gtot = (
            carve(mem.decay, n_d * i, TILES + 1, H) for i in (0, 1, 2, 3, 4, 5, 7))
        small = ctx.enter_context(nc.sbuf_tensor("small", [P, 640], F32))
        w_ba = carve(small, 0, DC, 2 * H)
        ba = carve(small, 128, TILES + 1, 2 * H)
        soft_x, soft_w, soft_z, soft_z2, soft_p = (carve(small, 208 + 48 * i, 48) for i in range(5))
        c_lru = carve(small, 448, DC)
        c_neg = carve(small, 456, DC)
        gate_half = carve(small, 464, 2 * DC)
        nexp_a = carve(small, 480, H)
        last_h = carve(small, 488, DC, 2)
        tails = ctx.enter_context(nc.sbuf_tensor("tails", [P, 32, 2 * GAP], F32))

        s_const, s_wba, s_gates = sem("consts_loaded"), sem("w_ba_loaded"), sem("gates_loaded")
        s_x = [sem("x_left_loaded"), sem("x_right_loaded")]
        s_xhi, s_xlo = sem("x_hi_ready"), sem("x_lo_ready")
        s_win = [sem("w_in_loaded_0"), sem("w_in_loaded_1")]
        s_whi, s_wlo = sem("w_hi_ready"), sem("w_lo_ready")
        s_proj, s_psum = sem("channels_projected"), sem("psum_read")
        s_ba, s_exp = sem("ba_projected"), sem("small_exps_ready")
        s_soft_e, s_softp = sem("softplus_argument"), sem("lru_rate_ready")
        s_g, s_gs, s_gread = sem("log_decay_ready"), sem("decay_summed"), sem("decay_exp_ready")
        s_conv, s_fin = sem("conv_ready"), sem("channels_finished")
        s_gate, s_gateread, s_gated = sem("gates_projected"), sem("gates_read"), sem("inputs_gated")
        s_a, s_sq, s_mult2, s_mult = sem("a_ready"), sem("a_squared"), sem("mult_squared"), sem("mult_ready")
        s_first, s_scaled = sem("first_multiplier_set"), sem("inputs_scaled")
        s_lru, s_lru_out, s_last = sem("channels_scanned"), sem("lru_outputs_ready"), sem("last_rows_ready")
        s_v = sem("vector_steps")
        s_out = sem("outputs_stored")
        block = ctx.enter_context(nc.Block())

        @block.sync
        def _(sp):
            def load(m, i, first=False):
                if not first:
                    sp.wait_ge(s_wlo, m - 1)
                    sp.sem_inc(mem.passed, 1)
                sp.dma_start(w_raw[i], dram["w_in"][bass.ds(m, 1)].rearrange("a p k n -> (a p) k n"))\
                    .then_inc(s_win[i], 16)

            load(0, 0, True)
            for half in range(2):
                ks = slice(4 * half, 4 * half + 4)
                sp.dma_start(x_t[:, ks, :], dram["x_t"][:, ks, :]).then_inc(s_x[half], 16)
            load(1, 1, True)
            sp.dma_start(w_ba, dram["w_ba"]).then_inc(s_wba, 16)
            sp.dma_start(mem.consts.tile[:, :], dram["consts"]).then_inc(s_const, 16)
            sp.dma_start(mem.params.tile[:, :], dram["params"]).then_inc(s_const, 16)
            load(2, 0)
            load(3, 1)
            sp.dma_start(gates, dram["gates"]).then_inc(s_gates, 16)
            with sp.Fori(2, NCH // 2) as pair:
                for i in range(2):
                    load(pair * 2 + i, i)
            sp.wait_ge(s_last, 1)
            sp.dma_start(dram["lru_last"], last_h).then_inc(s_out, 16)
            sp.wait_ge(s_conv, 32)
            sp.dma_start(dram["tails"], tails[:, :, :]).then_inc(s_out, 16)
            sp.wait_ge(s_out, 32)

        @block.gpsimd
        def _(pool):
            def split(m, i):
                pool.wait_ge(s_whi, m + 1)
                pool.tensor_tensor(w_lo[i], w_raw[i], w_hi[i], ALU.subtract).then_inc(s_wlo, 1)

            def scale_input(j):
                pool.wait_ge(s_first, 1)
                pool.tensor_tensor(t_i[:, j, :], t_i[:, j, :], mult[:, j, :], ALU.mult).then_inc(s_scaled, 1)

            with pool.Fori(0, 11) as pair:
                for i in range(2):
                    split(pair * 2 + i, i)
            scale_input(0)
            scale_input(1)
            for j in range(8):
                if j % 2 == 0:
                    split(22 + j // 2, (j // 2) % 2)
                if j < 6:
                    scale_input(j + 2)
                pool.wait_ge(s_lru, j + 1)
                pool.tensor_tensor(lru[:, j, :], lru[:, j, :], mult[:, j, :], ALU.mult).then_inc(s_lru_out, 1)
            with pool.Fori(13, NCH // 2) as pair:
                for i in range(2):
                    split(pair * 2 + i, i)

        def project(pe, n, j, first=False):
            pe.wait_ge(s_wlo, n + 1)
            if not first:
                pe.wait_ge(s_psum, n - 1)
            wh, wl = w_hi[j % 2], w_lo[j % 2]
            for half in range(2):
                out = mem.bank[2 * (j % 2) + half][:, 0:HALF]
                at = slice(half * HALF, (half + 1) * HALF)
                for k in range(DC):
                    if isinstance(n, int) and n == 0 and half == 0:
                        pe.wait_ge(s_xlo, k + 1)
                    nc.tensor.matmul(out, wh[:, k, :], x_hi[:, k, at], start=(k == 0), stop=False)
                    nc.tensor.matmul(out, wh[:, k, :], x_lo[:, k, at], start=False, stop=False)
                    last = nc.tensor.matmul(out, wl[:, k, :], x_hi[:, k, at], start=False, stop=(k == DC - 1))
            last.then_inc(s_proj, 1)

        @block.tensor
        def _(pe):
            for n in range(16):
                project(pe, n, n % 8, n < 2)
                if n == 0:
                    pe.wait_ge(s_wba, 16)
                    for t in range(TILES + 1):
                        at, w = (t * P, P) if t < TILES else (S0, DEC)
                        for k in range(DC):
                            last = nc.tensor.matmul(mem.bank[4][0:w, 16 * t:16 * t + 16], x_t[:, k, at:at + w],
                                                    w_ba[:, k, :], start=(k == 0), stop=(k == DC - 1))
                    last.then_inc(s_ba, 1)
                if n == 3:
                    pe.wait_ge(s_g, 1)
                    nc.tensor.matmul(mem.bank[5][:, 0:n_d], C("tri"), g_.rearrange("p t h -> p (t h)"),
                                     start=True, stop=True)
                    nc.tensor.matmul(mem.bank[6][:, 0:n_d], C("ones"), g_.rearrange("p t h -> p (t h)"),
                                     start=True, stop=True).then_inc(s_gs, 1)
                if n >= 8:
                    b = n - 8
                    if b == 0:
                        pe.wait_ge(s_gates, 16)
                        pe.wait_ge(s_gread, 1)
                    pe.wait_ge(s_conv, b + 1)
                    if b:
                        pe.wait_ge(s_gateread, b)
                    for m in range(2):
                        for half in range(2):
                            last = nc.tensor.matmul(mem.bank[4 + 2 * m + half][:, 0:HALF], gates[:, m * DC + b, :],
                                                    xc[:, b, half * HALF:(half + 1) * HALF], start=True, stop=True)
                    last.then_inc(s_gate, 1)
            with pe.Fori(2, 6) as u:
                for j in range(8):
                    project(pe, u * 8 + j, j)

        def two_halves(j, out, func, **kw):
            nc.scalar.activation(out[0], mem.bank[2 * (j % 2)][:, 0:HALF], func, **kw)
            return nc.scalar.activation(out[1], mem.bank[2 * (j % 2) + 1][:, 0:HALF], func, **kw)

        def halves(x):
            return x[:, 0:HALF], x[:, HALF:TW]

        def evacuate(act, n, j, m, first):
            act.wait_ge(s_proj, n + 1)
            if not first:
                act.wait_ge(s_conv, m - 3)
            two_halves(j, halves(raw[j % 4][:, GAP:RW]), ACT.Copy).then_inc(s_psum, 1)

        @block.scalar
        def _(act):
            def split(m, j):
                act.wait_ge(s_win[j % 2], (m - j % 2) * 8 + 16)
                nc.scalar.activation(w_hi[j % 2], w_raw[j % 2], ACT.Copy).then_inc(s_whi, 1)

            split(0, 0)
            for k in range(DC):
                act.wait_ge(s_x[k // 4], 16)
                nc.scalar.activation(x_hi[:, k, :], x_t[:, k, :], ACT.Copy).then_inc(s_xhi, 1)
            split(1, 1)
            for n in range(8):
                evacuate(act, n, n, n, n < 4)
                split(n + 2, (n + 2) % 8)
                if n == 0:
                    act.wait_ge(s_soft_e, 1)
                    nc.scalar.activation(soft_w, soft_w, ACT.Exp, scale=-1.0)
                    nc.scalar.activation(nexp_a, PR("a_log"), ACT.Exp)
                    nc.scalar.activation(beta, ba[:, :, 0:H], ACT.Tanh, scale=0.5).then_inc(s_exp, 1)
                if n == 3:
                    act.wait_ge(s_gs, 1)
                    flat = [v.rearrange("p t h -> p (t h)") for v in (gsum, gneg, eg, egl, gtot)]
                    nc.scalar.activation(flat[0], mem.bank[5][:, 0:n_d], ACT.Copy)
                    nc.scalar.activation(flat[1], mem.bank[5][:, 0:n_d], ACT.Copy, scale=-1.0)
                    nc.scalar.activation(flat[2], mem.bank[5][:, 0:n_d], ACT.Exp)
                    nc.scalar.activation(flat[4], mem.bank[6][:, 0:n_d], ACT.Copy)
                    nc.scalar.activation(flat[3], mem.bank[6][:, 0:n_d], ACT.Exp).then_inc(s_gread, 1)
            act.wait_ge(s_softp, 1)
            for j in range(8):
                act.wait_ge(s_proj, 8 + j + 1)
                two_halves(j, halves(lru[:, j, :]), ACT.Gelu_apprx_tanh).then_inc(s_psum, 1)
                split(10 + j, (10 + j) % 8)
                act.wait_ge(s_gate, j + 1)
                for m, out in enumerate((t_r, t_i)):
                    for half, part in enumerate(halves(out[:, j, :])):
                        last = nc.scalar.activation(part, mem.bank[4 + 2 * m + half][:, 0:HALF], ACT.Tanh,
                                                    bias=gate_half[:, m * DC + j:m * DC + j + 1], scale=0.5)
                last.then_inc(s_gateread, 1)
                act.wait_ge(s_gateread, j + 1)
                nc.scalar.activation(mult[:, j, :], t_r[:, j, :], ACT.Tanh, bias=c_neg[:, j:j + 1],
                                     scale=c_neg[:, j:j + 1])

            def silu(u, j):
                act.wait_ge(s_conv, u * 8 + (j - 8 + 1))
                nc.scalar.activation(qkv[:, bass.ds(u * 8 + (j - 16), 1), :].rearrange("p a t -> p (a t)"),
                                     conv[j % 2], ACT.Silu).then_inc(s_fin, 1)

            def convolved_tile(u, j):
                evacuate(act, u * 8 + j, j, u * 8 + (j - 8), False)
                split(u * 8 + (j + 2), (j + 2) % 8)
                if j:
                    silu(u, j - 1)

            def rates(js):
                for j in js:
                    nc.scalar.activation(t_r[:, j, :], t_r[:, j, :], ACT.Exp, bias=c_lru[:, j:j + 1],
                                         scale=c_lru[:, j:j + 1]).then_inc(s_a, 1)

            rates(range(4))
            for j in range(8):
                convolved_tile(2, j)
                if j == 0:
                    rates(range(4, 8))
                    act.wait_ge(s_a, 8)
                    act.wait_ge(s_gated, 8)
                    nc.scalar.activation(xc, t_r, ACT.Square).then_inc(s_sq, 1)
                if j == 3:
                    act.wait_ge(s_mult2, 1)
                    nc.scalar.activation(mult, mult, ACT.Sqrt, scale=0.25).then_inc(s_mult, 1)
            silu(2, 7)
            act.wait_ge(s_lru, 8)
            with act.Fori(3, 5) as u:
                for j in range(8):
                    convolved_tile(u, j)
                silu(u, 7)
            act.wait_ge(s_lru_out, 8)
            act.wait_ge(s_last, 1)
            for j in range(8):
                act.wait_ge(s_proj, 40 + j + 1)
                two_halves(j, halves(zt[:, j, :]), ACT.Silu).then_inc(s_psum, 1)
                if j < 6:
                    split(42 + j, (42 + j) % 8)

        def convolve(dve, steps, n, m, j, out):
            r = raw[j % 4]

            def param(name, per_tile, at, width=1):
                return PR(name)[:, bass.ds(m * per_tile + at, width)]

            dve.wait_ge(s_psum, n + 1)
            steps.link(nc.vector.tensor_scalar(r[:, S0:S0 + GAP], param("hist", GAP, 0, GAP), 1.0, None, ALU.mult))
            for which, at in enumerate((SEQ, S0 + DEC)):
                nc.vector.tensor_scalar(tails[:, bass.ds(m, 1), GAP * which:GAP * (which + 1)]
                                        .rearrange("p a t -> p (a t)"), r[:, at:at + GAP], 1.0, None, ALU.mult)
            acc = conv[j % 2]
            steps.link(nc.vector.tensor_scalar(acc, r[:, 0:TW], param("conv_w", CONV, 0), param("conv_b", 1, 0),
                                               ALU.mult, ALU.add))
            for k in range(1, CONV):
                last = nc.vector.scalar_tensor_tensor(out if k == CONV - 1 else acc, r[:, k:k + TW],
                                                      param("conv_w", CONV, k), acc, ALU.mult, ALU.add)
                if k < CONV - 1:
                    steps.link(last)
            return last

        LINKS = CONV

        @block.vector
        def _(dve):
            steps = Steps(dve, s_v)
            for r in raw:
                nc.vector.memset(r[:, 0:GAP], 0.0)
            steps.link(nc.vector.memset(ba, 0.0))
            for k in range(DC):
                dve.wait_ge(s_xhi, k + 1)
                nc.vector.tensor_tensor(x_lo[:, k, :], x_t[:, k, :], x_hi[:, k, :], ALU.subtract).then_inc(s_xlo, 1)
            dve.wait_ge(s_const, 32)
            dve.wait_ge(s_ba, 1)
            nc.vector.tensor_copy(ba[:, 0:TILES, :], mem.bank[4][:, 0:16 * TILES].rearrange("p (t c) -> p t c", c=16))
            steps.link(nc.vector.tensor_copy(ba[0:DEC, TILES, :], mem.bank[4][0:DEC, 16 * TILES:16 * TILES + 16]))
            nc.vector.tensor_scalar(soft_x[:, 0:DC], PR("lam"), -1.0, None, ALU.mult)
            steps.link(nc.vector.tensor_tensor(
                soft_x[:, DC:].rearrange("p (t h) -> p t h", h=H), ba[:, :, H:2 * H],
                PR("dt").unsqueeze(1).to_broadcast([P, TILES + 1, H]), ALU.add))
            steps.link(nc.vector.tensor_scalar(soft_w, soft_x, -1.0, None, ALU.mult))
            nc.vector.tensor_tensor(soft_w, soft_w, soft_x, ALU.max).then_inc(s_soft_e, 1)
            dve.wait_ge(s_exp, 1)
            steps.link(nc.vector.tensor_scalar(soft_z, soft_w, 2.0, None, ALU.add))
            steps.link(nc.vector.reciprocal(soft_z, soft_z))
            steps.link(nc.vector.tensor_tensor(soft_z, soft_z, soft_w, ALU.mult))
            steps.link(nc.vector.tensor_tensor(soft_z2, soft_z, soft_z, ALU.mult))
            steps.link(nc.vector.tensor_scalar(soft_p, soft_z2, 1.0 / 15, None, ALU.mult))
            for odd in (13, 11, 9, 7, 5, 3):
                steps.link(nc.vector.scalar_tensor_tensor(soft_p, soft_p, 1.0 / odd, soft_z2, ALU.add, ALU.mult))
            steps.link(nc.vector.scalar_tensor_tensor(soft_p, soft_p, 1.0, soft_z, ALU.add, ALU.mult))
            steps.link(nc.vector.tensor_scalar(soft_x, soft_x, 0.0, None, ALU.max))
            steps.link(nc.vector.scalar_tensor_tensor(soft_x, soft_p, 2.0, soft_x, ALU.mult, ALU.add))
            nc.vector.tensor_scalar(c_lru, soft_x[:, 0:DC], -0.5 * LRU_C, None, ALU.mult)
            nc.vector.tensor_scalar(c_neg, soft_x[:, 0:DC], 0.5 * LRU_C, None, ALU.mult)
            nc.vector.tensor_scalar(gate_half, PR("gate_b"), 0.5, None, ALU.mult).then_inc(s_softp, 1)
            valid = C("valid").unsqueeze(2).to_broadcast([P, TILES + 1, H])
            steps.link(nc.vector.tensor_scalar(nexp_a, nexp_a, -1.0, None, ALU.mult))
            steps.link(nc.vector.tensor_tensor(g_, soft_x[:, DC:].rearrange("p (t h) -> p t h", h=H),
                                               nexp_a.unsqueeze(1).to_broadcast([P, TILES + 1, H]), ALU.mult))
            nc.vector.tensor_tensor(g_, g_, valid, ALU.mult).then_inc(s_g, 1)
            steps.link(nc.vector.tensor_scalar(beta, beta, 0.5, 0.5, ALU.mult, ALU.add))
            steps.link(nc.vector.tensor_tensor(beta, beta, valid, ALU.mult))
            for j in range(8):
                convolve(dve, steps, j, j, j, xc[:, j, :]).then_inc(s_conv, 1)
            for j in range(8):
                dve.wait_ge(s_gateread, j + 1)
                nc.vector.scalar_tensor_tensor(t_i[:, j, :], t_i[:, j, :], 1.0, xc[:, j, :], ALU.add, ALU.mult)\
                    .then_inc(s_gated, 1)

            def convolved_tile(steps, u, j):
                if j >= 2 or not isinstance(u, int):
                    dve.wait_ge(s_fin, u * 8 + ((j - 1 if j >= 2 else 0) - 16))
                convolve(dve, steps, u * 8 + j, u * 8 + (j - 8), j, conv[j % 2]).then_inc(s_conv, 1)

            for j in range(8):
                convolved_tile(steps, 2, j)
                if j == 1:
                    dve.wait_ge(s_sq, 1)
                    nc.vector.scalar_tensor_tensor(mult, xc, 1.0, mult, ALU.add, ALU.mult).then_inc(s_mult2, 1)
                if j == 3:
                    dve.wait_ge(s_mult, 1)
                    nc.vector.memset(mult[:, :, 0:1], 0.5).then_inc(s_first, 1)
                if j >= 4:
                    for c in (2 * j - 8, 2 * j - 7):
                        dve.wait_ge(s_scaled, c + 1)
                        nc.vector.tensor_tensor_scan(out=mult[:, c, 0:S0], data0=t_r[:, c, 0:S0],
                                                     data1=t_i[:, c, 0:S0], initial=0.0, op0=ALU.mult, op1=ALU.add)
                        nc.vector.tensor_tensor_scan(out=mult[:, c, S0:TW], data0=t_r[:, c, S0:TW],
                                                     data1=t_i[:, c, S0:TW], initial=PR("h0")[:, c:c + 1],
                                                     op0=ALU.mult, op1=ALU.add).then_inc(s_lru, 1)
            dve.wait_ge(s_lru, 8)
            nc.vector.tensor_copy(last_h[:, :, 0:1], mult[:, :, SEQ - 1:SEQ])
            nc.vector.tensor_copy(last_h[:, :, 1:2], mult[:, :, S0 + DEC - 1:S0 + DEC]).then_inc(s_last, 1)
            base = steps.n
            with dve.Fori(3, 5) as u:
                inner = Steps(dve, s_v, u * (8 * LINKS) + (base - 24 * LINKS))
                for j in range(8):
                    convolved_tile(inner, u, j)
                assert inner.n == 8 * LINKS


def token_tiles():
    return [(t, t * P, P, LEVELS, 0) for t in range(TILES)] + [(TILES, S0, DEC, 5, 1)]


def delta_rule_stage(nc, mem, dram):
    with ExitStack() as ctx:
        def sem(name):
            return ctx.enter_context(nc.semaphore(name))

        C, PR = mem.consts, mem.params
        carve = mem.carve
        work = mem.sbuf(ctx, "delta_work", 22 * H * P)
        qkv = carve(mem.qkv, 0, NQ, TW)
        zt = carve(mem.zt, 0, DC, TW)
        state = [carve(mem.states, H * P * i, H, P) for i in range(2)]
        n_d = (TILES + 1) * H
        beta, g_, gsum, gneg, eg, egl, egd, gtot = (carve(mem.decay, n_d * i, TILES + 1, H) for i in range(8))
        squares = carve(work, 0, 2 * H, P)
        rg, decay, lower_t, x_inv, joined, rhs, new, o_state, o, o_sq = (
            carve(work, 2 * H * P + H * P * i, H, P) for i in range(10))
        attn_t, x_inv_t, v_beta, k_dec = (
            [carve(work, 12 * H * P + H * P * (2 * i + parity), H, P) for parity in range(2)] for i in range(4))
        row_mask = [carve(work, 20 * H * P + H * P * i, H, P) for i in range(2)]
        small = ctx.enter_context(nc.sbuf_tensor("factors", [P, 256], F32))
        norm_a, norm_b, norm_c = (carve(small, 16 * i, 2 * H) for i in range(3))
        o_sum, o_a, o_b, o_rs = (carve(small, 48 + 8 * i, H) for i in range(4))
        norm, row_f, ks_f, kd_f, qs_f = (
            [carve(small, 80 + 48 * parity + at, n) for parity in range(2)]
            for at, n in ((0, 2 * H), (16, H), (24, H), (32, H), (40, H)))
        ident_b = ctx.enter_context(nc.sbuf_tensor("ident_bf16", [P, P], BF16))
        future_b = ctx.enter_context(nc.sbuf_tensor("future_bf16", [P, 4 * P], BF16))

        s_state, s_setup, s_egd = sem("state_loaded"), sem("masks_ready"), sem("decay_to_end_ready")
        s_sq, s_ss, s_ssr, s_root = sem("squares_ready"), sem("square_sums_ready"), sem("square_sums_read"), sem("roots_ready")
        s_mask = sem("masks_scaled")
        s_osq, s_rms, s_oroot, s_ors = sem("o_squared"), sem("o_square_sums_ready"), sem("o_root_ready"), sem("o_factor_ready")
        s_vt, s_kt = sem("v_transposed"), sem("k_transposed")
        s_vb, s_kd = sem("v_beta_ready"), sem("k_decayed_ready")
        s_norm, s_rg, s_grow, s_et = sem("factors_ready"), sem("decay_rows_ready"), sem("decay_sums_ready"), sem("decay_ready")
        s_kk, s_kq, s_u, s_at = sem("kk_ready"), sem("kq_ready"), sem("lower_ready"), sem("attention_ready")
        s_pa, s_p, s_px, s_x = sem("join_product"), sem("join_ready"), sem("join_applied"), sem("inverse_ready")
        s_ks, s_r, s_vn, s_vns = sem("k_state_ready"), sem("rhs_ready"), sem("new_values"), sem("new_values_read")
        s_os, s_osr, s_oa, s_o = sem("q_state_ready"), sem("q_state_read"), sem("attended"), sem("o_ready")
        s_su, s_s = sem("state_update"), sem("state_ready")
        s_on, s_ot, s_otr = sem("o_normed"), sem("o_transposed"), sem("o_gated")
        s_v = sem("delta_vector_steps")
        s_out = sem("states_stored")
        block = ctx.enter_context(nc.Block())
        groups = [(g, slice(4 * g, 4 * g + 4)) for g in range(2)]

        def in_bank(b, rows, width):
            return mem.bank[b][0:rows, :].rearrange("p (h i) -> p h i", h=4)[:, :, 0:width]

        def inverse_steps(t, level, g):
            return 2 * LEVELS * t + 2 * level + g + 1

        def mask_steps(t, level):
            return LEVELS * t + level + 1

        @block.sync
        def _(sp):
            sp.dma_start(state[1], dram["state"]).then_inc(s_state, 16)
            sp.wait_ge(s_s, 2 * TILES)
            sp.dma_start(dram["states"][0], state[0]).then_inc(s_out, 16)
            sp.wait_ge(s_s, 2 * TILES + 2)
            sp.dma_start(dram["states"][1], state[1]).then_inc(s_out, 16)
            sp.wait_ge(s_out, 32)

        tiles = token_tiles()

        @block.tensor
        def _(pe):
            def sums(t):
                w = tiles[t][2]
                pe.wait_ge(s_sq, t + 1)
                if t >= 2:
                    pe.wait_ge(s_s, 2 * (t - 1))
                for j in range(2 * H):
                    last = nc.tensor.matmul(mem.bank[6][0:w, j:j + 1], squares[:, j, 0:w], C("ones")[:, 0:1],
                                            start=True, stop=True)
                last.then_inc(s_ss, 1)

            def columns(t):
                _, at, w, _, _ = tiles[t]
                return [qkv[:, 8 * i:8 * i + 8, at:at + w] for i in range(3)]

            def transposed(t, which, first_bank, done):
                w = tiles[t][2]
                if t:
                    pe.wait_ge(s_x, inverse_steps(t - 1, tiles[t - 1][3] - 1, 1))
                for g, hs in groups:
                    for h in range(4):
                        last = nc.tensor.transpose(in_bank(first_bank + g, w, P)[:, h, :],
                                                   columns(t)[which][:, 4 * g + h, :], C("ident"))
                    last.then_inc(done, 1)

            def decay_rows(t):
                w = tiles[t][2]
                pe.wait_ge(s_rg, t + 1)
                for g, hs in groups:
                    nc.tensor.matmul(in_bank(4 + g, w, w), C("ones")[0:w, 0:w], rg[0:w, hs, 0:w], start=True, stop=False)
                    nc.tensor.matmul(in_bank(4 + g, w, w), ident_b[0:w, 0:w],
                                     future_b[0:w, :].rearrange("p (h i) -> p h i", h=4)[:, :, 0:w],
                                     start=False, stop=True).then_inc(s_grow, 1)

            def with_k(t, which, first_bank, read, done):
                w = tiles[t][2]
                k, other = columns(t)[1], columns(t)[which]
                for g, hs in groups:
                    pe.wait_ge(read, 2 * t + g + 1)
                    for h in range(4):
                        last = nc.tensor.matmul(in_bank(first_bank + g, w, w)[:, h, :], k[:, 4 * g + h, :],
                                                other[:, 4 * g + h, :], start=True, stop=True)
                    last.then_inc(done, 1)

            def join(t, level):
                _, _, w, levels, _ = tiles[t]
                xt = x_inv_t[t % 2]
                for g, hs in groups:
                    if level:
                        pe.wait_ge(s_x, inverse_steps(t, level - 1, g))
                    else:
                        pe.wait_ge(s_u, 2 * t + g + 1)
                        pe.wait_ge(s_et, 2 * t + g + 1)
                    for h in range(4):
                        out, left = in_bank(4 + g, w, w)[:, h, :], lower_t[0:w, 4 * g + h, 0:w]
                        if level:
                            last = nc.tensor.matmul(out, left, x_inv[0:w, 4 * g + h, 0:w], start=True, stop=True)
                        else:
                            last = nc.tensor.transpose(out, left, C("ident")[0:w, 0:w])
                    last.then_inc(s_pa, 1)
                for g, hs in groups:
                    pe.wait_ge(s_p, inverse_steps(t, level, g))
                    if not level:
                        pe.wait_ge(s_at, 2 * t + g + 1)
                    for h in range(4):
                        if 0 < level < levels - 1:
                            nc.tensor.matmul(in_bank(g, w, w)[:, h, :], xt[0:w, 4 * g + h, 0:w],
                                             joined[0:w, 4 * g + h, 0:w], start=True, stop=True)
                        out, left = in_bank(2 + g, w, w)[:, h, :], joined[0:w, 4 * g + h, 0:w]
                        if level:
                            last = nc.tensor.matmul(out, left, xt[0:w, 4 * g + h, 0:w], start=True, stop=True)
                        else:
                            last = nc.tensor.transpose(out, left, C("ident")[0:w, 0:w])
                    last.then_inc(s_px, 1)

            def on_state(t, which, done, read=None):
                _, _, w, _, stream = tiles[t]
                left = columns(t)[which]
                if stream:
                    pe.wait_ge(s_state, 16)
                elif t:
                    pe.wait_ge(s_s, 2 * t)
                for g, hs in groups:
                    if read:
                        pe.wait_ge(read, 2 * t + g + 1)
                    for h in range(4):
                        last = nc.tensor.matmul(in_bank(6 + g, w, P)[:, h, :], left[:, 4 * g + h, :],
                                                state[stream][:, 4 * g + h, :], start=True, stop=True)
                    last.then_inc(done, 1)

            def k_state(t):
                pe.wait_ge(s_ssr, t + 1)
                if t:
                    pe.wait_ge(s_otr, 2 * t)
                if t + 1 <= TILES:
                    pe.wait_ge(s_ssr, t + 2)
                on_state(t, 1, s_ks)

            def new_values(t):
                w = tiles[t][2]
                for g, hs in groups:
                    pe.wait_ge(s_r, 2 * t + g + 1)
                    for h in range(4):
                        last = nc.tensor.matmul(in_bank(6 + g, w, P)[:, h, :], x_inv_t[t % 2][0:w, 4 * g + h, 0:w],
                                                rhs[0:w, 4 * g + h, :], start=True, stop=True)
                    last.then_inc(s_vn, 1)

            def q_state(t):
                on_state(t, 0, s_os, s_vns)

            def attend(t):
                w = tiles[t][2]
                for g, hs in groups:
                    pe.wait_ge(s_osr, 2 * t + g + 1)
                    for h in range(4):
                        last = nc.tensor.matmul(in_bank(6 + g, w, P)[:, h, :], attn_t[t % 2][0:w, 4 * g + h, 0:w],
                                                new[0:w, 4 * g + h, :], start=True, stop=True)
                    last.then_inc(s_oa, 1)

            def update(t):
                w = tiles[t][2]
                for g, hs in groups:
                    pe.wait_ge(s_o, 2 * t + g + 1)
                    for h in range(4):
                        last = nc.tensor.matmul(in_bank(6 + g, P, P)[:, h, :], k_dec[t % 2][0:w, 4 * g + h, :],
                                                new[0:w, 4 * g + h, :], start=True, stop=True)
                    last.then_inc(s_su, 1)

            def transpose_o(t):
                w = tiles[t][2]
                pe.wait_ge(s_on, t + 1)
                if t + 2 <= TILES:
                    pe.wait_ge(s_ssr, t + 3)
                for g, hs in groups:
                    pe.wait_ge(s_s, 2 * t + g + 1)
                    for h in range(4):
                        last = nc.tensor.transpose(in_bank(6 + g, P, w)[:, h, :], o[0:w, 4 * g + h, :],
                                                   C("ident")[0:w, 0:w])
                    last.then_inc(s_ot, 1)

            pe.wait_ge(s_setup, 1)
            sums(0)
            for t in range(TILES + 1):
                transposed(t, 2, 0, s_vt)
                if t:
                    k_state(t - 1)
                transposed(t, 1, 2, s_kt)
                decay_rows(t)
                if t:
                    new_values(t - 1)
                with_k(t, 1, 0, s_vb, s_kk)
                if t:
                    q_state(t - 1)
                with_k(t, 0, 2, s_kd, s_kq)
                if t:
                    attend(t - 1)
                levels = tiles[t][3]
                for level in range(levels):
                    join(t, level)
                    if t and level == 1:
                        update(t - 1)
                    if t < TILES and level == 3:
                        pe.wait_ge(s_ssr, t + 1)
                        sums(t + 1)
                    if t and level == levels - 1:
                        transpose_o(t - 1)
            for part in (k_state, new_values, q_state, attend, update, transpose_o):
                part(TILES)

        @block.scalar
        def _(act):
            def square(t):
                _, at, w, _, _ = tiles[t]
                if t:
                    act.wait_ge(s_ss, t)
                nc.scalar.activation(squares[:, :, 0:w], qkv[:, 0:2 * H, at:at + w], ACT.Square).then_inc(s_sq, 1)

            def root(t):
                w = tiles[t][2]
                act.wait_ge(s_ssr, t + 1)
                nc.scalar.activation(norm_b[0:w], norm_a[0:w], ACT.Sqrt).then_inc(s_root, 1)

            def v_and_k(t):
                w = tiles[t][2]
                for g, hs in groups:
                    act.wait_ge(s_vt, 2 * t + g + 1)
                    for h in range(4):
                        last = nc.scalar.activation(v_beta[t % 2][0:w, 4 * g + h, :], in_bank(g, w, P)[:, h, :], ACT.Copy,
                                                    scale=beta[0:w, t, 4 * g + h:4 * g + h + 1])
                    last.then_inc(s_vb, 1)
                act.wait_ge(s_norm, t + 1)
                for g, hs in groups:
                    act.wait_ge(s_kt, 2 * t + g + 1)
                    for h in range(4):
                        last = nc.scalar.activation(k_dec[t % 2][0:w, 4 * g + h, :], in_bank(2 + g, w, P)[:, h, :],
                                                    ACT.Copy, scale=kd_f[t % 2][0:w, 4 * g + h:4 * g + h + 1])
                    last.then_inc(s_kd, 1)

            def decays(t):
                w = tiles[t][2]
                for g, hs in groups:
                    act.wait_ge(s_grow, 2 * t + g + 1)
                    if t:
                        act.wait_ge(s_at, 2 * t)
                    for h in range(4):
                        last = nc.scalar.activation(decay[0:w, 4 * g + h, 0:w], in_bank(4 + g, w, w)[:, h, :], ACT.Exp,
                                                    bias=gneg[0:w, t, 4 * g + h:4 * g + h + 1])
                    last.then_inc(s_et, 1)

            def from_state(t):
                w = tiles[t][2]
                for g, hs in groups:
                    act.wait_ge(s_vn, 2 * t + g + 1)
                    if t:
                        act.wait_ge(s_su, 2 * t)
                    nc.scalar.activation(new[0:w, hs, :], in_bank(6 + g, w, P), ACT.Copy).then_inc(s_vns, 1)
                for g, hs in groups:
                    act.wait_ge(s_os, 2 * t + g + 1)
                    if t:
                        act.wait_ge(s_o, 2 * t)
                    for h in range(4):
                        last = nc.scalar.activation(o_state[0:w, 4 * g + h, :], in_bank(6 + g, w, P)[:, h, :], ACT.Copy,
                                                    scale=qs_f[t % 2][0:w, 4 * g + h:4 * g + h + 1])
                    last.then_inc(s_osr, 1)

            def o_root(t):
                w = tiles[t][2]
                act.wait_ge(s_rms, t + 1)
                nc.scalar.activation(o_b[0:w], o_a[0:w], ACT.Sqrt).then_inc(s_oroot, 1)

            act.wait_ge(s_setup, 1)
            nc.scalar.activation(egd, egd, ACT.Exp).then_inc(s_egd, 1)
            square(0)
            root(0)
            for t in range(TILES + 1):
                v_and_k(t)
                decays(t)
                if t:
                    from_state(t - 1)
                if t < TILES:
                    square(t + 1)
                if t:
                    o_root(t - 1)
                if t < TILES:
                    root(t + 1)
            from_state(TILES)
            o_root(TILES)

        @block.gpsimd
        def _(pool):
            def scale_masks(t, *of):
                _, _, w, levels, _ = tiles[t]
                pool.wait_ge(s_norm, t + 1)
                for level in of:
                    if level >= levels:
                        break
                    if mask_steps(t, level) > 2:
                        pool.wait_ge(s_p, inverse_steps(t, level - 2, 1) if level >= 2 else
                                     inverse_steps(t - 1, tiles[t - 1][3] - (2 - level), 1))
                    mask = C("masks")[0:w, P * level:P * level + w]
                    pool.tensor_tensor(row_mask[mask_steps(t, level) % 2][0:w, :, 0:w], mask.unsqueeze(1).to_broadcast([w, H, w]),
                                       row_f[t % 2][0:w].unsqueeze(2).to_broadcast([w, H, w]), ALU.mult)\
                        .then_inc(s_mask, 1)

            def square_o(t):
                w = tiles[t][2]
                pool.wait_ge(s_o, 2 * t + 2)
                pool.tensor_tensor(o_sq[0:w], o[0:w], o[0:w], ALU.mult).then_inc(s_osq, 1)

            def scale_o(t):
                w = tiles[t][2]
                pool.wait_ge(s_ors, t + 1)
                pool.tensor_tensor(o[0:w], o[0:w], o_rs[0:w].unsqueeze(2).to_broadcast([w, H, P]), ALU.mult)\
                    .then_inc(s_on, 1)

            def log_decays(t):
                w = tiles[t][2]
                if t:
                    pool.wait_ge(s_grow, 2 * t)
                pool.tensor_tensor(rg[0:w, :, 0:w], C("tri")[0:w, 0:w].unsqueeze(1).to_broadcast([w, H, w]),
                                   g_[0:w, t, :].unsqueeze(2).to_broadcast([w, H, w]), ALU.mult).then_inc(s_rg, 1)

            log_decays(0)
            for t in range(TILES + 1):
                scale_masks(t, 0, 1)
                if t:
                    square_o(t - 1)
                scale_masks(t, 2, 3, 4, 5)
                if t:
                    scale_o(t - 1)
                scale_masks(t, 6)
                if t < TILES:
                    log_decays(t + 1)
            square_o(TILES)
            scale_o(TILES)

        @block.vector
        def _(dve):
            steps = Steps(dve, s_v)

            def read_sums(t):
                w = tiles[t][2]
                dve.wait_ge(s_ss, t + 1)
                nc.vector.tensor_scalar(norm_a[0:w], mem.bank[6][0:w, 0:2 * H], 1e-6, None, ALU.add).then_inc(s_ssr, 1)

            def factors(t):
                w = tiles[t][2]
                i = t % 2
                dve.wait_ge(s_root, t + 1)
                inverse_root(nc, steps, norm[i][0:w], norm_a[0:w], norm_b[0:w], norm_c[0:w])
                rk, rq = norm[i][0:w, H:2 * H], norm[i][0:w, 0:H]
                steps.done(nc.vector.tensor_scalar(rq, rq, P ** -0.5, None, ALU.mult))
                steps.done(nc.vector.tensor_tensor(row_f[i][0:w], rk, beta[0:w, t, :], ALU.mult))
                steps.done(nc.vector.tensor_tensor(kd_f[i][0:w], rk, egd[0:w, t, :], ALU.mult)).wait()
                steps.link(nc.vector.tensor_tensor(ks_f[i][0:w], row_f[i][0:w], eg[0:w, t, :], ALU.mult))
                nc.vector.tensor_scalar(ks_f[i][0:w], ks_f[i][0:w], -1.0, None, ALU.mult)
                nc.vector.tensor_tensor(qs_f[i][0:w], rq, eg[0:w, t, :], ALU.mult).then_inc(s_norm, 1)

            def k_state_read(t):
                w = tiles[t][2]
                for g, hs in groups:
                    dve.wait_ge(s_ks, 2 * t + g + 1)
                    dve.wait_ge(s_vb, 2 * t + g + 1)
                    dve.wait_ge(s_norm, t + 1)
                    for h in range(4):
                        n = 4 * g + h
                        last = nc.vector.scalar_tensor_tensor(rhs[0:w, n, :], in_bank(6 + g, w, P)[:, h, :],
                                                              ks_f[t % 2][0:w, n:n + 1], v_beta[t % 2][0:w, n, :],
                                                              ALU.mult, ALU.add)
                    last.then_inc(s_r, 1)

            def decayed(t, first_bank, out, ready, done):
                w = tiles[t][2]
                for g, hs in groups:
                    dve.wait_ge(ready, 2 * t + g + 1)
                    dve.wait_ge(s_et, 2 * t + g + 1)
                    for h in range(4):
                        n = 4 * g + h
                        last = nc.vector.scalar_tensor_tensor(
                            out[0:w, n, 0:w], in_bank(first_bank + g, w, w)[:, h, :],
                            norm[t % 2][0:w, H + n:H + n + 1], decay[0:w, n, 0:w], ALU.mult, ALU.mult)
                    last.then_inc(done, 1)

            def while_joining(t, level):
                if t and level < 2:
                    output(t - 1, level)
                if t and level in (2, 3):
                    update(t - 1, level - 2)
                if t and level == 4:
                    o_mean_square(t - 1)
                if t < TILES and level == 4:
                    read_sums(t + 1)
                if t and level == 5:
                    o_factor(t - 1)
                if t < TILES and level == 6:
                    factors(t + 1)

            def join(t, level):
                _, _, w, levels, _ = tiles[t]
                xt = x_inv_t[t % 2]
                eye = C("ident")[0:w, 0:w].unsqueeze(1).to_broadcast([w, 4, w])
                dve.wait_ge(s_mask, mask_steps(t, level))
                for g, hs in groups:
                    dve.wait_ge(s_pa, inverse_steps(t, level, g))
                    nc.vector.tensor_tensor(joined[0:w, hs, 0:w], in_bank(4 + g, w, w),
                                            row_mask[mask_steps(t, level) % 2][0:w, hs, 0:w], ALU.mult).then_inc(s_p, 1)
                while_joining(t, level)
                for g, hs in groups:
                    if not level:
                        dve.wait_ge(s_p, inverse_steps(t, level, g))
                        nc.vector.tensor_tensor(x_inv[0:w, hs, 0:w], eye, joined[0:w, hs, 0:w], ALU.subtract)
                    dve.wait_ge(s_px, inverse_steps(t, level, g))
                    if 0 < level < levels - 1:
                        nc.vector.tensor_tensor(x_inv[0:w, hs, 0:w], x_inv[0:w, hs, 0:w], in_bank(g, w, w),
                                                ALU.subtract)
                    nc.vector.tensor_tensor(xt[0:w, hs, 0:w], xt[0:w, hs, 0:w] if level else eye,
                                            in_bank(2 + g, w, w), ALU.subtract).then_inc(s_x, 1)

            def output(t, g):
                w = tiles[t][2]
                dve.wait_ge(s_oa, 2 * t + g + 1)
                dve.wait_ge(s_osr, 2 * t + g + 1)
                if t:
                    dve.wait_ge(s_ot, 2 * t)
                for h in range(4):
                    n = 4 * g + h
                    last = nc.vector.scalar_tensor_tensor(o[0:w, n, :], in_bank(6 + g, w, P)[:, h, :],
                                                          norm[t % 2][0:w, n:n + 1], o_state[0:w, n, :],
                                                          ALU.mult, ALU.add)
                last.then_inc(s_o, 1)

            def update(t, g):
                stream = tiles[t][4]
                dve.wait_ge(s_su, 2 * t + g + 1)
                for h in range(4):
                    n = 4 * g + h
                    last = nc.vector.scalar_tensor_tensor(state[stream][:, n, :], state[stream][:, n, :],
                                                          egl[:, t, n:n + 1], in_bank(6 + g, P, P)[:, h, :],
                                                          ALU.mult, ALU.add)
                last.then_inc(s_s, 1)

            def o_mean_square(t):
                w = tiles[t][2]
                dve.wait_ge(s_osq, t + 1)
                steps.link(nc.vector.tensor_reduce(o_sum[0:w], o_sq[0:w], AX.X, ALU.add))
                nc.vector.tensor_scalar(o_a[0:w], o_sum[0:w], 1.0 / P, RMS_EPS, ALU.mult, ALU.add).then_inc(s_rms, 1)

            def o_factor(t):
                w = tiles[t][2]
                dve.wait_ge(s_oroot, t + 1)
                inverse_root(nc, steps, o_rs[0:w], o_a[0:w], o_b[0:w], o_sum[0:w])
                dve.sem_inc(s_ors, 1)

            def gate(t):
                _, at, w, _, _ = tiles[t]
                for g, hs in groups:
                    dve.wait_ge(s_ot, 2 * t + g + 1)
                    nc.vector.scalar_tensor_tensor(zt[:, hs, at:at + w], in_bank(6 + g, P, w), PR("norm_w"),
                                                   zt[:, hs, at:at + w], ALU.mult, ALU.mult).then_inc(s_otr, 1)

            nc.vector.memset(state[0], 0.0)
            nc.vector.tensor_copy(ident_b[:, :], C("ident"))
            nc.vector.tensor_copy(future_b[:, :].rearrange("p (h i) -> p h i", h=4),
                                  C("future").unsqueeze(1).to_broadcast([P, 4, P]))
            nc.vector.tensor_tensor(egd, gtot, gsum, ALU.subtract).then_inc(s_setup, 1)
            dve.wait_ge(s_egd, 1)
            read_sums(0)
            factors(0)
            for t in range(TILES + 1):
                if t:
                    k_state_read(t - 1)
                decayed(t, 0, lower_t, s_kk, s_u)
                decayed(t, 2, attn_t[t % 2], s_kq, s_at)
                levels = tiles[t][3]
                for level in range(levels):
                    join(t, level)
                if t and levels < 6:
                    o_factor(t - 1)
                if t:
                    gate(t - 1)
            t = TILES
            k_state_read(t)
            for part in (output, update):
                for g in range(2):
                    part(t, g)
            for part in (o_mean_square, o_factor, gate):
                part(t)


class Routing:

    def __init__(self, mem):
        at = 0

        def take(*dims):
            nonlocal at
            view = mem.carve(mem.states, at, *dims)
            at += int(np.prod(dims))
            return view

        self.chosen = mem.carve(mem.chosen, 0, TILES + 1, NE)
        self.dest = take(TILES + 1, NE)
        self.row = mem.carve(mem.row, 0, TILES + 1, NE, 2)
        self.weight = take(TILES + 1, TOPK)
        self.block_expert = take(P).bitcast(I32)
        self.n_blocks = take(2).bitcast(I32)
        self.count, self.n, self.upto, self.first = (take(NE) for _ in range(4))
        self.over = take(NE, TILES + 1)
        self.block_col = take(2)


def layer_norm(nc, steps, x, stats, gain, bias, out):
    for i in range(2):
        last = nc.vector.bn_stats(stats[:, 6 * i:6 * i + 6], x[:, 512 * i:512 * i + 512])
    steps.link(last)
    steps.link(nc.vector.bn_aggr(stats[:, 12:14], stats[:, 0:12]))
    steps.link(nc.vector.tensor_scalar(stats[:, 14:15], stats[:, 13:14], LN_EPS, None, ALU.add))
    rsqrt(nc, steps, stats[:, 15:16], stats[:, 14:15], (stats[:, 16:17], stats[:, 17:18]))
    steps.link(nc.vector.tensor_scalar(x, x, stats[:, 12:13], stats[:, 15:16], ALU.subtract, ALU.mult))
    steps.link(nc.vector.tensor_tensor(x, x, gain, ALU.mult))
    return nc.vector.tensor_tensor(out, x, bias, ALU.add)


W_OUT_PARTS = (0, 1, 4, 9, 2 * DC)


def mixing_stage(nc, mem, dram, route):
    with ExitStack() as ctx:
        def sem(name):
            return ctx.enter_context(nc.semaphore(name))

        C, PR = mem.consts, mem.params
        carve = mem.carve
        zt = carve(mem.zt, 0, DC, TW)
        lru = carve(mem.lru, 0, DC, TW)
        w_out = carve(mem.sbuf(ctx, "w_out", 2 * DC * D), 0, 2 * DC, D)
        work = mem.sbuf(ctx, "mixing_work", 20480)
        at = 0

        def take(*dims):
            nonlocal at
            view = carve(work, at, *dims)
            at += int(np.prod(dims))
            return view

        w_gu, w_dn, w_router, ln = take(DC, 2 * FF), take(FC, D), take(DC, NE), take(2, D)
        x = [take(D) for _ in range(2)]
        x1, h1_t = take(D), take(DC, P)
        h1 = [take(D) for _ in range(2)]
        acc = [take(D) for _ in range(2)]
        act_g, hidden, hidden_t = take(FF), take(FF), take(FC, P)
        stats, scores, biased, masked = take(32), take(NE), take(NE), take(NE)
        best, group, group_best, group_f = take(NG, 8), take(NG), take(NG), take(NG)
        group_i, top_i = take(8).bitcast(U32), take(8).bitcast(U32)
        group_eq, group_on, penalty, top_v, total = take(NG, TOPG), take(NG), take(NG), take(8), take(2)
        expert, which = take(TOPK), take(NE)
        hot, hot_s = take(TOPK, NE), take(TOPK, NE)
        assert at <= 20480

        before_b, ones_b = (ctx.enter_context(nc.sbuf_tensor(n, [P, P], BF16)) for n in ("before_bf16", "ones_bf16"))

        s_w = [sem(f"w_out_loaded_{i}") for i in range(4)]
        s_sh, s_ln = sem("shared_loaded"), sem("norm_loaded")
        s_x = [sem("x_loaded_0"), sem("x_loaded_1")]
        s_mix, s_x1, s_h1, s_ht, s_htr = sem("mixed"), sem("mix_read"), sem("h1_ready"), sem("h1_transposed"), sem("h1_t_ready")
        s_sc, s_gu, s_g, s_hid = sem("scores_read"), sem("routed_then_shared_up"), sem("shared_gate_ready"), sem("shared_hidden")
        s_hdt, s_hdr, s_dn, s_acc = sem("hidden_transposed"), sem("hidden_t_ready"), sem("shared_down"), sem("residual_ready")
        s_h1out = [sem("h1_stored_0"), sem("h1_stored_1")]
        s_accout = [sem("residual_stored_0"), sem("residual_stored_1")]
        s_sel, s_rank, s_eb, s_ebt, s_v = sem("chosen_ready"), sem("ranks_ready"), sem("block_experts"), sem("block_experts_row"), sem("mix_vector_steps")
        block = ctx.enter_context(nc.Block())
        tiles = token_tiles()
        h1_rows, acc_rows = dram["h1"], dram["residual"]

        @block.sync
        def _(sp):
            for i, (a, b) in enumerate(zip(W_OUT_PARTS, W_OUT_PARTS[1:])):
                sp.dma_start(w_out[:, a:b, :], dram["w_out"][:, a:b, :]).then_inc(s_w[i], 16)
            sp.dma_start(x[0], dram["x_rows"][0:P, :]).then_inc(s_x[0], 16)
            sp.dma_start(ln, dram["norms"][:, 0:2, :]).then_inc(s_ln, 16)
            sp.dma_start(x[1], dram["x_rows"][P:2 * P, :]).then_inc(s_x[1], 16)
            n_gu = DC * 2 * FF
            sp.dma_start(w_gu, dram["w_sh"][:, 0:n_gu].rearrange("p (k n) -> p k n", k=DC)).then_inc(s_sh, 16)
            sp.dma_start(w_dn, dram["w_sh"][:, n_gu:].rearrange("p (k n) -> p k n", k=FC)).then_inc(s_sh, 16)
            sp.dma_start(w_router, dram["w_router"]).then_inc(s_sh, 16)
            for t, _, w, _, _ in tiles:
                rows = slice(P * t, P * t + w)
                sp.wait_ge(s_h1, t + 1)
                sp.dma_start(h1_rows[rows, :], h1[t % 2][0:w]).then_inc(s_h1out[t % 2], 16)
                if t + 2 <= TILES:
                    w2 = tiles[t + 2][2]
                    sp.dma_start(x[t % 2][0:w2], dram["x_rows"][P * (t + 2):P * (t + 2) + w2, :]).then_inc(s_x[t % 2], 16)
                sp.wait_ge(s_acc, t + 1)
                sp.dma_start(acc_rows[rows, :], acc[t % 2][0:w]).then_inc(s_accout[t % 2], 16)
            for i, n in ((0, 3), (1, 2)):
                sp.wait_ge(s_h1out[i], 16 * n)
                sp.wait_ge(s_accout[i], 16 * n)

        @block.tensor
        def _(pe):
            def mix(t, chunks=range(2 * DC)):
                if t > TILES:
                    return
                _, at, w, _, _ = tiles[t]
                if t and chunks[0] == 0:
                    pe.wait_ge(s_x1, t)
                for f in chunks:
                    if t == 0 and f in W_OUT_PARTS:
                        pe.wait_ge(s_w[W_OUT_PARTS.index(f)], 16)
                    half = (zt if f < DC else lru)[:, f % DC, at:at + w]
                    for n in range(2):
                        last = nc.tensor.matmul(mem.bank[n][0:w, :], half, w_out[:, f, 512 * n:512 * n + 512],
                                                start=(f == 0), stop=(f == 2 * DC - 1))
                if chunks[-1] == 2 * DC - 1:
                    last.then_inc(s_mix, 1)

            mix(0)
            mix(1)
            for t, at, w, _, _ in tiles:
                pe.wait_ge(s_h1, t + 1)
                for k in range(DC):
                    last = nc.tensor.transpose(mem.bank[2 + k // 4][:, P * (k % 4):P * (k % 4) + w],
                                               h1[t % 2][0:w, P * k:P * k + P], C("ident")[0:w, 0:w])
                last.then_inc(s_ht, 1)
                mix(t + 2, range(0, 2))
                if t == 0:
                    pe.wait_ge(s_sh, 48)
                pe.wait_ge(s_htr, t + 1)
                if t:
                    pe.wait_ge(s_hdr, t)
                for k in range(DC):
                    last = nc.tensor.matmul(mem.bank[4][0:w, 0:NE], h1_t[:, k, 0:w], w_router[:, k, :],
                                            start=(k == 0), stop=(k == DC - 1))
                last.then_inc(s_gu, 1)
                for k in range(DC):
                    last = nc.tensor.matmul(mem.bank[5][0:w, :], h1_t[:, k, 0:w], w_gu[:, k, :],
                                            start=(k == 0), stop=(k == DC - 1))
                last.then_inc(s_gu, 1)
                mix(t + 2, range(2, 4))
                if t == TILES:
                    pe.wait_ge(s_sel, TILES + 1)
                    for t2 in range(TILES + 1):
                        for other in range(t2 + 1):
                            nc.tensor.matmul(mem.bank[0][:, NE * t2:NE * t2 + NE],
                                             before_b[:, :] if other == t2 else ones_b[:, :],
                                             route.chosen[:, other, :], start=(other == 0), stop=(other == t2))
                    for t2 in range(TILES + 1):
                        last = nc.tensor.matmul(mem.bank[1][:, 0:NE], ones_b[:, :], route.chosen[:, t2, :],
                                                start=(t2 == 0), stop=(t2 == TILES))
                    last.then_inc(s_rank, 1)
                pe.wait_ge(s_hid, t + 1)
                pe.wait_ge(s_sc, t + 1)
                for c in range(FC):
                    last = nc.tensor.transpose(mem.bank[4][:, P * c:P * c + w], hidden[0:w, P * c:P * c + P],
                                               C("ident")[0:w, 0:w])
                last.then_inc(s_hdt, 1)
                mix(t + 2, range(4, 5))
                pe.wait_ge(s_hdr, t + 1)
                if t:
                    pe.wait_ge(s_acc, t)
                for n in range(2):
                    for c in range(FC):
                        last = nc.tensor.matmul(mem.bank[6 + n][0:w, :], hidden_t[:, c, 0:w],
                                                w_dn[:, c, 512 * n:512 * n + 512], start=(c == 0), stop=(c == FC - 1))
                last.then_inc(s_dn, 1)
                mix(t + 2, range(5, 2 * DC))
            pe.wait_ge(s_eb, 1)
            nc.tensor.matmul(mem.bank[2][0:1, 0:P], route.block_col[:, 0:1], C("ident"), start=True, stop=True)\
                .then_inc(s_ebt, 1)

        @block.scalar
        def _(act):
            for t, at, w, _, _ in tiles:
                act.wait_ge(s_ht, t + 1)
                if t:
                    act.wait_ge(s_gu, 2 * t)
                for i in range(2):
                    last = nc.scalar.activation(h1_t[:, 4 * i:4 * i + 4, 0:w],
                                                mem.bank[2 + i][:, :].rearrange("p (k i) -> p k i", k=4)[:, :, 0:w],
                                                ACT.Copy)
                last.then_inc(s_htr, 1)
                act.wait_ge(s_gu, 2 * t + 1)
                if t:
                    act.wait_ge(s_sel, t)
                nc.scalar.activation(scores[0:w], mem.bank[4][0:w, 0:NE], ACT.Tanh, scale=0.5).then_inc(s_sc, 1)
                act.wait_ge(s_gu, 2 * t + 2)
                nc.scalar.activation(act_g[0:w], mem.bank[5][0:w, 0:FF], ACT.Silu).then_inc(s_g, 1)

        @block.vector
        def _(dve):
            steps = Steps(dve, s_v)
            nc.vector.tensor_copy(before_b[:, :], C("before"))
            nc.vector.tensor_copy(ones_b[:, :], C("ones"))
            steps.link(nc.vector.memset(route.chosen, 0.0))
            steps.link(nc.vector.tensor_scalar(route.row.rearrange("p t e c -> p t (e c)"),
                                               C("token_base").unsqueeze(2).to_broadcast([P, TILES + 1, 2 * NE]),
                                               1.0, None, ALU.mult))

            def choose(t, w):
                sc, bi, ma = scores[0:w], biased[0:w], masked[0:w]
                experts = C("experts")[0:w]
                steps.link(nc.vector.tensor_scalar(sc, sc, 0.5, 0.5, ALU.mult, ALU.add))
                steps.link(nc.vector.tensor_tensor(bi, sc, PR("route_b")[0:w], ALU.add))
                for n in range(NG):
                    last = nc.vector.max(best[0:w, n, :], bi[:, GE * n:GE * n + GE])
                steps.link(last)
                steps.link(nc.vector.tensor_tensor(group[0:w], best[0:w, :, 0], best[0:w, :, 1], ALU.add))
                steps.link(nc.vector.max(group_best[0:w], group[0:w]))
                steps.link(nc.vector.max_index(group_i[0:w], group_best[0:w], group[0:w]))
                steps.link(nc.vector.tensor_copy(group_f[0:w], group_i[0:w]))
                steps.link(nc.vector.tensor_tensor(
                    group_eq[0:w], experts[:, 0:NG].unsqueeze(2).to_broadcast([w, NG, TOPG]),
                    group_f[0:w, 0:TOPG].unsqueeze(1).to_broadcast([w, NG, TOPG]), ALU.is_equal))
                steps.link(nc.vector.tensor_reduce(group_on[0:w], group_eq[0:w], AX.X, ALU.add))
                steps.link(nc.vector.tensor_scalar(penalty[0:w], group_on[0:w], -1.0, BIG, ALU.add, ALU.mult))
                by_group = [v.rearrange("p (g e) -> p g e", g=NG) for v in (bi, ma)]
                steps.link(nc.vector.tensor_tensor(by_group[1], by_group[0],
                                                   group_on[0:w].unsqueeze(2).to_broadcast([w, NG, GE]), ALU.mult))
                steps.link(nc.vector.tensor_tensor(by_group[1], by_group[1],
                                                   penalty[0:w].unsqueeze(2).to_broadcast([w, NG, GE]), ALU.add))
                steps.link(nc.vector.max(top_v[0:w], ma))
                steps.link(nc.vector.max_index(top_i[0:w], top_v[0:w], ma))
                steps.link(nc.vector.tensor_copy(expert[0:w], top_i[0:w]))
                steps.link(nc.vector.tensor_tensor(
                    hot[0:w], experts.unsqueeze(1).to_broadcast([w, TOPK, NE]),
                    expert[0:w].unsqueeze(2).to_broadcast([w, TOPK, NE]), ALU.is_equal))
                steps.link(nc.vector.tensor_tensor(hot_s[0:w], hot[0:w], sc.unsqueeze(1).to_broadcast([w, TOPK, NE]),
                                                   ALU.mult))
                steps.link(nc.vector.tensor_reduce(route.weight[0:w, t, :], hot_s[0:w], AX.X, ALU.add))
                steps.link(nc.vector.tensor_reduce(total[0:w, 0:1], route.weight[0:w, t, :], AX.X, ALU.add))
                steps.link(nc.vector.reciprocal(total[0:w, 1:2], total[0:w, 0:1]))
                steps.link(nc.vector.tensor_scalar(route.weight[0:w, t, :], route.weight[0:w, t, :], total[0:w, 1:2],
                                                   SCALE, ALU.mult, ALU.mult))
                steps.link(nc.vector.tensor_tensor(
                    hot_s[0:w], hot[0:w], experts[:, 0:TOPK].unsqueeze(2).to_broadcast([w, TOPK, NE]), ALU.mult))
                steps.link(nc.vector.tensor_reduce(which[0:w], hot_s[0:w].rearrange("p j e -> p e j"), AX.X, ALU.add))
                nc.vector.tensor_copy(route.row[0:w, t, :, 1], which[0:w])
                steps.link(nc.vector.tensor_reduce(ma, hot[0:w].rearrange("p j e -> p e j"), AX.X, ALU.add))
                nc.vector.tensor_copy(route.chosen[0:w, t, :], ma).then_inc(s_sel, 1)

            def normalise(t):
                _, _, w, _, _ = tiles[t]
                dve.wait_ge(s_x[t % 2], 16 * (t // 2 + 1))
                dve.wait_ge(s_mix, t + 1)
                if t:
                    dve.wait_ge(s_h1, t)
                for n in range(2):
                    last = nc.vector.scalar_tensor_tensor(
                        x1[0:w, 512 * n:512 * n + 512], x[t % 2][0:w, 512 * n:512 * n + 512], ALPHA,
                        mem.bank[n][0:w, :], ALU.mult, ALU.add)
                last.then_inc(s_x1, 1)
                dve.wait_ge(s_x1, t + 1)
                if t >= 2:
                    dve.wait_ge(s_h1out[t % 2], 16 * (t // 2))
                layer_norm(nc, steps, x1[0:w], stats[0:w], ln[0:w, 0, :], ln[0:w, 1, :], h1[t % 2][0:w])\
                    .then_inc(s_h1, 1)

            dve.wait_ge(s_ln, 16)
            normalise(0)
            def add_shared(t, w):
                dve.wait_ge(s_dn, t + 1)
                dve.wait_ge(s_h1, t + 1)
                if t >= 2:
                    dve.wait_ge(s_accout[t % 2], 16 * (t // 2))
                for n in range(2):
                    last = nc.vector.scalar_tensor_tensor(
                        acc[t % 2][0:w, 512 * n:512 * n + 512], h1[t % 2][0:w, 512 * n:512 * n + 512], ALPHA,
                        mem.bank[6 + n][0:w, :], ALU.mult, ALU.add)
                last.then_inc(s_acc, 1)

            for t, at, w, _, _ in tiles:
                if t < TILES:
                    normalise(t + 1)
                dve.wait_ge(s_sc, t + 1)
                if t == TILES:
                    choose(t, w)
                dve.wait_ge(s_g, t + 1)
                nc.vector.tensor_tensor(hidden[0:w], act_g[0:w], mem.bank[5][0:w, FF:2 * FF], ALU.mult).then_inc(s_hid, 1)
                dve.wait_ge(s_hdt, t + 1)
                if t:
                    dve.wait_ge(s_dn, t)
                nc.vector.tensor_copy(hidden_t[:, :, 0:w], mem.bank[4][:, 0:FC * P]
                                      .rearrange("p (c i) -> p c i", c=FC)[:, :, 0:w]).then_inc(s_hdr, 1)
                if t < TILES:
                    choose(t, w)
                    add_shared(t, w)
            dve.wait_ge(s_rank, 1)
            r = route
            steps.link(nc.vector.tensor_copy(r.count, mem.bank[1][:, 0:NE]))
            steps.link(nc.vector.tensor_tensor(r.over, r.count.unsqueeze(2).to_broadcast([P, NE, TILES + 1]),
                                               C("over").unsqueeze(1).to_broadcast([P, NE, TILES + 1]), ALU.is_gt))
            steps.link(nc.vector.tensor_reduce(r.n, r.over, AX.X, ALU.add))
            steps.link(nc.vector.tensor_tensor_scan(out=r.upto, data0=C("ones")[:, 0:NE], data1=r.n, initial=0.0,
                                                    op0=ALU.mult, op1=ALU.add))
            steps.link(nc.vector.tensor_tensor(r.first, r.upto, r.n, ALU.subtract))
            steps.link(nc.vector.tensor_scalar(r.first, r.first, float(P), None, ALU.mult))
            steps.link(nc.vector.tensor_tensor(r.dest, mem.bank[0][:, 0:(TILES + 1) * NE]
                                               .rearrange("p (t e) -> p t e", e=NE),
                                               r.first.unsqueeze(1).to_broadcast([P, TILES + 1, NE]), ALU.add))
            steps.link(nc.vector.scalar_tensor_tensor(r.dest, r.dest, 1.0, r.chosen, ALU.add, ALU.mult))
            steps.link(nc.vector.tensor_scalar(r.dest, r.dest, -1.0, None, ALU.add))
            steps.link(nc.vector.tensor_scalar(r.n, r.upto, C("row"), None, ALU.is_le))
            steps.link(nc.vector.tensor_reduce(r.block_col[:, 0:1], r.n, AX.X, ALU.add))
            nc.vector.tensor_scalar(r.block_col[:, 0:1], r.block_col[:, 0:1], NE - 1.0, None, ALU.min).then_inc(s_eb, 1)
            add_shared(TILES, DEC)
            nc.vector.tensor_copy(r.n_blocks[0:1, 0:1], r.upto[0:1, NE - 1:NE])
            dve.wait_ge(s_ebt, 1)
            nc.vector.tensor_copy(r.block_expert[0:1, :], mem.bank[2][0:1, 0:P])


W_GU = DC * 2 * FF
W_EXP = W_GU + FC * D
BY_TENSOR = 4
CHUNK = 8
CHUNKS = -(-(NB2 - 1) // CHUNK)
assert CHUNKS * CHUNK == NB2 - 1
UNIT = 1024
UNITS = W_EXP // UNIT
BY_POOL = (1, 3)
BY_VECTOR = tuple(u for u in range(UNITS) if u not in BY_POOL)


def expert_stage(nc, mem, dram, route):
    with ExitStack() as ctx:
        def sem(name):
            return ctx.enter_context(nc.semaphore(name))

        C = mem.consts
        carve = mem.carve

        def take(name, *dims, dt=F32):
            return carve(mem.sbuf(ctx, name, int(np.prod(dims)), dt), 0, *dims)

        weights = [take(f"weights{i}", W_EXP) for i in range(2)]
        w_hi = [take(f"weights_hi{i}", W_EXP, dt=F32R) for i in range(2)]
        w_lo = [take(f"weights_lo{i}", W_EXP, dt=F32R) for i in range(2)]
        rows = [take(f"rows{i}", D) for i in range(2)]
        x_hi = [take(f"rows_hi{i}", DC, P, dt=F32R) for i in range(2)]
        x_lo = [take(f"rows_lo{i}", DC, P, dt=F32R) for i in range(2)]
        y = [take(f"y{i}", D) for i in range(2)]
        hot = take("slot_match", TILES + 1, P, dt=F32R)
        act_g, hidden = take("gate", FF), take("hidden", FF)
        h_hi, h_lo = (take(n, FC, P, dt=F32R) for n in ("hidden_hi", "hidden_lo"))
        token, row_id = ([ctx.enter_context(nc.sbuf_tensor(f"{n}{i}", [P, 1], U32)) for i in range(2)]
                         for n in ("token", "row_id"))
        row_next = [ctx.enter_context(nc.sbuf_tensor(f"row_next{i}", [P, 1], F32)) for i in range(2)]
        pair_j = ctx.enter_context(nc.sbuf_tensor("which_expert", [P, 1], F32))

        s_w = [[sem(f"expert_{n}_loaded_{i}") for i in range(2)] for n in ("gate_up", "down")]
        s_whi, s_wlo, s_wlo_pool = sem("weights_hi_ready"), sem("weights_lo_ready"), sem("weights_lo_by_pool_ready")
        s_clear = sem("rows_cleared")
        s_hot, s_idp, s_ids, s_row = sem("slot_matches"), sem("ids_summed"), sem("id_steps"), sem("row_ids_ready")
        s_rows = [sem("rows_gathered_0"), sem("rows_gathered_1")]

        s_xt, s_xhi, s_xlo = sem("row_halves_transposed"), sem("row_halves_hi_ready"), sem("row_halves_lo_ready")
        s_gu, s_g, s_hid, s_hdt, s_hhi, s_hlo = (sem("up_ready"), sem("gate_ready"), sem("hidden_ready"),
                                                 sem("hidden_transposed"), sem("hidden_hi_ready"), sem("hidden_lo_ready"))
        s_dn, s_y0, s_y1 = sem("down_ready"), sem("y_left_ready"), sem("y_right_ready")
        s_out = [sem("y_stored_0"), sem("y_stored_1")]
        block = ctx.enter_context(nc.Block())

        def used_blocks(engine, body, with_n=False):
            n = engine.value_load(route.n_blocks[0:1, 0:1], min_val=T * TOPK // P, max_val=2 * NB2)
            if with_n:
                body = functools.partial(body, n=n)
            for i in range(2):
                body(i, i, True)
            with engine.Fori(0, CHUNKS) as chunk:
                with engine.If(chunk * (2 * CHUNK) + 2 < n):
                    with engine.Fori(0, CHUNK) as pair:
                        even = engine.snap(chunk * (2 * CHUNK) + pair * 2 + 2)
                        with engine.If(even < n):
                            body(even, 0, False)
                            with engine.If(even + 1 < n):
                                body(even + 1, 1, False)
                            engine.nop()
                        engine.nop()
                engine.nop()
            return n

        def expert_of(engine, b):
            return engine.value_load(route.block_expert[0:1, bass.ds(b, 1)], min_val=0, max_val=NE - 1)

        def unit(x, u):
            return x[:, UNIT * u:UNIT * u + UNIT]

        @block.sync
        def _(sp):
            def last_split(b):
                sp.wait_ge(s_wlo, (b - 1) * len(BY_VECTOR))
                sp.sem_inc(mem.passed, 1)
                sp.wait_ge(s_wlo_pool, (b - 1) * len(BY_POOL))
                sp.sem_inc(mem.passed, 1)

            def load(b, i):
                e = expert_of(sp, b)
                for part, (at, n) in enumerate(((0, W_GU), (W_GU, W_EXP - W_GU))):
                    sp.dma_start(weights[i][:, at:at + n], dram["w_exp"][bass.ds(e, 1), :, at:at + n]
                                 .rearrange("a p n -> (a p) n")).then_inc(s_w[part][i], 16)

            def next_load(b, i, first, n):
                if not (first and i == 0):
                    last_split(b + 1)
                if first:
                    load(b + 1, 1 - i)
                    return
                with sp.If(b + 1 < n):
                    load(b + 1, 1 - i)
                with sp.If(b + 1 >= n):
                    for part in range(2):
                        sp.sem_inc(s_w[part][1 - i], 16)
                sp.nop()

            load(0, 0)
            used_blocks(sp, next_load, True)

        @block.gpsimd
        def _(pool):
            pool.memset(rows[0], 0.0)
            pool.memset(rows[1], 0.0).then_inc(s_clear, 1)
            pool.wait_ge(s_clear, 1)

            def gather(b, i, first):
                pool.wait_ge(s_ids, b * 3 + 1)
                if not first:
                    pool.wait_ge(s_xt, b * 2 - 2)
                pool.sem_inc(mem.passed, 1)
                pool.indirect_dma_start(out=rows[i], out_offset=None, in_=dram["h1"],
                                        in_offset=bass.IndirectOffsetOnAxis(ap=token[i][:, 0:1], axis=0),
                                        bounds_check=T - 1, oob_is_err=False).then_inc(s_rows[i], 16)

            def scatter(b, i):
                pool.wait_ge(s_row, b + 1)
                pool.wait_ge(s_y0, b + 1)
                pool.wait_ge(s_y1, b + 1)
                pool.sem_inc(mem.passed, 1)
                pool.indirect_dma_start(out=dram["expert_rows"],
                                        out_offset=bass.IndirectOffsetOnAxis(ap=row_id[i][:, 0:1], axis=0),
                                        in_=y[i], in_offset=None, bounds_check=T * TOPK - 1, oob_is_err=False)\
                    .then_inc(s_out[i], 16)

            def split(b, i):
                for n, u in enumerate(BY_POOL):
                    pool.wait_ge(s_whi, b * UNITS + (u + 1))
                    pool.tensor_tensor(unit(w_lo[i], u), unit(weights[i], u), unit(w_hi[i], u), ALU.subtract)\
                        .then_inc(s_wlo_pool, 1)

            def work(b, i, first):
                gather(b + 2, i, False)
                split(b + 1, 1 - i)
                scatter(b, i)

            gather(0, 0, True)
            gather(1, 1, True)
            split(0, 0)
            n = used_blocks(pool, work)
            even, odd = pool.snap(((n + 1) >> 1) * 16), pool.snap((n >> 1) * 16)
            even_rows, odd_rows = pool.snap(((n + 1) >> 1) * 16 + 16), pool.snap((n >> 1) * 16 + 16)
            for done, value in ((s_rows[0], even_rows), (s_rows[1], odd_rows), (s_out[0], even), (s_out[1], odd)):
                pool.wait_ge(done, value)
                pool.sem_inc(mem.passed, 1)

        @block.tensor
        def _(pe):
            def sum_ids(b, first=False):
                e = expert_of(pe, b)
                pe.wait_ge(s_hot, b + 1)
                if not first:
                    pe.wait_ge(s_ids, b * 3)
                for t in range(TILES + 1):
                    last = nc.tensor.matmul(mem.bank[6][:, 0:2], hot[:, t, :],
                                            route.row[:, t, bass.ds(e, 1), :].rearrange("p a c -> p (a c)"),
                                            start=(t == 0), stop=(t == TILES))
                last.then_inc(s_idp, 1)

            def transpose_rows(b, i, half, first=False):
                if half == 0:
                    pe.wait_ge(s_rows[i], (b - i) * 8 + 16)
                if not first:
                    pe.wait_ge(s_xlo, b * 2 - 1 + half)
                for k in range(4):
                    at = P * (4 * half + k)
                    last = nc.tensor.transpose(mem.bank[half][:, P * k:P * k + P], rows[i][:, at:at + P], C("ident"))
                last.then_inc(s_xt, 1)

            def product(out, x_parts, w_parts, c, start, stop):
                (xh, xl), (wh, wl) = x_parts, w_parts
                nc.tensor.matmul(out, xh[:, c, :], wh, start=start, stop=False)
                nc.tensor.matmul(out, xh[:, c, :], wl, start=False, stop=False)
                return nc.tensor.matmul(out, xl[:, c, :], wh, start=False, stop=stop)

            def work(b, i, first):
                sum_ids(b + 2)
                pe.wait_ge(s_xlo, b * 2 + 2)
                if not (first and i == 0):
                    pe.wait_ge(s_hid, b)
                for k in range(DC):
                    if k % 2 == 0:
                        wait_unit(b, k // 2)
                    at = slice(512 * k, 512 * k + 512)
                    last = product(mem.bank[2][:, :], (x_hi[i], x_lo[i]), (w_hi[i][:, at], w_lo[i][:, at]), k,
                                   k == 0, k == DC - 1)
                last.then_inc(s_gu, 1)
                transpose_rows(b + 1, 1 - i, 0)
                pe.wait_ge(s_hid, b + 1)
                if not (first and i == 0):
                    pe.wait_ge(s_hlo, b)
                for c in range(FC):
                    last = nc.tensor.transpose(mem.bank[3][:, P * c:P * c + P], hidden[:, P * c:P * c + P], C("ident"))
                last.then_inc(s_hdt, 1)
                transpose_rows(b + 1, 1 - i, 1)
                pe.wait_ge(s_hlo, b + 1)
                if not (first and i == 0):
                    pe.wait_ge(s_y0, b)
                    pe.wait_ge(s_y1, b)
                for c in range(FC):
                    wait_unit(b, UNITS - FC + c)
                    for n in range(2):
                        at = slice(W_GU + D * c + 512 * n, W_GU + D * c + 512 * n + 512)
                        last = product(mem.bank[4 + n][:, :], (h_hi, h_lo), (w_hi[i][:, at], w_lo[i][:, at]), c,
                                       c == 0, c == FC - 1)
                last.then_inc(s_dn, 1)

            def wait_unit(b, u):
                if u in BY_POOL:
                    pe.wait_ge(s_wlo_pool, b * len(BY_POOL) + (BY_POOL.index(u) + 1))
                else:
                    pe.wait_ge(s_wlo, b * len(BY_VECTOR) + (BY_VECTOR.index(u) + 1))

            sum_ids(0, True)
            sum_ids(1)
            for half in range(2):
                transpose_rows(0, 0, half, True)
            used_blocks(pe, work)

        @block.scalar
        def _(act):
            def split(b, i, units, first=False):
                for u in units:
                    if u == 0:
                        act.wait_ge(s_w[0][i], (b - i) * 8 + 16)
                    if u == UNITS - FC:
                        act.wait_ge(s_w[1][i], (b - i) * 8 + 16)
                        if not first:
                            act.wait_ge(s_dn, b - 1)
                    nc.scalar.activation(unit(w_hi[i], u), unit(weights[i], u), ACT.Copy).then_inc(s_whi, 1)

            def read_rows(b, i, half, first=False):
                if not first:
                    act.wait_ge(s_gu, b - 1)
                act.wait_ge(s_xt, b * 2 + (1 + half))
                nc.scalar.activation(x_hi[i][:, 4 * half:4 * half + 4, :],
                                     mem.bank[half][:, :].rearrange("p (k i) -> p k i", k=4), ACT.Copy)\
                    .then_inc(s_xhi, 1)

            def work(b, i, first):
                begin = first and i == 0
                if not begin:
                    act.wait_ge(s_gu, b)
                split(b + 1, 1 - i, range(UNITS - FC), begin)
                act.wait_ge(s_gu, b + 1)
                if not begin:
                    act.wait_ge(s_hid, b)
                nc.scalar.activation(act_g, mem.bank[2][:, 0:FF], ACT.Silu).then_inc(s_g, 1)
                read_rows(b + 1, 1 - i, 0, begin)
                act.wait_ge(s_hdt, b + 1)
                if not begin:
                    act.wait_ge(s_dn, b)
                nc.scalar.activation(h_hi, mem.bank[3][:, 0:FC * P].rearrange("p (c i) -> p c i", c=FC), ACT.Copy)\
                    .then_inc(s_hhi, 1)
                read_rows(b + 1, 1 - i, 1, begin)
                split(b + 1, 1 - i, range(UNITS - FC, UNITS), begin)
                act.wait_ge(s_dn, b + 1)
                if not first:
                    act.wait_ge(s_out[i], (b - i) * 8)
                nc.scalar.activation(y[i][:, 0:512], mem.bank[4][:, :], ACT.Copy).then_inc(s_y0, 1)

            for half in range(2):
                read_rows(0, 0, half, True)
            split(0, 0, range(UNITS), True)
            used_blocks(act, work)

        @block.vector
        def _(dve):
            def match(b, first=False):
                e = expert_of(dve, b)
                if not first:
                    dve.wait_ge(s_idp, b)
                for t in range(TILES + 1):
                    last = nc.vector.tensor_scalar(hot[:, t, :], C("slots"),
                                                   route.dest[:, t, bass.ds(e, 1)], C("block")[:, bass.ds(b, 1)],
                                                   ALU.subtract, ALU.is_equal)
                last.then_inc(s_hot, 1)

            def read_ids(b, i):
                dve.wait_ge(s_idp, b + 1)
                nc.vector.tensor_scalar(token[i][:, :], mem.bank[6][:, 0:1], NO_TOKEN, None, ALU.add)\
                    .then_inc(s_ids, 1)
                nc.vector.tensor_copy(pair_j[:, :], mem.bank[6][:, 1:2]).then_inc(s_ids, 1)
                dve.wait_ge(s_ids, b * 3 + 2)
                nc.vector.scalar_tensor_tensor(row_next[i][:, :], mem.bank[6][:, 0:1], float(TOPK), pair_j[:, :],
                                               ALU.mult, ALU.add).then_inc(s_ids, 1)

            def keep_row_id(b, i, first):
                dve.wait_ge(s_ids, b * 3 + 3)
                if not first:
                    dve.wait_ge(s_out[i], (b - i) * 8)
                nc.vector.tensor_scalar(row_id[i][:, :], row_next[i][:, :], NO_TOKEN * TOPK, None, ALU.add)\
                    .then_inc(s_row, 1)
                dve.wait_ge(s_row, b + 1)

            def split(b, i, units):
                for u in units:
                    if u in BY_VECTOR:
                        dve.wait_ge(s_whi, b * UNITS + (u + 1))
                        nc.vector.tensor_tensor(unit(w_lo[i], u), unit(weights[i], u), unit(w_hi[i], u),
                                                ALU.subtract).then_inc(s_wlo, 1)

            def split_rows(b, i, half):
                dve.wait_ge(s_xhi, b * 2 + (1 + half))
                at = slice(4 * half, 4 * half + 4)
                nc.vector.tensor_tensor(x_lo[i][:, at, :], mem.bank[half][:, :].rearrange("p (k i) -> p k i", k=4),
                                        x_hi[i][:, at, :], ALU.subtract).then_inc(s_xlo, 1)

            def work(b, i, first):
                split(b + 1, 1 - i, range(0, 2))
                keep_row_id(b, i, first)
                read_ids(b + 2, i)
                match(b + 3)
                split(b + 1, 1 - i, range(2, UNITS - FC))
                dve.wait_ge(s_g, b + 1)
                if not (first and i == 0):
                    dve.wait_ge(s_hdt, b)
                nc.vector.tensor_tensor(hidden, act_g, mem.bank[2][:, FF:2 * FF], ALU.mult).then_inc(s_hid, 1)
                split_rows(b + 1, 1 - i, 0)
                dve.wait_ge(s_hhi, b + 1)
                nc.vector.tensor_tensor(h_lo, mem.bank[3][:, 0:FC * P].rearrange("p (c i) -> p c i", c=FC), h_hi,
                                        ALU.subtract).then_inc(s_hlo, 1)
                split_rows(b + 1, 1 - i, 1)
                split(b + 1, 1 - i, range(UNITS - FC, UNITS))
                dve.wait_ge(s_dn, b + 1)
                if not first:
                    dve.wait_ge(s_out[i], (b - i) * 8)
                nc.vector.tensor_copy(y[i][:, 512:D], mem.bank[5][:, :]).then_inc(s_y1, 1)

            match(0, True)
            for b in range(2):
                read_ids(b, b)
                match(b + 1)
            for half in range(2):
                split_rows(0, 0, half)
            split(0, 0, range(UNITS))
            used_blocks(dve, work)


def combine_stage(nc, mem, dram, route):
    with ExitStack() as ctx:
        def sem(name):
            return ctx.enter_context(nc.semaphore(name))

        def take(name, *dims):
            return mem.carve(mem.sbuf(ctx, name, int(np.prod(dims))), 0, *dims)

        C = mem.consts
        got = [take(f"expert_rows{i}", TOPK, D) for i in range(2)]
        acc = [take(f"sum{i}", D) for i in range(2)]
        out = [take(f"out{i}", D) for i in range(2)]
        diag = [take(f"diagonals{i}", BY_TENSOR, P) for i in range(2)]
        ln = take("norm", 2, D)
        stats = [take(f"stats{i}", 32) for i in range(2)]

        s_ln = sem("norm_loaded")
        s_acc = [sem("residual_loaded_0"), sem("residual_loaded_1")]
        s_got = [[sem(f"expert_rows_{part}_loaded_{i}") for i in range(2)] for part in ("first", "others")]
        s_diag, s_sum, s_all = sem("diagonals_ready"), sem("rows_summed"), sem("token_sums_ready")
        s_norm, s_gain, s_y, s_v = sem("normed"), sem("gained"), sem("y_ready"), sem("combine_vector_steps")
        s_var, s_dev, s_scale = sem("variance_ready"), sem("deviation_ready"), sem("norm_factors_ready")
        s_out = [sem("y_stored_0"), sem("y_stored_1")]
        block = ctx.enter_context(nc.Block())
        tiles = token_tiles()
        by_token = dram["expert_rows"].rearrange("(t j) d -> t j d", j=TOPK)
        parts = (slice(0, BY_TENSOR), slice(BY_TENSOR, TOPK))

        @block.sync
        def _(sp):
            def load(t):
                w = tiles[t][2]
                def rows(part):
                    js = parts[part]
                    sp.dma_start(got[t % 2][0:w, js, :], by_token[P * t:P * t + w, js, :]).then_inc(s_got[part][t % 2], 16)

                if t >= 2:
                    sp.wait_ge(s_sum, t - 1)
                rows(0)
                if t >= 2:
                    sp.wait_ge(s_gain, t - 1)
                sp.dma_start(acc[t % 2][0:w], dram["residual"][P * t:P * t + w, :]).then_inc(s_acc[t % 2], 16)
                rows(1)

            load(0)
            load(1)
            sp.dma_start(ln, dram["norms"][:, 2:4, :]).then_inc(s_ln, 16)
            for t, _, w, _, _ in tiles:
                if t + 2 <= TILES:
                    load(t + 2)
                sp.wait_ge(s_y, t + 1)
                sp.dma_start(dram["y"][P * t:P * t + w, :], out[t % 2][0:w]).then_inc(s_out[t % 2], 16)
            sp.wait_ge(s_out[0], 48)
            sp.wait_ge(s_out[1], 32)

        @block.tensor
        def _(pe):
            for t, _, w, _, _ in tiles:
                i = t % 2
                pe.wait_ge(s_diag, t + 1)
                pe.wait_ge(s_got[0][i], 16 * (t // 2 + 1))
                if t >= 2:
                    pe.wait_ge(s_all, t - 1)
                for j in range(BY_TENSOR):
                    for n in range(2):
                        last = nc.tensor.matmul(mem.bank[2 * i + n][0:w, :], diag[i][0:w, j, 0:w],
                                                got[i][0:w, j, 512 * n:512 * n + 512],
                                                start=(j == 0), stop=(j == BY_TENSOR - 1))
                last.then_inc(s_sum, 1)

        def finish(act, t):
            _, _, w, _, _ = tiles[t]
            st = stats[t % 2][0:w]
            act.wait_ge(s_var, t + 1)
            nc.scalar.activation(st[:, 17:18], st[:, 13:14], ACT.Sqrt, bias=C("ln_eps")[0:w]).then_inc(s_dev, 1)
            act.wait_ge(s_scale, t + 1)
            nc.scalar.activation(acc[t % 2][0:w], acc[t % 2][0:w], ACT.Identity, bias=st[:, 18:19],
                                 scale=st[:, 15:16]).then_inc(s_norm, 1)

        @block.scalar
        def _(act):
            for t, _, w, _, _ in tiles:
                i = t % 2
                if t >= 2:
                    act.wait_ge(s_sum, t - 1)
                for j in range(BY_TENSOR):
                    last = nc.scalar.activation(diag[i][0:w, j, 0:w], C("ident")[0:w, 0:w], ACT.Copy,
                                                scale=route.weight[0:w, t, j:j + 1])
                last.then_inc(s_diag, 1)
                if t:
                    finish(act, t - 1)
            finish(act, TILES)

        @block.gpsimd
        def _(pool):
            pool.wait_ge(s_ln, 16)
            for t, _, w, _, _ in tiles:
                i = t % 2
                pool.wait_ge(s_norm, t + 1)
                if t >= 2:
                    pool.wait_ge(s_out[i], 16 * (t // 2))
                pool.tensor_tensor(out[i][0:w], acc[i][0:w], ln[0:w, 0, :], ALU.mult).then_inc(s_gain, 1)
                pool.wait_ge(s_gain, t + 1)
                pool.tensor_tensor(out[i][0:w], out[i][0:w], ln[0:w, 1, :], ALU.add).then_inc(s_y, 1)

        @block.vector
        def _(dve):
            steps = Steps(dve, s_v)
            for t, _, w, _, _ in tiles:
                i = t % 2
                dve.wait_ge(s_acc[i], 16 * (t // 2 + 1))
                dve.wait_ge(s_got[1][i], 16 * (t // 2 + 1))
                a = acc[i][0:w]
                for j in range(BY_TENSOR, TOPK):
                    steps.link(nc.vector.scalar_tensor_tensor(a, got[i][0:w, j, :], route.weight[0:w, t, j:j + 1], a,
                                                              ALU.mult, ALU.add))
                dve.wait_ge(s_sum, t + 1)
                for n in range(2):
                    at = slice(512 * n, 512 * n + 512)
                    last = nc.vector.tensor_tensor(a[:, at], a[:, at], mem.bank[2 * i + n][0:w, :], ALU.add)
                last.then_inc(s_all, 1)
                dve.wait_ge(s_all, t + 1)
                st = stats[i][0:w]
                if t >= 2:
                    dve.wait_ge(s_norm, t - 1)
                for n in range(2):
                    last = nc.vector.bn_stats(st[:, 6 * n:6 * n + 6], a[:, 512 * n:512 * n + 512])
                steps.link(last)
                nc.vector.bn_aggr(st[:, 12:14], st[:, 0:12]).then_inc(s_var, 1)
                dve.wait_ge(s_var, t + 1)
                steps.done(nc.vector.tensor_scalar(st[:, 14:15], st[:, 13:14], LN_EPS, None, ALU.add))
                dve.wait_ge(s_dev, t + 1)
                inverse_root(nc, steps, st[:, 15:16], st[:, 14:15], st[:, 17:18], st[:, 16:17])
                nc.vector.scalar_tensor_tensor(st[:, 18:19], st[:, 12:13], -1.0, st[:, 15:16], ALU.mult, ALU.mult)\
                    .then_inc(s_scale, 1)


def build(nc, dram):
    with ExitStack() as ctx:
        dram = dict(dram, h1=nc.dram_tensor("h1_rows", (T, D), F32, kind="Internal").ap(),
                    residual=nc.dram_tensor("residual_rows", (T, D), F32, kind="Internal").ap(),
                    expert_rows=nc.dram_tensor("expert_rows", (T * TOPK, D), F32, kind="Internal").ap())
        mem = Memory(nc, ctx)
        route = Routing(mem)
        with ExitStack() as front:
            mem.mixed_rows(front)
            with ExitStack() as delta:
                mem.delta_inputs(delta)
                projection_stage(nc, mem, dram)
                delta_rule_stage(nc, mem, dram)
            mixing_stage(nc, mem, dram, route)
        expert_stage(nc, mem, dram, route)
        combine_stage(nc, mem, dram, route)


def constant_tables():
    c = np.zeros((P, N_CONSTS), np.float32)

    def put(name, value):
        at, n = CONSTS[name]
        c[:, at:at + n] = value

    p, q = np.arange(P)[:, None], np.arange(P)[None, :]
    put("ident", p == q)
    put("tri", p <= q)
    put("before", p < q)
    put("ones", 1.0)
    put("masks", np.concatenate([((p >> l) % 2 == 1) & ((q >> l) == (p >> l) - 1) for l in range(LEVELS)], 1))
    put("future", np.where(q < p, -BIG, 0.0))
    put("slots", q)
    put("experts", np.arange(NE)[None, :])
    t = np.arange(TILES + 1)[None, :]
    put("token_base", p + P * t - NO_TOKEN)
    put("valid", (p + P * t) < T)
    put("row", p)
    put("ln_eps", LN_EPS)
    put("block", -float(P) * np.arange(2 * NB2 + 3)[None, :])
    put("over", P * t)
    return c


def kernel(**inputs):
    from concourse import bacc
    from concourse.bass_utils import run_bass_kernel_spmd

    x = {k: np.asarray(v) for k, v in inputs.items()}

    def feature_major(a, n):
        return a.reshape(-1, n, P).transpose(2, 1, 0)

    def rows(a):
        return np.broadcast_to(a.reshape(1, -1), (P, a.size))

    both = np.concatenate([x["x_prompt"][0], x["x_sample"][0]])
    x_t = np.zeros((P, DC, TW), np.float32)
    x_t[:, :, :SEQ] = feature_major(both[:SEQ], DC)
    x_t[:, :, S0:S0 + DEC] = feature_major(both[SEQ:], DC)
    w = x["w_in"][0]
    v_end, z_end = QKV, QKV + D
    lx, ly = z_end + 2 * H, z_end + 2 * H + D
    order = np.concatenate([w[:, lx:lx + D], w[:, ly:ly + D], w[:, :v_end], w[:, v_end:z_end]], 1)
    w_in = order.reshape(DC, P, NCH, P).transpose(2, 1, 0, 3)
    w_ba = w[:, z_end:lx].reshape(DC, P, 2 * H).transpose(1, 0, 2)
    conv_w = np.concatenate([x["lru_conv_w"][0], x["gdn_conv_w"][0]], 1)
    conv_b = np.concatenate([x["lru_conv_b"][0], np.zeros(QKV, np.float32)])
    hist = np.concatenate([x["state_lru_conv"][0, 0], x["state_gdn_conv"][0, 0]], 1)
    params = np.concatenate([
        feature_major(conv_w, 32).reshape(P, -1), feature_major(conv_b, 32).reshape(P, -1),
        feature_major(hist, 32).reshape(P, -1), feature_major(x["state_lru"][0, 0], DC).reshape(P, -1),
        feature_major(x["lru_lambda"][0], DC).reshape(P, -1),
        feature_major(x["lru_ba"][0], DC).reshape(P, -1), feature_major(x["lru_bx"][0], DC).reshape(P, -1),
        rows(x["gdn_dt_bias"][0]), rows(x["gdn_a_log"][0]), x["gdn_norm_w"][0].reshape(P, 1),
        rows(x["router_bias"][0]),
    ], 1)
    gates = np.concatenate([x["lru_wa"][0], x["lru_wx"][0]]).transpose(1, 0, 2)
    w_gu = np.stack([x["exp_w_gate"][0], x["exp_w_up"][0]], 2).reshape(NE, DC, P, 2 * FF).transpose(0, 2, 1, 3)
    w_dn = x["exp_w_down"][0].reshape(NE, FC, P, D).transpose(0, 2, 1, 3)
    w_exp = np.concatenate([w_gu.reshape(NE, P, -1), w_dn.reshape(NE, P, -1)], 2)
    s_gu = np.stack([x["sh_w_gate"][0], x["sh_w_up"][0]], 1).reshape(DC, P, 2 * FF).transpose(1, 0, 2)
    s_dn = x["sh_w_down"][0].reshape(FC, P, D).transpose(1, 0, 2)
    w_sh = np.concatenate([s_gu.reshape(P, -1), s_dn.reshape(P, -1)], 1)
    ins = {
        "consts": constant_tables(), "params": params, "x_t": x_t, "x_rows": both, "w_in": w_in, "w_ba": w_ba,
        "gates": gates, "state": x["state_gdn"][0, 0].transpose(1, 0, 2),
        "w_out": x["w_out"][0].reshape(2 * DC, P, D).transpose(1, 0, 2),
        "norms": np.stack([rows(x[n][0]) for n in ("ln1_g", "ln1_b", "ln2_g", "ln2_b")], 1),
        "w_router": x["router_w"][0].reshape(DC, P, NE).transpose(1, 0, 2), "w_sh": w_sh, "w_exp": w_exp,
    }
    ins = {k: np.ascontiguousarray(v) for k, v in ins.items()}
    outs = {
        "y": (T, D), "tails": (P, 32, 2 * GAP), "states": (2, P, H, P), "lru_last": (P, DC, 2),
    }
    nc = bacc.Bacc("TRN2", target_bir_lowering=False, num_devices=1)
    dram = {}
    for name, a in ins.items():
        dram[name] = nc.dram_tensor(f"in_{name}", a.shape, mybir.dt.from_np(a.dtype), kind="ExternalInput").ap()
    for name, shape in outs.items():
        dram[name] = nc.dram_tensor(f"out_{name}", shape, F32, kind="ExternalOutput").ap()
    build(nc, dram)
    got = run_bass_kernel_spmd(nc, [{f"in_{k}": v for k, v in ins.items()}], core_ids=[0]).results[0]
    y, tails, states, last = (got[f"out_{n}"] for n in outs)

    def tail(lo, hi, which):
        a = tails[:, lo:hi, GAP * which:GAP * (which + 1)]
        return a.transpose(2, 1, 0).reshape(1, 1, GAP, (hi - lo) * P)

    def result(which):
        return (tail(DC, 32, which), states[which].transpose(1, 0, 2)[None, None], tail(0, DC, which),
                last[:, :, which].T.reshape(1, 1, D))

    return (y[:SEQ][None], y[SEQ:][None], *result(0), *result(1))
```
